# Optimizing a Trainium2 kernel written in Bass

```python
import jax, jax.numpy as jnp
from jax import lax
import numpy as np

"""Hybrid streaming encoder, one inference step of DEPTH layers for two request groups sharing weights.

Each layer is post-norm with DeepNorm residual scaling (alpha = (2*DEPTH)^(1/4)):
  x <- LN1(alpha*x + W_out[ MLA head group (8 heads) || short gated conv group (512 channels) ](x))
  x <- LN2(alpha*x + CrossAttn(x, 256 memory tokens, 4 heads))
  x <- LN3(alpha*x + HierMoE(x))  (top-1 of 4 expert groups, then top-2 of 8 gated-MLP experts in that group)
All token mixing is chunk-causal with CHUNK = 64 (MLA uses the block-causal chunk mask, the conv is causal).

Inputs:
  x_prompt (BATCH, SEQ, D_MODEL), x_sample (DEC_BATCH, DEC_SEQ, D_MODEL)
  cache_kv_latent (DEPTH, DEC_BATCH, PAST_LEN, KV_LORA)   normalised MLA latent rows
  cache_k_rope    (DEPTH, DEC_BATCH, PAST_LEN, QK_ROPE)   rotated decoupled rotary key rows
  cache_conv      (DEPTH, DEC_BATCH, CONV_K-1, CONV_WIDTH) last conv input rows
  cache_mem_k / cache_mem_v (DEPTH, DEC_BATCH, N_MEM, X_HEADS, X_HEAD_DIM) memory keys / values
  mem_prompt (BATCH, N_MEM, D_MODEL); all weights carry a leading DEPTH axis.
Output tuple:
  y_prompt (BATCH, SEQ, D_MODEL), y_sample (DEC_BATCH, DEC_SEQ, D_MODEL),
  new_kv_latent_prompt (DEPTH, BATCH, SEQ, KV_LORA), new_k_rope_prompt (DEPTH, BATCH, SEQ, QK_ROPE),
  new_conv_prompt (DEPTH, BATCH, CONV_K-1, CONV_WIDTH),
  new_mem_k_prompt, new_mem_v_prompt (DEPTH, BATCH, N_MEM, X_HEADS, X_HEAD_DIM),
  new_kv_latent_sample (DEPTH, DEC_BATCH, DEC_SEQ, KV_LORA), new_k_rope_sample (DEPTH, DEC_BATCH, DEC_SEQ, QK_ROPE),
  new_conv_sample (DEPTH, DEC_BATCH, CONV_K-1, CONV_WIDTH).
"""

D_MODEL = 1024
BATCH = 1
SEQ = 1024
DEPTH = 1
DEC_BATCH = 8
DEC_SEQ = 16
PAST_LEN = 512

CHUNK = 64
Q_BLOCK = 128
N_HEADS = 8
QK_NOPE = 64
QK_ROPE = 32
V_HEAD = 64
Q_LORA = 256
KV_LORA = 128
ROPE_THETA = 10000.0
MLA_SCALE = (QK_NOPE + QK_ROPE) ** -0.5
CONV_WIDTH = 512
CONV_K = 3
MIX_WIDTH = N_HEADS * V_HEAD + CONV_WIDTH
IN_WIDTH = Q_LORA + KV_LORA + QK_ROPE + 3 * CONV_WIDTH
SPLITS = [Q_LORA, Q_LORA + KV_LORA, Q_LORA + KV_LORA + QK_ROPE,
          Q_LORA + KV_LORA + QK_ROPE + CONV_WIDTH, Q_LORA + KV_LORA + QK_ROPE + 2 * CONV_WIDTH]
N_MEM = 256
X_HEADS = 4
X_HEAD_DIM = D_MODEL // X_HEADS
X_SCALE = X_HEAD_DIM ** -0.5
N_GROUPS = 4
EXPERTS_PER_GROUP = 8
N_EXPERTS = N_GROUPS * EXPERTS_PER_GROUP
TOP_K = 2
D_EXPERT = 512
MOE_BLOCK = 128
ALPHA = (2 * DEPTH) ** 0.25
BETA = (8 * DEPTH) ** -0.25
LN_EPS = 1e-5
RMS_EPS = 1e-6

kernel_name = "hybrid_mla_shortconv_hiermoe_stream_step"

def layer_norm(x, g, b):
    xf = x.astype(jnp.float32)
    mu = xf.mean(-1, keepdims=True)
    var = jnp.square(xf - mu).mean(-1, keepdims=True)
    return ((xf - mu) * lax.rsqrt(var + LN_EPS) * g.astype(jnp.float32) + b.astype(jnp.float32)).astype(x.dtype)

def rms_norm(x, g):
    xf = x.astype(jnp.float32)
    return (xf * lax.rsqrt(jnp.mean(xf * xf, -1, keepdims=True) + RMS_EPS) * g.astype(jnp.float32)).astype(x.dtype)

def rope(x, pos):
    half = QK_ROPE // 2
    inv = ROPE_THETA ** (-jnp.arange(half, dtype=jnp.float32) / half)
    ang = pos.astype(jnp.float32)[:, None] * inv[None, :]
    ang = ang.reshape(ang.shape[0], *([1] * (x.ndim - 3)), half)
    cos, sin = jnp.cos(ang), jnp.sin(ang)
    xf = x.astype(jnp.float32)
    x1, x2 = xf[..., :half], xf[..., half:]
    return jnp.concatenate([x1 * cos - x2 * sin, x1 * sin + x2 * cos], -1).astype(x.dtype)

def mla_scores(qn, qr, kn, kr):
    s = jnp.einsum('bqhd,bkhd->bhqk', qn, kn) + jnp.einsum('bqhr,bkr->bhqk', qr, kr)
    return s.astype(jnp.float32) * MLA_SCALE

def mla_attend_prompt(qn, qr, kn, kr, v):
    B, S = qn.shape[:2]
    key_chunk = jnp.arange(S) // CHUNK

    def block(i):
        s0 = i * Q_BLOCK
        qn_b = lax.dynamic_slice_in_dim(qn, s0, Q_BLOCK, axis=1)
        qr_b = lax.dynamic_slice_in_dim(qr, s0, Q_BLOCK, axis=1)
        sc = mla_scores(qn_b, qr_b, kn, kr)
        q_chunk = (s0 + jnp.arange(Q_BLOCK)) // CHUNK
        sc = jnp.where(key_chunk[None, :] <= q_chunk[:, None], sc, -jnp.inf)
        p = jax.nn.softmax(sc, axis=-1).astype(v.dtype)
        return jnp.einsum('bhqk,bkhd->bqhd', p, v)

    out = lax.map(block, jnp.arange(S // Q_BLOCK))
    return out.transpose(1, 0, 2, 3, 4).reshape(B, S, N_HEADS * V_HEAD)

def mla_attend_all(qn, qr, kn, kr, v):
    B, S = qn.shape[:2]
    p = jax.nn.softmax(mla_scores(qn, qr, kn, kr), axis=-1).astype(v.dtype)
    return jnp.einsum('bhqk,bkhd->bqhd', p, v).reshape(B, S, N_HEADS * V_HEAD)

def token_mixer(x, pos, lat_past, kr_past, conv_past, lp):
    B, S, _ = x.shape
    proj = x @ lp['w_in']
    cq, ckv, kr, gb, gc, gv = jnp.split(proj, SPLITS, axis=-1)
    cq = rms_norm(cq, lp['q_norm_g'])
    ckv = rms_norm(ckv, lp['kv_norm_g'])
    kr = rope(kr, pos)
    q = (cq @ lp['w_uq']).reshape(B, S, N_HEADS, QK_NOPE + QK_ROPE)
    qn, qr = q[..., :QK_NOPE], rope(q[..., QK_NOPE:], pos)
    if lat_past is None:
        lat, kr_all = ckv, kr
    else:
        lat = jnp.concatenate([lat_past, ckv], axis=1)
        kr_all = jnp.concatenate([kr_past, kr], axis=1)
    kv = (lat @ lp['w_ukv']).reshape(B, lat.shape[1], N_HEADS, QK_NOPE + V_HEAD)
    kn, v = kv[..., :QK_NOPE], kv[..., QK_NOPE:]
    if lat_past is None:
        attn = mla_attend_prompt(qn, qr, kn, kr_all, v)
    else:
        attn = mla_attend_all(qn, qr, kn, kr_all, v)
    u = gc * gv
    if conv_past is None:
        u_all = jnp.pad(u, ((0, 0), (CONV_K - 1, 0), (0, 0)))
    else:
        u_all = jnp.concatenate([conv_past, u], axis=1)
    cw = lp['conv_w']
    conv = cw[0] * u_all[:, 0:S]
    for k in range(1, CONV_K):
        conv = conv + cw[k] * u_all[:, k:k + S]
    y_conv = gb * conv
    out = jnp.concatenate([attn, y_conv], axis=-1) @ lp['w_out']
    return out, ckv, kr, u_all[:, -(CONV_K - 1):]

def memory_kv(mem, w_xk, w_xv):
    B = mem.shape[0]
    mk = (mem @ w_xk).reshape(B, N_MEM, X_HEADS, X_HEAD_DIM)
    mv = (mem @ w_xv).reshape(B, N_MEM, X_HEADS, X_HEAD_DIM)
    return mk, mv

def cross_attend(x, mk, mv, w_xq, w_xo):
    B, S, _ = x.shape
    q = (x @ w_xq).reshape(B, S, X_HEADS, X_HEAD_DIM)
    sc = jnp.einsum('bqhd,bmhd->bhqm', q, mk).astype(jnp.float32) * X_SCALE
    p = jax.nn.softmax(sc, axis=-1).astype(mv.dtype)
    o = jnp.einsum('bhqm,bmhd->bqhd', p, mv).reshape(B, S, D_MODEL)
    return o @ w_xo

def hier_moe(x, lp):
    shp = x.shape
    xt = x.reshape(-1, shp[-1])
    T = xt.shape[0]
    TK = T * TOP_K
    logits_g = (xt @ lp['w_router_group']).astype(jnp.float32) + lp['b_router_group'].astype(jnp.float32)
    p_g = jax.nn.softmax(logits_g, axis=-1)
    g = jnp.argmax(logits_g, axis=-1)
    rows = jnp.arange(T)
    pg = p_g[rows, g]
    logits_e = (xt @ lp['w_router_expert']).astype(jnp.float32).reshape(T, N_GROUPS, EXPERTS_PER_GROUP)
    logits_e = logits_e + lp['b_router_expert'].astype(jnp.float32)
    le = logits_e[rows, g]
    top_v, top_i = lax.top_k(le, TOP_K)
    gate = (jax.nn.softmax(top_v, axis=-1) * pg[:, None]).reshape(-1)
    eid = (g[:, None] * EXPERTS_PER_GROUP + top_i).reshape(-1)
    tok = jnp.repeat(rows, TOP_K)
    order = jnp.argsort(eid, stable=True)
    se, stok, sgate = eid[order], tok[order], gate[order]
    counts = jnp.zeros((N_EXPERTS,), jnp.int32).at[eid].add(1)
    starts = jnp.cumsum(counts) - counts
    padded = (counts + MOE_BLOCK - 1) // MOE_BLOCK * MOE_BLOCK
    pends = jnp.cumsum(padded)
    pstarts = pends - padded
    dest = pstarts[se] + jnp.arange(TK) - starts[se]
    n_blocks = -(-TK // MOE_BLOCK) + N_EXPERTS
    P = n_blocks * MOE_BLOCK
    buf_tok = jnp.zeros((P,), jnp.int32).at[dest].set(stok)
    buf_gate = jnp.zeros((P,), jnp.float32).at[dest].set(sgate)
    block_e = jnp.minimum(jnp.searchsorted(pends, jnp.arange(n_blocks) * MOE_BLOCK, side='right'), N_EXPERTS - 1)
    w_g, w_u, w_d = lp['w_exp_gate'], lp['w_exp_up'], lp['w_exp_down']

    def expert_block(args):
        e, toks, wts = args
        xb = xt[toks]
        h = jax.nn.silu(xb @ w_g[e]) * (xb @ w_u[e])
        return (h @ w_d[e]) * wts[:, None].astype(xt.dtype)

    yb = lax.map(expert_block, (block_e, buf_tok.reshape(n_blocks, MOE_BLOCK), buf_gate.reshape(n_blocks, MOE_BLOCK)))
    out = jnp.zeros_like(xt).at[buf_tok].add(yb.reshape(P, shp[-1]))
    return out.reshape(shp)

def encoder_layer(x, pos, mk, mv, lat_past, kr_past, conv_past, lp):
    a, lat_new, kr_new, conv_new = token_mixer(x, pos, lat_past, kr_past, conv_past, lp)
    x = layer_norm(ALPHA * x + a, lp['ln1_g'], lp['ln1_b'])
    x = layer_norm(ALPHA * x + cross_attend(x, mk, mv, lp['w_xq'], lp['w_xo']), lp['ln2_g'], lp['ln2_b'])
    x = layer_norm(ALPHA * x + hier_moe(x, lp), lp['ln3_g'], lp['ln3_b'])
    return x, lat_new, kr_new, conv_new

def setup_inputs(seed: int = 0) -> dict:
    key = jax.random.key(seed)
    ks = iter(jax.random.split(key, 40))

    def nrm(shape, scale=1.0):
        return jax.random.normal(next(ks), shape, jnp.float32) * scale

    L = DEPTH
    D = D_MODEL
    return {
        'x_prompt': nrm((BATCH, SEQ, D)),
        'x_sample': nrm((DEC_BATCH, DEC_SEQ, D)),
        'cache_kv_latent': nrm((L, DEC_BATCH, PAST_LEN, KV_LORA)),
        'cache_k_rope': nrm((L, DEC_BATCH, PAST_LEN, QK_ROPE)),
        'cache_conv': nrm((L, DEC_BATCH, CONV_K - 1, CONV_WIDTH)),
        'cache_mem_k': nrm((L, DEC_BATCH, N_MEM, X_HEADS, X_HEAD_DIM)),
        'cache_mem_v': nrm((L, DEC_BATCH, N_MEM, X_HEADS, X_HEAD_DIM), BETA),
        'mem_prompt': nrm((BATCH, N_MEM, D)),
        'w_in': nrm((L, D, IN_WIDTH), D ** -0.5),
        'q_norm_g': 1.0 + nrm((L, Q_LORA), 0.02),
        'kv_norm_g': 1.0 + nrm((L, KV_LORA), 0.02),
        'w_uq': nrm((L, Q_LORA, N_HEADS * (QK_NOPE + QK_ROPE)), Q_LORA ** -0.5),
        'w_ukv': nrm((L, KV_LORA, N_HEADS * (QK_NOPE + V_HEAD)), KV_LORA ** -0.5),
        'conv_w': nrm((L, CONV_K, CONV_WIDTH), CONV_K ** -0.5),
        'w_out': nrm((L, MIX_WIDTH, D), MIX_WIDTH ** -0.5 * BETA),
        'ln1_g': 1.0 + nrm((L, D), 0.02),
        'ln1_b': nrm((L, D), 0.02),
        'w_xq': nrm((L, D, D), D ** -0.5),
        'w_xk': nrm((L, D, D), D ** -0.5),
        'w_xv': nrm((L, D, D), D ** -0.5 * BETA),
        'w_xo': nrm((L, D, D), D ** -0.5 * BETA),
        'ln2_g': 1.0 + nrm((L, D), 0.02),
        'ln2_b': nrm((L, D), 0.02),
        'w_router_group': nrm((L, D, N_GROUPS), D ** -0.5),
        'b_router_group': nrm((L, N_GROUPS), 0.01),
        'w_router_expert': nrm((L, D, N_GROUPS * EXPERTS_PER_GROUP), D ** -0.5),
        'b_router_expert': nrm((L, N_GROUPS, EXPERTS_PER_GROUP), 0.01),
        'w_exp_gate': nrm((L, N_EXPERTS, D, D_EXPERT), D ** -0.5),
        'w_exp_up': nrm((L, N_EXPERTS, D, D_EXPERT), D ** -0.5),
        'w_exp_down': nrm((L, N_EXPERTS, D_EXPERT, D), D_EXPERT ** -0.5 * BETA),
        'ln3_g': 1.0 + nrm((L, D), 0.02),
        'ln3_b': nrm((L, D), 0.02),
    }

def reference(x_prompt, x_sample, cache_kv_latent, cache_k_rope, cache_conv, cache_mem_k, cache_mem_v,
              mem_prompt, w_in, q_norm_g, kv_norm_g, w_uq, w_ukv, conv_w, w_out, ln1_g, ln1_b,
              w_xq, w_xk, w_xv, w_xo, ln2_g, ln2_b, w_router_group, b_router_group,
              w_router_expert, b_router_expert, w_exp_gate, w_exp_up, w_exp_down, ln3_g, ln3_b):
    pos_p = jnp.arange(x_prompt.shape[1])
    pos_s = cache_kv_latent.shape[2] + jnp.arange(x_sample.shape[1])
    xp, xs = x_prompt, x_sample
    lat_p, kr_p, conv_p, mk_p, mv_p = [], [], [], [], []
    lat_s, kr_s, conv_s = [], [], []
    for l in range(DEPTH):
        lp = dict(w_in=w_in[l], q_norm_g=q_norm_g[l], kv_norm_g=kv_norm_g[l], w_uq=w_uq[l], w_ukv=w_ukv[l],
                  conv_w=conv_w[l], w_out=w_out[l], ln1_g=ln1_g[l], ln1_b=ln1_b[l], w_xq=w_xq[l], w_xo=w_xo[l],
                  ln2_g=ln2_g[l], ln2_b=ln2_b[l], w_router_group=w_router_group[l],
                  b_router_group=b_router_group[l], w_router_expert=w_router_expert[l],
                  b_router_expert=b_router_expert[l], w_exp_gate=w_exp_gate[l], w_exp_up=w_exp_up[l],
                  w_exp_down=w_exp_down[l], ln3_g=ln3_g[l], ln3_b=ln3_b[l])
        mk, mv = memory_kv(mem_prompt, w_xk[l], w_xv[l])
        xp, lat_new, kr_new, conv_new = encoder_layer(xp, pos_p, mk, mv, None, None, None, lp)
        lat_p.append(lat_new); kr_p.append(kr_new); conv_p.append(conv_new); mk_p.append(mk); mv_p.append(mv)
        xs, lat_new, kr_new, conv_new = encoder_layer(xs, pos_s, cache_mem_k[l], cache_mem_v[l],
                                                      cache_kv_latent[l], cache_k_rope[l], cache_conv[l], lp)
        lat_s.append(lat_new); kr_s.append(kr_new); conv_s.append(conv_new)
    return (xp, xs, jnp.stack(lat_p), jnp.stack(kr_p), jnp.stack(conv_p), jnp.stack(mk_p), jnp.stack(mv_p),
            jnp.stack(lat_s), jnp.stack(kr_s), jnp.stack(conv_s))


_drawn_inputs = setup_inputs


def setup_inputs(seed=0):
    import zlib

    import numpy as np

    out = dict(_drawn_inputs(seed))
    spreads = {}
    factors = {'q_norm_g': 21.542,
     'b_router_group': 21.37,
     'b_router_expert': 15.986,
     'ln3_g': 7.669,
     'ln3_b': 8.024}
    for name, (base, spread) in spreads.items():
        noise = np.random.default_rng([zlib.crc32(name.encode()), seed]).standard_normal(out[name].shape)
        drawn = base * np.exp(spread * noise) if base else spread * noise
        out[name] = __import__('jax').numpy.asarray(drawn.astype(out[name].dtype))
    for name, factor in factors.items():
        out[name] = (out[name] * factor).astype(out[name].dtype)
    return out
```

```python
import concourse.bass as bass
from concourse import mybir
from contextlib import ExitStack, contextmanager


def consts_table():
    import numpy as np

    p = np.arange(128)
    ident = np.eye(128, dtype=np.float32)
    tri = (p[:, None] < p[None, :]).astype(np.float32)
    ones = np.ones((128, 128), np.float32)
    half = 16
    inv = (np.float32(10000.0) ** (-np.arange(half, dtype=np.float32) / np.float32(half))).astype(np.float32)
    rope = np.zeros((128, 9, 64), np.float32)
    for t in range(9):
        pos = (t * 128 + p if t < 8 else 512 + p % 16).astype(np.float32)
        ang = pos[:, None] * inv[None, :]
        c, s = np.cos(ang).astype(np.float32), np.sin(ang).astype(np.float32)
        rope[:, t] = np.concatenate([c, c, -s, s], 1)
    iota = np.broadcast_to(p.astype(np.float32), (128, 128))
    slot = 2 * (128 * np.arange(9)[None, :, None] + p[:, None, None]) + np.arange(2)[None, None, :] + 1
    return np.ascontiguousarray(np.concatenate(
        [ident, tri, ones, rope.reshape(128, -1), iota, slot.reshape(128, -1).astype(np.float32)], 1), np.float32)


class Count:

    def __init__(self, name):
        self.name, self.fixed, self.local, self.turn = name, 0, 0, None

    def next(self, by=1):
        self.local += by
        return by

    def value(self):
        own = self.fixed + self.local
        return own if self.turn is None else own + self.turn[0] * self.turn[1]

    @contextmanager
    def loop(self, j, per, turns):
        self.fixed, self.local, self.turn = self.fixed + self.local, 0, (j, per)
        yield
        assert self.local == per, (self.name, self.local, per)
        self.fixed, self.local, self.turn = self.fixed + turns * per, 0, None


def encoder_layer_kernel(nc, A, O):
    f32, i32, u32 = mybir.dt.float32, mybir.dt.int32, mybir.dt.uint32
    ALU, ACT, AX = mybir.AluOpType, mybir.ActivationFunctionType, mybir.AxisListType
    ds = bass.ds

    P, D, NT, PT = 128, 1024, 9, 8
    NB, ROWS, PAST = 8, 16, 512
    H, DN, DR, DV = 8, 64, 32, 64
    HW = DN + DR
    QL, KL, CW = 256, 128, 512
    INW = QL + KL + DR + 3 * CW
    XH, XD, MEM = 4, 256, 256
    NG, EG, NE, FE = 4, 8, 32, 512
    NBLK = 50
    KT = D // P
    ALPHA = 2.0 ** 0.25
    MLA_SCALE, X_SCALE = float(HW) ** -0.5, float(XD) ** -0.5
    LN_EPS, RMS_EPS = 1e-5, 1e-6
    FAR = -1e30

    x_p = A["x_prompt"].rearrange("b s d -> (b s) d")
    x_s = A["x_sample"].rearrange("b s d -> (b s) d")
    y_p = O["y_prompt"].rearrange("b s d -> (b s) d")
    y_s = O["y_sample"].rearrange("b s d -> (b s) d")
    lat_p = O["new_kv_latent_prompt"].rearrange("l b s d -> (l b s) d")
    lat_s = O["new_kv_latent_sample"].rearrange("l b s d -> (l b s) d")
    kr_p = O["new_k_rope_prompt"].rearrange("l b s d -> (l b s) d")
    kr_s = O["new_k_rope_sample"].rearrange("l b s d -> (l b s) d")
    conv_p = O["new_conv_prompt"].rearrange("l b s d -> (l b s) d")
    conv_s = O["new_conv_sample"].rearrange("l b s d -> (l b) s d")
    mem_k_out = O["new_mem_k_prompt"].rearrange("l b (c p) h d -> p (l b c) (h d)", p=P)
    mem_v_out = O["new_mem_v_prompt"].rearrange("l b (c p) h d -> p (l b c) (h d)", p=P)
    mem_rows = A["mem_prompt"].rearrange("b (c p) d -> p (b c) d", p=P)
    cache_lat = A["cache_kv_latent"].rearrange("l b (c p) d -> (l b) p c d", p=P)
    cache_kr = A["cache_k_rope"].rearrange("l b (c p) d -> (l b) p c d", p=P)
    cache_conv = A["cache_conv"].rearrange("l b s d -> (l b) s d")
    cache_mk = A["cache_mem_k"].rearrange("l b (c p) h d -> (l b) p c (h d)", p=P)
    cache_mv = A["cache_mem_v"].rearrange("l b (c p) h d -> (l b) p c (h d)", p=P)

    def by_rows(name):
        return A[name].rearrange("l (k p) n -> p (l k) n", p=P)

    w_in_rows = by_rows("w_in")
    w_gate = A["w_exp_gate"].rearrange("l e (k p) n -> (l e) p k n", p=P)
    w_up = A["w_exp_up"].rearrange("l e (k p) n -> (l e) p k n", p=P)
    w_down = A["w_exp_down"].rearrange("l e (k p) n -> (l e) p k n", p=P)

    q_dram = nc.dram_tensor("q_rows", [NT * P, H * HW], f32).ap()
    u_dram = nc.dram_tensor("u_rows_prompt", [PT * P + 2, CW], f32).ap()
    us_dram = nc.dram_tensor("u_rows_sample", [NB, ROWS + 2, CW], f32).ap()
    gb_dram = nc.dram_tensor("gate_rows", [NT * P, CW], f32).ap()
    x2_dram = nc.dram_tensor("x2_rows", [NT * P, D], f32).ap()
    ye_dram = nc.dram_tensor("expert_rows", [2 * NT * P, D], f32).ap()
    ye_pairs = ye_dram.rearrange("(r k) d -> r k d", k=2)

    ctx = ExitStack()
    with ctx:
        def sb(name, shape, dt=f32):
            return ctx.enter_context(nc.sbuf_tensor(name, shape, dt))[tuple(slice(None) for _ in shape)]

        def sem(name):
            return ctx.enter_context(nc.semaphore(name))

        tables = sb("tables", [P, 3 * P + NT * 64 + P + 2 * NT])
        ident, tri, ones = (tables[:, i * P:(i + 1) * P] for i in range(3))
        rope = tables[:, 3 * P:3 * P + NT * 64].rearrange("p (t c) -> p t c", t=NT)
        iota = tables[:, 3 * P + NT * 64:4 * P + NT * 64]
        slot_id = tables[:, 4 * P + NT * 64:].rearrange("p (t k) -> p t k", k=2)
        conv_w = sb("conv_w_rows", [P, 3, CW])
        w_router = sb("w_router", [P, KT, NG + NE])
        b_router = sb("b_router", [P, NG + NE])
        logits = sb("logits", [P, NT, NG + NE])
        gates = sb("gates", [P, 2, NT])
        minus_half = sb("minus_half", [P, 2])
        zero_row = sb("zero_row", [2, CW])
        shift2 = sb("shift2", [P, D])
        sumsq = [sb(f"sumsq{u}", [P, 2]) for u in (0, 1)]
        rrms = [sb(f"rrms{u}", [P, 2]) for u in (0, 1)]
        negmax = [sb(f"negmax{u}", [P, 1]) for u in (0, 1)]
        rsum = [sb(f"rsum{u}", [P, 1]) for u in (0, 1)]
        rinv = [sb(f"rinv{u}", [P, 1]) for u in (0, 1)]
        stats = [sb(f"stats{u}", [P, 12]) for u in (0, 1)]
        moments = [sb(f"moments{u}", [P, 2]) for u in (0, 1)]
        rstd = [sb(f"rstd{u}", [P, 1]) for u in (0, 1)]
        xmax = [sb(f"xmax{u}", [P, XH]) for u in (0, 1)]
        xsum = [sb(f"xsum{u}", [P, XH]) for u in (0, 1)]
        route_tok = sb("route_tok", [P, NBLK + 2], u32)
        route_out = sb("route_out", [P, NBLK + 2], u32)
        tok_now = [sb(f"tok_now{u}", [P, 1], u32) for u in (0, 1)]
        out_now = [sb(f"out_now{u}", [P, 1], u32) for u in (0, 1)]
        plan = sb("plan", [1, NBLK + 1], i32)

        ARENA = 47912
        arena = sb("arena", [P, ARENA])

        def area(at, *dims):
            n = 1
            for d in dims:
                n *= d
            assert at + n <= ARENA, (at, dims)
            got, names = arena[:, at:at + n], "abc"[:len(dims)]
            if len(dims) == 1:
                return got
            return got.rearrange(f"p ({' '.join(names)}) -> p {' '.join(names)}",
                                 **{c: d for c, d in zip(names, dims)})

        def pair(at, *dims):
            n = 1
            for d in dims:
                n *= d
            return [area(at + u * n, *dims) for u in (0, 1)]

        WA, KEEP = 0, 3 * KT * D
        w_ukv = area(KEEP, H, DN + DV)
        latT = area(KEEP + 1024, NT * P)
        krTs = area(KEEP + 2176, P)
        memkT = area(KEEP + 2304, KT, MEM)
        memv = area(KEEP + 4352, 2, D)
        ATT = KEEP + 6400
        attn = area(ATT, PT, H * DV)
        VAL = ATT + 4096
        value = area(VAL, PT, H * DV)
        WORK = VAL + 4096
        mixTs = area(46336, 4, P)

        mem, memT, memk = area(VAL, 2, D), area(VAL + 2048, 2, KT, P), area(ATT + 2 * D, 2, D)
        w_xk, w_xv = area(WA, KT, D), area(WA + 8192, KT, D)
        w_in = [area(WA + 16384 + k * INW if k < 4 else WA + (k - 4) * INW, INW) for k in range(KT)]
        x_a, xT_a = pair(ATT, D), pair(ATT + 2 * D, KT, P)
        w_uq, sq_junk = area(VAL, 2, H * HW), area(VAL + 1536, QL)
        rot_q = [(area(o, H, DR), area(o + H * DR, H, DR)) for o in (VAL + 1792, WORK + 7040)]
        rot_k = [(area(o, 1, DR), area(o + DR, 1, DR)) for o in (VAL + 3776, VAL + 3840)]
        cqn, ckvn, krpad, cqT = pair(VAL + 2304, QL), pair(VAL + 2816, KL), pair(VAL + 3072, HW), pair(VAL + 3264, 2, P)
        kT = pair(WORK, D)
        gbs, gvs, us = pair(WORK + 2048, CW), pair(WORK + 3072, CW), pair(WORK + 4096, CW)
        qrow = pair(WORK + 5120, H * HW)
        q_gain, kv_gain = area(WORK + 6656, QL), area(WORK + 6912, KL)
        qh, wk = pair(WA + 16384, PT, HW), pair(WA + 17920, DN)
        qT, pr, prT = pair(WORK + 2048, D), pair(WORK + 4096, D), area(WORK + 6144, PT, P)
        lat_b, kr_b = pair(WA + 16384, 4, KL), pair(WA + 17408, 4, HW)
        lat_new, q_s = area(WA + 18176, NB, KL), area(WA + 19200, H, HW)
        wukT, qabs, ctxT = area(VAL, H, P), area(VAL + 1024, H, P), area(VAL + 2048, H, P)
        qTs = area(VAL + 3072, H, P)
        latTb, krTb, p_b = pair(WORK, PAST + ROWS), pair(WORK + 1056, PAST + ROWS), pair(WORK + 2112, PAST + ROWS)
        pT_b = pair(WORK + 3168, 5, P)
        qa_b, qr_b, latn_b = pair(WORK + 4448, H, ROWS), pair(WORK + 4704, H, ROWS), pair(WORK + 4960, KL)
        w_out, w_xq, w_xo = area(WA, KT, D), area(WA + 8192, KT, D), area(WA + 16384, KT, D)
        xr, aT = [area(VAL + u * 4096, D) for u in (0, 1)], [area(VAL + u * 4096 + 1024, KT, P) for u in (0, 1)]
        mix, res = [area(VAL + u * 4096 + 2048, D) for u in (0, 1)], [area(VAL + u * 4096 + 3072, D) for u in (0, 1)]
        cv = area(VAL + 8192, 4, CW)
        conv_rows = pair(46848, CW)
        gain1, shift1, gain2 = area(KEEP, D), area(KEEP + D, D), area(VAL + 10240, D)
        mk_b, mv_b = [area(ATT, 2, D), area(VAL + 4096, 2, D)], [area(ATT + 2048, 2, D), area(VAL + 6144, 2, D)]
        mkT_b = memkT
        qx_b, px_b, pxT_b = area(VAL + 8192, KT, 32), area(VAL + 8448, MEM), area(VAL + 8704, 2, P)
        oxT = mix[0].rearrange("p (k c) -> p k c", k=KT)
        GU = KT * FE
        w_g = [area(WA + u * 12288, KT, FE) for u in (0, 1)]
        w_u = [area(WA + u * 12288 + GU, KT, FE) for u in (0, 1)]
        w_d = [area(WA + u * 12288 + 2 * GU, 4, D) for u in (0, 1)]
        xg, xgT, hid, hidT = pair(KEEP, D), pair(KEEP + 2048, KT, P), pair(KEEP + 4096, FE), pair(KEEP + 5120, 4, P)
        yo = pair(KEEP + 6144, D)
        at = [WA]

        def route(*dims, dt=f32):
            got = area(at[0], *dims)
            size = 1
            for d in dims:
                size *= d
            at[0] += size
            return got if dt is f32 else got.bitcast(dt)

        r_best, r_first, r_v1, r_v2, r_d2, r_e2, r_sum, r_den, r_lim = (route(NT) for _ in range(9))
        r_s4, r_group, r_gd, r_eg = (route(NT, NG) for _ in range(4))
        r_le, r_s8, r_pick1, r_pick2 = (route(NT, EG) for _ in range(4))
        r_all, r_hot, picks = route(NT * NE), route(2, NT, NE), route(NT * NE)
        r_all = r_all.rearrange("p (t g e) -> p t g e", t=NT, g=NG)
        r_before, r_total, r_rank, r_cmp = route(NT + 1, NE), route(NT, NE), route(NT, NE), route(NE, NT)
        r_blocks, r_end, r_start = (route(NE) for _ in range(3))
        r_slot, r_int, r_int2 = route(NT, 2), route(2 * NT, dt=i32), route(2 * NT, dt=i32)
        r_blk, r_pos, r_plan, r_row, r_int3 = route(2 * NT), route(2 * NT), route(NBLK, NE), route(NBLK + 1), route(NBLK + 1, dt=i32)
        r_map, r_mapi, r_mapi2 = route(NBLK), route(NBLK, dt=i32), route(NBLK, dt=i32)
        sel_slot, sel_blk = (route(P), route(P)), (route(NBLK), route(NBLK))
        LAST = KEEP + 14000
        yk, xl, rl = pair(LAST, 2, D), pair(LAST + 4096, D), pair(LAST + 6144, D)
        gain3, shift3 = area(KEEP + 12900 - 2048, D), area(KEEP + 12900 - 1024, D)

        T = [ctx.enter_context(nc.psum_tensor(f"T{u}", [P, 1024], f32)) for u in (0, 1)]
        M = [ctx.enter_context(nc.psum_tensor(f"M{u}", [P, 1024], f32)) for u in (0, 1)]

        tables_in, consts_in, mem_in = sem("tables_in"), sem("consts_in"), sem("mem_in")
        wxk_in, wxv_in, win_lo_in, win_hi_in = sem("wxk_in"), sem("wxv_in"), sem("win_lo_in"), sem("win_hi_in")
        memT_ps, memT_ready = sem("memT_ps"), sem("memT_ready")
        memk_ps, memk_rows, memv_ps, memv_rows = sem("memk_ps"), sem("memk_rows"), sem("memv_ps"), sem("memv_rows")
        memkT_ps, memkT_ready, mem_out = sem("memkT_ps"), sem("memkT_ready"), sem("mem_out")
        dve_step, pool_step = sem("dve_step"), sem("pool_step")
        dve_waited, pool_waited = sem("dve_waited"), sem("pool_waited")
        pads_zero, pool_consts = sem("pads_zero"), sem("pool_consts")
        x_in = [sem(f"x_in{u}") for u in (0, 1)]
        xT_ps, xT_ready = sem("xT_ps"), sem("xT_ready")
        latent_ps, conv_ps = sem("latent_ps"), sem("conv_ps")
        sumsq_ready, rrms_ready, gb_ready, gv_ready = (sem(n) for n in ("sumsq_ready", "rrms_ready", "gb_ready", "gv_ready"))
        norm_done, u_ready, cT_ps, cqT_ready = (sem(n) for n in ("norm_done", "u_ready", "cT_ps", "cqT_ready"))
        latT_ready, q_ps, q_rows, q_turned = (sem(n) for n in ("latT_ready", "q_ps", "q_rows", "q_turned"))
        gb_out, lat_out, u_out, q_out = ([sem(f"{n}{u}") for u in (0, 1)] for n in ("gb_out", "lat_out", "u_out", "q_out"))
        edge_out = sem("edge_out")
        value_ps, value_ready = sem("value_ps"), sem("value_ready")
        head_in = [sem(f"head_in{u}") for u in (0, 1)]
        qT_ps, kT_ps, qT_ready, kT_ready = (sem(n) for n in ("qT_ps", "kT_ps", "qT_ready", "kT_ready"))
        s_ps, negmax_ready, exp_done, pT_ps, pT_ready, o_ps, o_done = (
            sem(n) for n in ("s_ps", "negmax_ready", "exp_done", "pT_ps", "pT_ready", "o_ps", "o_done"))
        sq_in, sqT_ps, sqT_ready, wukT_ready, qabs_ps, qabs_ready = (
            sem(n) for n in ("sq_in", "sqT_ps", "sqT_ready", "wukT_ready", "qabs_ps", "qabs_ready"))
        cache_in = [sem(f"cache_in{u}") for u in (0, 1)]
        bq_ready, latb_ps, latb_ready, sb_ps, sb_negmax, sb_exp, sb_p, pTb_ps, pTb_ready, ctx_ps, ctx_done = (
            sem(n) for n in ("bq_ready", "latb_ps", "latb_ready", "sb_ps", "sb_negmax", "sb_exp", "sb_p",
                             "pTb_ps", "pTb_ready", "ctx_ps", "ctx_done"))
        mixTs_ps, mixTs_ready = sem("mixTs_ps"), sem("mixTs_ready")
        woq_in, wxo_in, ln_in = sem("woq_in"), sem("wxo_in"), sem("ln_in")
        conv_in, conv_ready, attn_copied = sem("conv_in"), sem("conv_ready"), sem("attn_copied")
        xr_in = [sem(f"xr_in{u}") for u in (0, 1)]
        rowsT_ps, rowsT_ready, product_ps = sem("rowsT_ps"), sem("rowsT_ready"), sem("product_ps")
        var_ready, rstd_ready, x1_ready, xq_rows, xmax_ready, px_ready, ox_ready, x2_ready, logits_done = (
            sem(n) for n in ("var_ready", "rstd_ready", "x1_ready", "xq_rows", "xmax_ready", "px_ready", "ox_ready",
                             "x2_ready", "logits_done"))
        x2_out = [sem(f"x2_out{u}") for u in (0, 1)]
        mkv_in = [sem(f"mkv_in{u}") for u in (0, 1)]
        qx_ready, mkT_ps, mkT_lo, mkT_hi, sx_ps, sx_negmax, sx_exp, sx_p, sxT_ps, sxT_ready, sxo_ps, sxo_done = (
            sem(n) for n in ("qx_ready", "mkT_ps", "mkT_lo", "mkT_hi", "sx_ps", "sx_negmax", "sx_exp", "sx_p",
                             "sxT_ps", "sxT_ready", "sxo_ps", "sxo_done"))
        softmax_in, softmax_exp = sem("softmax_in"), sem("softmax_exp")
        picks_ready, rank_ps, sel_ready, map_ps, plan_ready = (
            sem(n) for n in ("picks_ready", "rank_ps", "sel_ready", "map_ps", "plan_ready"))
        gu_in, down_in, xg_in, ye_out = ([sem(f"{n}{u}") for u in (0, 1)] for n in ("gu_in", "down_in", "xg_in", "ye_out"))
        xgT_ps, xgT_ready, gate_ps, up_ps, silu_ready, hid_ready, hidT_ps, hidT_ready, ye_ps, ye_rows = (
            sem(n) for n in ("xgT_ps", "xgT_ready", "gate_ps", "up_ps", "silu_ready", "hid_ready", "hidT_ps",
                             "hidT_ready", "ye_ps", "ye_rows"))
        yo_free, idx_ready, experts_done, ln3_in = sem("yo_free"), sem("idx_ready"), sem("experts_done"), sem("ln3_in")
        last_in = [sem(f"last_in{u}") for u in (0, 1)]
        var3_ready, rstd3_ready, y_ready = sem("var3_ready"), sem("rstd3_ready"), sem("y_ready")
        y_out = [sem(f"y_out{u}") for u in (0, 1)]

        block = ctx.enter_context(nc.Block())

        def tokens(p, s, t):
            return s if isinstance(t, int) and t == PT else p[ds(t * P, P), :]

        def two(j):
            return [(2 * j, 0, j), (2 * j + 1, 1, j)]

        LAST_TILE = [(PT, 0, PT // 2)]
        GB, GC, GV = QL + KL + DR, QL + KL + DR + CW, QL + KL + DR + 2 * CW

        @block.sync
        def _(sp):
            for u in (0, 1):
                sp.sem_inc(gb_out[u], 16)
                sp.sem_inc(lat_out[u], 32)
                sp.sem_inc(u_out[u], 16)
                sp.sem_inc(q_out[u], 16)
                sp.sem_inc(x2_out[u], 16)
                sp.sem_inc(y_out[u], 16)
            sp.dma_start(tables, A["tables"]).then_inc(tables_in, 16)
            sp.dma_start(mem, mem_rows).then_inc(mem_in, 16)
            sp.dma_start(w_xk, by_rows("w_xk")).then_inc(wxk_in, 16)
            sp.dma_start(w_xv, by_rows("w_xv")).then_inc(wxv_in, 16)
            for u in (0, 1):
                sp.dma_start(x_a[u], x_p[u * P:(u + 1) * P, :]).then_inc(x_in[u], 16)
            for k in range(4):
                sp.dma_start(w_in[k], w_in_rows[:, k, :]).then_inc(win_lo_in, 16)
            for dst, src in ((q_gain, A["q_norm_g"]), (kv_gain, A["kv_norm_g"]), (b_router[:, 0:NG], A["b_router_group"]),
                             (b_router[:, NG:], A["b_router_expert"].rearrange("l g e -> l (g e)")),
                             (shift2, A["ln2_b"])):
                sp.dma_start(dst, src.to_broadcast([P, dst.shape[1]])).then_inc(consts_in, 16)
            for k in range(3):
                sp.dma_start(conv_w[:, k, :], A["conv_w"][0, k:k + 1, :].to_broadcast([P, CW])).then_inc(consts_in, 16)
            sp.dma_start(w_router[:, :, 0:NG], by_rows("w_router_group")).then_inc(consts_in, 16)
            sp.dma_start(w_router[:, :, NG:], by_rows("w_router_expert")).then_inc(consts_in, 16)
            sp.dma_start(w_ukv, A["w_ukv"].rearrange("l p (h c) -> p (l h) c", h=H)).then_inc(win_hi_in, 16)
            sp.wait_ge(memT_ps, 2)
            sp.dma_start(w_uq, by_rows("w_uq")).then_inc(win_hi_in, 16)
            sp.wait_ge(memk_ps, 2)
            for k in range(4, KT):
                sp.dma_start(w_in[k], w_in_rows[:, k, :]).then_inc(win_hi_in, 16)
            sp.wait_ge(memk_rows, 2)
            sp.dma_start(mem_k_out, memk).then_inc(mem_out, 16)
            sp.wait_ge(memv_rows, 2)
            sp.dma_start(mem_v_out, memv).then_inc(mem_out, 16)
            sp.wait_ge(pads_zero, 1)
            sp.dma_start(u_dram[0:2, :], zero_row).then_inc(edge_out, 16)
            sp.dma_start(us_dram[:, 0:2, :], cache_conv).then_inc(edge_out, 16)

            def store_rows(tiles):
                for t, u, n in tiles:
                    sp.wait_ge(gb_ready, t + 1)
                    sp.dma_start(gb_dram[ds(t * P, P), :], gbs[u]).then_inc(gb_out[u], 16)
                for t, u, n in tiles:
                    sp.wait_ge(norm_done, t + 1)
                    sp.dma_start(tokens(lat_p, lat_s, t), ckvn[u]).then_inc(lat_out[u], 16)
                    sp.dma_start(tokens(kr_p, kr_s, t), krpad[u][:, DN:]).then_inc(lat_out[u], 16)
                for t, u, n in tiles:
                    sp.wait_ge(u_ready, t + 1)
                    if isinstance(t, int) and t == PT:
                        for b in range(NB):
                            sp.dma_start(us_dram[b, 2:, :], us[u][b * ROWS:(b + 1) * ROWS, :]).then_inc(edge_out, 16)
                        sp.sem_inc(u_out[u], 16)
                    else:
                        sp.dma_start(u_dram[ds(t * P + 2, P), :], us[u]).then_inc(u_out[u], 16)
                for t, u, n in tiles:
                    sp.wait_ge(q_turned, t + 1)
                    sp.dma_start(q_dram[ds(t * P, P), :], qrow[u]).then_inc(q_out[u], 16)

            with sp.Fori(0, 3) as j:
                for t, u, n in two(j):
                    sp.wait_ge(xT_ps, t + 1)
                    sp.dma_start(x_a[u], x_p[ds((t + 2) * P, P), :]).then_inc(x_in[u], 16)
                store_rows(two(j))
            sp.wait_ge(xT_ps, 7)
            sp.dma_start(x_a[0], x_s).then_inc(x_in[0], 16)
            store_rows(two(3))
            store_rows(LAST_TILE)

            for u, uses in ((0, 5), (1, 4)):
                sp.wait_ge(q_out[u], 16 + 16 * uses)
                sp.wait_ge(lat_out[u], 32 + 32 * uses)
                sp.wait_ge(u_out[u], 16 + 16 * uses)
                sp.wait_ge(gb_out[u], 16 + 16 * uses)
            sp.wait_ge(conv_ps, NT)
            q_heads = q_dram[0:PT * P, :].rearrange("(i p) c -> p i c", p=P)
            w_ukv_cols = A["w_ukv"].rearrange("l p c -> (l p) c")

            def load_head(h, u):
                sp.dma_start(qh[u], q_heads[:, :, ds(h * HW, HW)]).then_inc(head_in[u], 16)
                sp.dma_start(wk[u], w_ukv_cols[:, ds(h * (DN + DV), DN)]).then_inc(head_in[u], 16)

            load_head(0, 0)
            load_head(1, 1)
            sp.dma_start(w_out, by_rows("w_out")).then_inc(woq_in, 16)
            sp.dma_start(w_xq, by_rows("w_xq")).then_inc(woq_in, 16)
            sp.dma_start(q_s, q_dram[PT * P:, :].rearrange("p (h c) -> p h c", h=H)).then_inc(sq_in, 16)
            sp.dma_start(lat_new[0:ROWS, :, :], lat_s.rearrange("(b r) c -> r b c", r=ROWS)).then_inc(sq_in, 16)
            sp.wait_ge(edge_out, 16 * (2 + NB))
            sp.dma_start(conv_p, u_dram[PT * P:PT * P + 2, :]).then_inc(edge_out, 16)
            sp.dma_start(conv_s, us_dram[:, ROWS:, :]).then_inc(edge_out, 16)
            with sp.Fori(0, 3) as j:
                for h, u, n in two(j):
                    sp.wait_ge(kT_ps, h + 3)
                    load_head(h + 2, u)
            sp.wait_ge(kT_ps, 2 + H)

            with sp.Fori(0, NB // 2) as j:
                for b, u, n in two(j):
                    sp.wait_ge(ctx_ps, b + 1)
                    sp.dma_start(lat_b[u], cache_lat[ds(b, 1), :, :, :].rearrange("b p c d -> p (b c) d")).then_inc(cache_in[u], 16)
                    sp.dma_start(kr_b[u][:, :, DN:], cache_kr[ds(b, 1), :, :, :].rearrange("b p c d -> p (b c) d")).then_inc(cache_in[u], 16)

            sp.wait_ge(mixTs_ps, 1)

            def load_conv(t):
                if isinstance(t, int) and t == PT:
                    for k in range(3):
                        for b in range(NB):
                            sp.dma_start(cv[b * ROWS:(b + 1) * ROWS, k, :], us_dram[b, k:k + ROWS, :]).then_inc(conv_in, 16)
                else:
                    for k in range(3):
                        sp.dma_start(cv[:, k, :], u_dram[ds(t * P + k, P), :]).then_inc(conv_in, 16)
                sp.dma_start(cv[:, 3, :], gb_dram[ds(t * P, P), :]).then_inc(conv_in, 16)

            load_conv(0)
            for dst, name in ((gain1, "ln1_g"), (shift1, "ln1_b"), (gain2, "ln2_g")):
                sp.dma_start(dst, A[name].to_broadcast([P, D])).then_inc(ln_in, 16)
            sp.wait_ge(conv_ready, 1)
            load_conv(1)
            sp.dma_start(w_xo, by_rows("w_xo")).then_inc(wxo_in, 16)

            def load_x(tiles):
                for t, u, n in tiles:
                    sp.wait_ge(logits_done, t + 1)
                    sp.wait_ge(x2_out[u], 16 * n + 16)
                    sp.dma_start(xr[u], tokens(x_p, x_s, t)).then_inc(xr_in[u], 16)

            def store_x2(tiles):
                for t, u, n in tiles:
                    sp.wait_ge(x2_ready, t + 1)
                    sp.dma_start(x2_dram[ds(t * P, P), :], xr[u]).then_inc(x2_out[u], 16)

            with sp.Fori(0, 3) as j:
                load_x(two(j))
                for t, u, n in two(j):
                    sp.wait_ge(conv_ready, t + 2)
                    load_conv(t + 2)
                store_x2(two(j))
            load_x(two(3))
            sp.wait_ge(conv_ready, PT)
            load_conv(PT)
            store_x2(two(3))
            load_x(LAST_TILE)

            sp.wait_ge(x2_out[1], 16 + 16 * 4)
            with sp.Fori(0, NB // 2) as j:
                for b, u, n in two(j):
                    sp.wait_ge(sxo_ps, b + 1)
                    if u == 0:
                        sp.wait_ge(attn_copied, PT)
                    else:
                        sp.wait_ge(logits_done, PT + 2)
                    sp.dma_start(mk_b[u], cache_mk[ds(b, 1), :, :, :].rearrange("b p c d -> p (b c) d")).then_inc(mkv_in[u], 16)
                    sp.dma_start(mv_b[u], cache_mv[ds(b, 1), :, :, :].rearrange("b p c d -> p (b c) d")).then_inc(mkv_in[u], 16)
            store_x2(LAST_TILE)

            sp.wait_ge(logits_done, NT + 2)
            sp.dma_start(gain3, A["ln3_g"].to_broadcast([P, D])).then_inc(ln3_in, 16)
            sp.dma_start(shift3, A["ln3_b"].to_broadcast([P, D])).then_inc(ln3_in, 16)
            sp.wait_ge(plan_ready, 1)
            pairs = sp.value_load(plan[0:1, NBLK:NBLK + 1], min_val=1, max_val=NBLK // 2)
            with sp.Fori(0, NBLK // 2) as j:
                with sp.If(j < pairs):
                    for b, u, n in two(j):
                        e = sp.value_load(plan[0:1, ds(b, 1)], min_val=0, max_val=NE - 1)
                        sp.wait_ge(up_ps, b + 1)
                        sp.dma_start(w_g[u], w_gate[ds(e, 1), :, :, :].rearrange("e p k n -> p (e k) n")).then_inc(gu_in[u], 16)
                        sp.dma_start(w_u[u], w_up[ds(e, 1), :, :, :].rearrange("e p k n -> p (e k) n")).then_inc(gu_in[u], 16)
                        sp.wait_ge(ye_ps, b + 1)
                        sp.dma_start(w_d[u], w_down[ds(e, 1), :, :, :].rearrange("e p k n -> p (e k) n")).then_inc(down_in[u], 16)

            sp.wait_ge(experts_done, 1)

            def load_last(tiles):
                for t, u, n in tiles:
                    sp.wait_ge(y_out[u], 16 * n + 16)
                    sp.dma_start(yk[u], ye_pairs[ds(t * P, P), :, :]).then_inc(last_in[u], 16)
                    sp.dma_start(xl[u], x2_dram[ds(t * P, P), :]).then_inc(last_in[u], 16)

            def store_y(tiles):
                for t, u, n in tiles:
                    sp.wait_ge(y_ready, t + 1)
                    sp.dma_start(tokens(y_p, y_s, t), rl[u]).then_inc(y_out[u], 16)

            with sp.Fori(0, PT // 2) as j:
                load_last(two(j))
                store_y(two(j))
            load_last(LAST_TILE)
            store_y(LAST_TILE)
            sp.wait_ge(y_out[0], 16 + 16 * 5)
            sp.wait_ge(y_out[1], 16 + 16 * 4)
            sp.wait_ge(mem_out, 32)
            sp.wait_ge(edge_out, 16 * (4 + NB))
            sp.wait_ge(lat_out[0], 32 + 32 * 5)
            sp.wait_ge(lat_out[1], 32 + 32 * 4)
            sp.wait_ge(x2_out[0], 16 + 16 * 5)

        @block.tensor
        def _(pe):
            for two_ahead in (kT_ps, ctx_ps, sxo_ps, up_ps, ye_ps):
                pe.sem_inc(two_ahead, 2)

            def transposes(out, rows, n, width=P):
                for k in range(n):
                    got = nc.tensor.transpose(out[:, k * P:(k + 1) * P] if width == P else out[0:width, k * P:(k + 1) * P],
                                              rows[:, k * width:(k + 1) * width], ident)
                return got

            def product(out, lhsT, w, cols):
                for half, (c0, c1) in enumerate(cols):
                    for k in range(KT):
                        w_k = w[k] if isinstance(w, list) else w[:, k, :]
                        got = nc.tensor.matmul(out[:, half * 512:half * 512 + c1 - c0], lhsT[:, k, :], w_k[:, c0:c1],
                                               start=(k == 0), stop=(k == KT - 1))
                return got

            BOTH = [(0, 512), (512, 1024)]
            pe.wait_ge(tables_in, 16)
            pe.wait_ge(mem_in, 16)
            for c in (0, 1):
                transposes(T[c], mem[:, c, :], KT).then_inc(memT_ps, 1)
            pe.wait_ge(wxk_in, 16)
            for c in (0, 1):
                pe.wait_ge(memT_ready, c + 1)
                product(M[c], memT[:, c, :, :], w_xk, BOTH).then_inc(memk_ps, 1)
            pe.wait_ge(wxv_in, 16)
            for c in (0, 1):
                product(T[c], memT[:, c, :, :], w_xv, BOTH).then_inc(memv_ps, 1)
            for c in (0, 1):
                pe.wait_ge(memk_rows, c + 1)
                transposes(M[c], memk[:, c, :], KT).then_inc(memkT_ps, 1)
            pe.wait_ge(memv_rows, 2)
            pe.wait_ge(memkT_ready, 2)
            pe.wait_ge(win_lo_in, 64)
            pe.wait_ge(win_hi_in, 96)
            pe.wait_ge(pads_zero, 1)

            def project(tiles):
                for t, u, n in tiles:
                    pe.wait_ge(x_in[u], 16 * n + 16)
                    pe.wait_ge(q_rows, t + 1)
                    transposes(T[u], x_a[u], KT).then_inc(xT_ps, 1)
                for t, u, n in tiles:
                    pe.wait_ge(xT_ready, t + 1)
                    product(M[u], xT_a[u], w_in, [(0, GB), (GB, GC)]).then_inc(latent_ps, 1)
                for t, u, n in tiles:
                    product(T[u], xT_a[u], w_in, [(GC, GV), (GV, INW)]).then_inc(conv_ps, 1)
                for t, u, n in tiles:
                    pe.wait_ge(norm_done, t + 1)
                    transposes(M[u], cqn[u], 2)
                    nc.tensor.transpose(M[u][:, 2 * P:3 * P], ckvn[u], ident)
                    nc.tensor.transpose(M[u][0:HW, 3 * P:4 * P], krpad[u], ident).then_inc(cT_ps, 1)
                for t, u, n in tiles:
                    pe.wait_ge(cqT_ready, t + 1)
                    pe.wait_ge(u_ready, t + 1)
                    for dst, c in ((M[u][:, 512:896], 0), (T[u][:, 0:384], 384)):
                        for k in (0, 1):
                            got = nc.tensor.matmul(dst, cqT[u][:, k, :], w_uq[:, k, c:c + 384], start=(k == 0), stop=(k == 1))
                    got.then_inc(q_ps, 1)

            with pe.Fori(0, PT // 2) as j:
                project(two(j))
            project(LAST_TILE)

            pe.wait_ge(latT_ready, NT)
            pe.wait_ge(q_rows, 2 + NT)
            for c, dst in enumerate((T[0], T[1], M[0], M[1])):
                for i in (0, 1):
                    got = nc.tensor.matmul(dst[:, i * 512:(i + 1) * 512], latT[:, (2 * c + i) * P:(2 * c + i + 1) * P],
                                           w_ukv[:, :, DN:], start=True, stop=True)
                got.then_inc(value_ps, 1)
            pe.wait_ge(value_ready, 4)
            with pe.Fori(0, H // 2) as j:
                for h, u, n in two(j):
                    pe.wait_ge(head_in[u], 32 * n + 32)
                    pe.wait_ge(pT_ready, PT * h + 1)
                    for i in range(PT):
                        got = nc.tensor.transpose(M[0][0:HW, i * P:(i + 1) * P], qh[u][:, i, :], ident)
                    got.then_inc(qT_ps, 1)
                    pe.wait_ge(o_done, PT * h + 2)
                    for c in (0, 1):
                        got = nc.tensor.matmul(M[1][0:DN, c * 512:(c + 1) * 512], wk[u], latT[:, c * 512:(c + 1) * 512],
                                               start=True, stop=True)
                    got.then_inc(kT_ps, 1)
                    pe.wait_ge(qT_ready, h + 1)
                    pe.wait_ge(kT_ready, h + 1)

                    def scores(i):
                        pe.wait_ge(exp_done, PT * h + i + 1)
                        for c in range(0, (i + 1) * P, 512):
                            c1 = min(c + 512, (i + 1) * P)
                            got = nc.tensor.matmul(T[i % 2][:, c:c1], qT[u][0:HW, i * P:(i + 1) * P], kT[u][0:HW, c:c1],
                                                   start=True, stop=True)
                        got.then_inc(s_ps, 1)

                    scores(0)
                    scores(1)
                    for i in range(PT):
                        pe.wait_ge(exp_done, PT * h + i + 3)
                        pe.wait_ge(pT_ready, PT * h + i + 1)
                        transposes(M[0], pr[i % 2], i + 1).then_inc(pT_ps, 1)
                        if i + 2 < PT:
                            scores(i + 2)
                        pe.wait_ge(pT_ready, PT * h + i + 2)
                        pe.wait_ge(o_done, PT * h + i + 1)
                        o = M[1][:, (i % 2) * 512:(i % 2) * 512 + DV]
                        for c in range(i + 1):
                            got = nc.tensor.matmul(o, prT[:, c, :], value[:, c, ds(h * DV, DV)], start=(c == 0), stop=(c == i))
                        got.then_inc(o_ps, 1)

            pe.wait_ge(sq_in, 32)
            pe.wait_ge(pT_ready, PT * H + 1)
            for h in range(H):
                got = nc.tensor.transpose(M[0][0:HW, h * P:(h + 1) * P], q_s[:, h, :], ident)
            got.then_inc(sqT_ps, 1)
            for h in range(H):
                got = nc.tensor.transpose(T[0][0:DN, h * P:(h + 1) * P], w_ukv[:, h, 0:DN], ident)
            got.then_inc(sqT_ps, 1)
            pe.wait_ge(sqT_ready, 1)
            pe.wait_ge(wukT_ready, 1)
            pe.wait_ge(o_done, 2 + PT * H)
            for h in range(H):
                got = nc.tensor.matmul(M[1][:, h * P:(h + 1) * P], wukT[0:DN, h, :], qTs[0:DN, h, :], start=True, stop=True)
            got.then_inc(qabs_ps, 1)
            pe.wait_ge(qabs_ready, 1)
            pe.wait_ge(pads_zero, 2)
            N_KEYS = PAST + ROWS
            with pe.Fori(0, NB // 2) as j:
                for b, u, n in two(j):
                    pe.wait_ge(cache_in[u], 32 * n + 32)
                    for c in range(4):
                        nc.tensor.transpose(T[u][:, c * P:(c + 1) * P], lat_b[u][:, c, :], ident)
                    for c in range(4):
                        got = nc.tensor.transpose(T[u][0:HW, 512 + c * P:512 + (c + 1) * P], kr_b[u][:, c, :], ident)
                    got.then_inc(latb_ps, 1)
                for b, u, n in two(j):
                    pe.wait_ge(latb_ready, b + 1)
                    pe.wait_ge(bq_ready, b + 1)
                    pe.wait_ge(ctx_done, b + 1)
                    for c0, c1 in ((0, 512), (512, N_KEYS)):
                        nc.tensor.matmul(M[u][:, c0:c1], qa_b[u].rearrange("p h r -> p (h r)"), latTb[u][:, c0:c1], start=True, stop=False)
                        got = nc.tensor.matmul(M[u][:, c0:c1], qr_b[u][0:HW].rearrange("p h r -> p (h r)"), krTb[u][0:HW, c0:c1],
                                               start=False, stop=True)
                    got.then_inc(sb_ps, 1)
                for b, u, n in two(j):
                    pe.wait_ge(sb_p, b + 1)
                    transposes(T[u], p_b[u], 4)
                    nc.tensor.transpose(T[u][0:ROWS, 512:512 + P], p_b[u][:, PAST:], ident).then_inc(pTb_ps, 1)
                for b, u, n in two(j):
                    pe.wait_ge(pTb_ready, b + 1)
                    for c in range(4):
                        nc.tensor.matmul(M[u][:, 0:P], lat_b[u][:, c, :], pT_b[u][:, c, :], start=(c == 0), stop=False)
                    nc.tensor.matmul(M[u][:, 0:P], latn_b[u][0:ROWS, :], pT_b[u][0:ROWS, 4, :], start=False, stop=True).then_inc(ctx_ps, 1)
            pe.wait_ge(ctx_done, 2 + NB)
            for h in range(H):
                r = (h % 2) * DV
                got = nc.tensor.matmul(T[0][r:r + DV, (h // 2) * P:(h // 2 + 1) * P], w_ukv[:, h, DN:], ctxT[:, h, :],
                                       start=True, stop=True)
            got.then_inc(mixTs_ps, 1)

            pe.wait_ge(mixTs_ready, 1)
            pe.wait_ge(woq_in, 32)
            with pe.Fori(0, PT // 2) as j:
                def event(stage, u):
                    return 12 * j + 2 * stage + u + 1

                for t, u, n in two(j):
                    pe.wait_ge(attn_copied, t + 1)
                    pe.wait_ge(conv_ready, t + 1)
                    pe.wait_ge(logits_done, t + 1)
                    transposes(T[u], mix[u], 4)
                    transposes(T[u][:, 512:], conv_rows[u], 4).then_inc(rowsT_ps, 1)
                for t, u, n in two(j):
                    pe.wait_ge(rowsT_ready, event(0, u))
                    product(M[u], aT[u], w_out, BOTH).then_inc(product_ps, 1)
                for t, u, n in two(j):
                    pe.wait_ge(x1_ready, t + 1)
                    transposes(T[u], xr[u], KT).then_inc(rowsT_ps, 1)
                for t, u, n in two(j):
                    pe.wait_ge(rowsT_ready, event(1, u))
                    product(M[u], aT[u], w_xq, BOTH).then_inc(product_ps, 1)
                for t, u, n in two(j):
                    pe.wait_ge(xq_rows, t + 1)
                    transposes(T[u], res[u], KT).then_inc(rowsT_ps, 1)
                for t, u, n in two(j):
                    pe.wait_ge(rowsT_ready, event(2, u))
                    for h in range(XH):
                        for c in (0, 1):
                            got = nc.tensor.matmul(M[u][:, h * MEM:(h + 1) * MEM], aT[u][:, 2 * h + c, :], memkT[:, 2 * h + c, :],
                                                   start=(c == 0), stop=(c == 1))
                    got.then_inc(product_ps, 1)
                for t, u, n in two(j):
                    pe.wait_ge(px_ready, t + 1)
                    transposes(T[u], mix[u], KT).then_inc(rowsT_ps, 1)
                for t, u, n in two(j):
                    pe.wait_ge(rowsT_ready, event(3, u))
                    for h in range(XH):
                        for c in (0, 1):
                            got = nc.tensor.matmul(M[u][:, h * XD:(h + 1) * XD], aT[u][:, 2 * h + c, :], memv[:, c, h * XD:(h + 1) * XD],
                                                   start=(c == 0), stop=(c == 1))
                    got.then_inc(product_ps, 1)
                for t, u, n in two(j):
                    pe.wait_ge(ox_ready, t + 1)
                    transposes(T[u], res[u], KT).then_inc(rowsT_ps, 1)
                pe.wait_ge(wxo_in, 16)
                for t, u, n in two(j):
                    pe.wait_ge(rowsT_ready, event(4, u))
                    product(M[u], aT[u], w_xo, BOTH).then_inc(product_ps, 1)
                for t, u, n in two(j):
                    pe.wait_ge(x2_ready, t + 1)
                    transposes(T[u], xr[u], KT).then_inc(rowsT_ps, 1)
                for t, u, n in two(j):
                    pe.wait_ge(rowsT_ready, event(5, u))
                    for k in range(KT):
                        got = nc.tensor.matmul(M[u][:, 0:NG + NE], aT[u][:, k, :], w_router[:, k, :], start=(k == 0), stop=(k == KT - 1))
                    got.then_inc(product_ps, 1)

            E0 = 6 * PT
            pe.wait_ge(conv_ready, NT)
            pe.wait_ge(logits_done, NT)
            transposes(T[0][:, 512:], conv_rows[0], 4).then_inc(rowsT_ps, 1)
            pe.wait_ge(rowsT_ready, E0 + 1)
            product(M[0], aT[0], w_out, BOTH).then_inc(product_ps, 1)
            pe.wait_ge(x1_ready, NT)
            transposes(T[0], xr[0], KT).then_inc(rowsT_ps, 1)
            pe.wait_ge(rowsT_ready, E0 + 2)
            product(M[0], aT[0], w_xq, BOTH).then_inc(product_ps, 1)
            pe.wait_ge(xq_rows, NT)
            transposes(T[0], res[0], KT).then_inc(rowsT_ps, 1)
            pe.wait_ge(rowsT_ready, E0 + 3)

            def turn_memory(u, n):
                pe.wait_ge(mkv_in[u], 32 * n + 32)
                for c in (0, 1):
                    got = transposes(T[c], mk_b[u][:, c, :], KT)
                got.then_inc(mkT_ps, 1)

            def attend_memory(b, u, n, last):
                pe.wait_ge(mkT_lo, b + 1)
                pe.wait_ge(mkT_hi, b + 1)
                pe.wait_ge(qx_ready, b + 1)
                for h in range(XH):
                    for c in (0, 1):
                        got = nc.tensor.matmul(M[0][h * 32:(h + 1) * 32, 0:MEM], qx_b[:, 2 * h + c, :], mkT_b[:, 2 * h + c, :],
                                               start=(c == 0), stop=(c == 1))
                got.then_inc(sx_ps, 1)
                if not last:
                    turn_memory(1 - u, n + u)
                pe.wait_ge(sx_p, b + 1)
                transposes(M[0][:, 512:], px_b, 2).then_inc(sxT_ps, 1)
                pe.wait_ge(sxT_ready, b + 1)
                pe.wait_ge(sxo_done, b + 1)
                for h in range(XH):
                    for d in (0, 1):
                        for c in (0, 1):
                            got = nc.tensor.matmul(M[1][:, (2 * h + d) * ROWS:(2 * h + d + 1) * ROWS],
                                                   mv_b[u][:, c, h * XD + d * P:h * XD + (d + 1) * P],
                                                   pxT_b[:, c, h * 32:h * 32 + ROWS], start=(c == 0), stop=(c == 1))
                got.then_inc(sxo_ps, 1)

            turn_memory(0, 0)
            with pe.Fori(0, NB // 2 - 1) as j:
                for b, u, n in two(j):
                    attend_memory(b, u, n, False)
            for b, u, n in two(NB // 2 - 1):
                attend_memory(b, u, n, b == NB - 1)
            pe.wait_ge(sxo_done, NB + 1)
            product(M[0], oxT, w_xo, BOTH).then_inc(product_ps, 1)
            pe.wait_ge(x2_ready, NT)
            transposes(T[0], xr[0], KT).then_inc(rowsT_ps, 1)
            pe.wait_ge(rowsT_ready, E0 + 4)
            for k in range(KT):
                got = nc.tensor.matmul(M[0][:, 0:NG + NE], aT[0][:, k, :], w_router[:, k, :], start=(k == 0), stop=(k == KT - 1))
            got.then_inc(product_ps, 1)

            pe.wait_ge(picks_ready, 1)
            nc.tensor.matmul(T[0][:, 0:NT * NE], tri, picks, start=True, stop=True)
            nc.tensor.matmul(T[0][:, 512:512 + NT * NE], ones, picks, start=True, stop=True).then_inc(rank_ps, 1)
            for i in range(2 * NT):
                pe.wait_ge(sel_ready, i + 1)
                nc.tensor.matmul(M[1][:, 0:NBLK], sel_slot[i % 2], sel_blk[i % 2], start=(i == 0), stop=(i == 2 * NT - 1)).then_inc(map_ps, 1)

            pe.wait_ge(plan_ready, 1)
            pairs = pe.value_load(plan[0:1, NBLK:NBLK + 1], min_val=1, max_val=NBLK // 2)
            with pe.Fori(0, NBLK // 2) as j:
                with pe.If(j < pairs):
                    for b, u, n in two(j):
                        pe.wait_ge(xg_in[u], 16 * n + 16)
                        transposes(T[u], xg[u], KT).then_inc(xgT_ps, 1)
                    for b, u, n in two(j):
                        pe.wait_ge(xgT_ready, b + 1)
                        pe.wait_ge(gu_in[u], 32 * n + 32)
                        pe.wait_ge(ye_rows, b + 1)
                        product(M[u], xgT[u], w_g[u], [(0, 512)]).then_inc(gate_ps, 1)
                        product(M[u][:, 512:], xgT[u], w_u[u], [(0, 512)]).then_inc(up_ps, 1)
                        pe.wait_ge(hid_ready, b + 1)
                        transposes(T[u], hid[u], 4).then_inc(hidT_ps, 1)
                        pe.wait_ge(hidT_ready, b + 1)
                        pe.wait_ge(down_in[u], 16 * n + 16)
                        for half in (0, 1):
                            for k in range(4):
                                got = nc.tensor.matmul(M[u][:, half * 512:(half + 1) * 512], hidT[u][:, k, :],
                                                       w_d[u][:, k, half * 512:(half + 1) * 512], start=(k == 0), stop=(k == 3))
                        got.then_inc(ye_ps, 1)

        @block.scalar
        def _(act):
            act.sem_inc(q_rows, 2)
            act.sem_inc(exp_done, 2)
            act.sem_inc(sxo_done, 1)
            act.sem_inc(ye_rows, 2)
            for c in (0, 1):
                act.wait_ge(memT_ps, c + 1)
                nc.scalar.copy(memT[:, c, :, :].rearrange("p k c -> p (k c)"), T[c][:, :]).then_inc(memT_ready, 1)
            for c in (0, 1):
                act.wait_ge(memv_ps, c + 1)
                nc.scalar.copy(memv[:, c, :], T[c][:, :]).then_inc(memv_rows, 1)
            act.wait_ge(mem_out, 32)

            def project(tiles):
                for t, u, n in tiles:
                    act.wait_ge(xT_ps, t + 1)
                    nc.scalar.copy(xT_a[u].rearrange("p k c -> p (k c)"), T[u][:, :]).then_inc(xT_ready, 1)
                for t, u, n in tiles:
                    act.wait_ge(latent_ps, t + 1)
                    nc.scalar.activation(cqn[u], M[u][:, 0:QL], ACT.Square, scale=float(QL) ** -0.5, accum_out=sumsq[u][:, 0:1])
                    nc.scalar.activation(sq_junk[:, u * KL:(u + 1) * KL], M[u][:, QL:QL + KL], ACT.Square, scale=float(KL) ** -0.5,
                                         accum_out=sumsq[u][:, 1:2]).then_inc(sumsq_ready, 1)
                    act.wait_ge(gb_out[u], 16 * n + 16)
                    nc.scalar.copy(gbs[u], M[u][:, 512:1024]).then_inc(gb_ready, 1)
                for t, u, n in tiles:
                    act.wait_ge(conv_ps, t + 1)
                    nc.scalar.copy(gvs[u], T[u][:, 512:1024]).then_inc(gv_ready, 1)
                for t, u, n in tiles:
                    act.wait_ge(cT_ps, t + 1)
                    nc.scalar.copy(cqT[u].rearrange("p k c -> p (k c)"), M[u][:, 0:2 * P]).then_inc(cqT_ready, 1)
                    if isinstance(t, int) and t == PT:
                        nc.scalar.copy(latT[:, PT * P:], M[u][:, 2 * P:3 * P])
                        nc.scalar.copy(krTs[DN:HW, :], M[u][DN:HW, 3 * P:4 * P]).then_inc(latT_ready, 1)
                    else:
                        nc.scalar.copy(latT[:, ds(t * P, P)], M[u][:, 2 * P:3 * P])
                        nc.scalar.copy(kT[0][DN:HW, ds(t * P, P)], M[u][DN:HW, 3 * P:4 * P])
                        nc.scalar.copy(kT[1][DN:HW, ds(t * P, P)], M[u][DN:HW, 3 * P:4 * P]).then_inc(latT_ready, 1)
                for t, u, n in tiles:
                    act.wait_ge(q_ps, t + 1)
                    act.wait_ge(q_out[u], 16 * n + 16)
                    nc.scalar.copy(qrow[u][:, 0:384], M[u][:, 512:896])
                    nc.scalar.copy(qrow[u][:, 384:768], T[u][:, 0:384]).then_inc(q_rows, 1)

            with act.Fori(0, PT // 2) as j:
                project(two(j))
            project(LAST_TILE)

            act.wait_ge(q_turned, NT)
            for u, uses in ((0, 5), (1, 4)):
                act.wait_ge(q_out[u], 16 + 16 * uses)
                act.wait_ge(lat_out[u], 32 + 32 * uses)
                act.wait_ge(u_out[u], 16 + 16 * uses)
                act.wait_ge(gb_out[u], 16 + 16 * uses)
            act.wait_ge(edge_out, 16 * (2 + NB))
            for c, src in enumerate((T[0], T[1], M[0], M[1])):
                act.wait_ge(value_ps, c + 1)
                nc.scalar.copy(value[:, 2 * c:2 * c + 2, :].rearrange("p i c -> p (i c)"), src[:, :]).then_inc(value_ready, 1)
            with act.Fori(0, H // 2) as j:
                for h, u, n in two(j):
                    act.wait_ge(qT_ps, h + 1)
                    nc.scalar.mul(qT[u][0:HW, :], M[0][0:HW, :], MLA_SCALE).then_inc(qT_ready, 1)
                    for i in range(PT):
                        w = (i + 1) * P
                        act.wait_ge(negmax_ready, PT * h + i + 1)
                        nc.scalar.activation(pr[i % 2][:, 0:w], T[i % 2][:, 0:w], ACT.Exp, bias=negmax[i % 2][:, 0:1],
                                             scale=1.0, accum_out=rsum[i % 2][:, 0:1]).then_inc(exp_done, 1)

            act.wait_ge(sqT_ps, 1)
            nc.scalar.mul(qTs[0:HW, :, :].rearrange("p h c -> p (h c)"), M[0][0:HW, :], MLA_SCALE).then_inc(sqT_ready, 1)
            act.wait_ge(qabs_ps, 1)
            nc.scalar.copy(qabs.rearrange("p h c -> p (h c)"), M[1][:, :]).then_inc(qabs_ready, 1)
            with act.Fori(0, NB // 2) as j:
                for b, u, n in two(j):
                    act.wait_ge(latb_ps, b + 1)
                    nc.scalar.copy(latTb[u][:, 0:PAST], T[u][:, 0:512])
                    nc.scalar.copy(krTb[u][DN:HW, 0:PAST], T[u][DN:HW, 512:1024]).then_inc(latb_ready, 1)
                for b, u, n in two(j):
                    act.wait_ge(sb_negmax, b + 1)
                    nc.scalar.activation(p_b[u], M[u][:, 0:PAST + ROWS], ACT.Exp, bias=negmax[u][:, 0:1], scale=1.0,
                                         accum_out=rsum[u][:, 0:1]).then_inc(sb_exp, 1)
                for b, u, n in two(j):
                    act.wait_ge(pTb_ps, b + 1)
                    nc.scalar.copy(pT_b[u][:, 0:4, :].rearrange("p c q -> p (c q)"), T[u][:, 0:512])
                    nc.scalar.copy(pT_b[u][0:ROWS, 4, :], T[u][0:ROWS, 512:512 + P]).then_inc(pTb_ready, 1)
            act.wait_ge(mixTs_ps, 1)
            nc.scalar.copy(mixTs.rearrange("p k c -> p (k c)"), T[0][:, 0:512]).then_inc(mixTs_ready, 1)

            def turn(stage, u, base):
                act.wait_ge(rowsT_ps, base + 2 * stage + u + 1)
                nc.scalar.copy(aT[u].rearrange("p k c -> p (k c)"), T[u][:, :]).then_inc(rowsT_ready, 1)

            with act.Fori(0, PT // 2) as j:
                for t, u, n in two(j):
                    nc.scalar.copy(mix[u][:, 0:512], attn[:, ds(t, 1), :].rearrange("p a c -> p (a c)")).then_inc(attn_copied, 1)
                for t, u, n in two(j):
                    turn(0, u, 12 * j)
                for t, u, n in two(j):
                    turn(1, u, 12 * j)
                for t, u, n in two(j):
                    act.wait_ge(product_ps, 12 * j + 2 + u + 1)
                    nc.scalar.mul(res[u], M[u][:, :], X_SCALE).then_inc(xq_rows, 1)
                for t, u, n in two(j):
                    turn(2, u, 12 * j)
                for t, u, n in two(j):
                    act.wait_ge(xmax_ready, t + 1)
                    for h in range(XH):
                        got = nc.scalar.activation(mix[u][:, h * MEM:(h + 1) * MEM], M[u][:, h * MEM:(h + 1) * MEM], ACT.Exp,
                                                   bias=xmax[u][:, h:h + 1], scale=1.0, accum_out=xsum[u][:, h:h + 1])
                    got.then_inc(px_ready, 1)
                for stage in (3, 4, 5):
                    for t, u, n in two(j):
                        turn(stage, u, 12 * j)
            E0 = 6 * PT
            act.wait_ge(product_ps, E0)
            nc.scalar.copy(aT[0][:, 0:4, :].rearrange("p k c -> p (k c)"), mixTs.rearrange("p k c -> p (k c)"))
            act.wait_ge(rowsT_ps, E0 + 1)
            nc.scalar.copy(aT[0][:, 4:8, :].rearrange("p k c -> p (k c)"), T[0][:, 512:]).then_inc(rowsT_ready, 1)
            act.wait_ge(rowsT_ps, E0 + 2)
            nc.scalar.copy(aT[0].rearrange("p k c -> p (k c)"), T[0][:, :]).then_inc(rowsT_ready, 1)
            act.wait_ge(product_ps, E0 + 2)
            nc.scalar.mul(res[0], M[0][:, :], X_SCALE).then_inc(xq_rows, 1)
            act.wait_ge(rowsT_ps, E0 + 3)
            nc.scalar.copy(aT[0].rearrange("p k c -> p (k c)"), T[0][:, :]).then_inc(rowsT_ready, 1)

            def evacuate_memory(b):
                act.wait_ge(mkT_ps, b + 1)
                nc.scalar.copy(mkT_b[:, :, 0:P], T[0][:, :].rearrange("p (k c) -> p k c", k=KT)).then_inc(mkT_lo, 1)

            def attend_memory(b, last):
                act.wait_ge(sx_negmax, b + 1)
                nc.scalar.activation(px_b, M[0][:, 0:MEM], ACT.Exp, bias=negmax[0][:, 0:1], scale=1.0,
                                     accum_out=rsum[0][:, 0:1]).then_inc(sx_exp, 1)
                if not last:
                    evacuate_memory(b + 1)
                act.wait_ge(sxT_ps, b + 1)
                nc.scalar.copy(pxT_b.rearrange("p c q -> p (c q)"), M[0][:, 512:768]).then_inc(sxT_ready, 1)
                act.wait_ge(sxo_ps, b + 3)
                nc.scalar.copy(oxT[:, :, ds(b * ROWS, ROWS)], M[1][:, 0:P].rearrange("p (k r) -> p k r", k=KT)).then_inc(sxo_done, 1)

            evacuate_memory(0)
            with act.Fori(0, NB // 2 - 1) as j:
                for b, u, n in two(j):
                    attend_memory(b, False)
            for b, u, n in two(NB // 2 - 1):
                attend_memory(b, b == NB - 1)
            act.wait_ge(rowsT_ps, E0 + 4)
            nc.scalar.copy(aT[0].rearrange("p k c -> p (k c)"), T[0][:, :]).then_inc(rowsT_ready, 1)

            act.wait_ge(softmax_in, 1)
            nc.scalar.activation(r_eg, r_gd, ACT.Exp).then_inc(softmax_exp, 1)
            act.wait_ge(softmax_in, 2)
            nc.scalar.activation(r_e2, r_d2, ACT.Exp).then_inc(softmax_exp, 1)

            act.wait_ge(plan_ready, 1)
            pairs = act.value_load(plan[0:1, NBLK:NBLK + 1], min_val=1, max_val=NBLK // 2)
            with act.Fori(0, NBLK // 2) as j:
                with act.If(j < pairs):
                    for b, u, n in two(j):
                        act.wait_ge(xgT_ps, b + 1)
                        nc.scalar.copy(xgT[u].rearrange("p k c -> p (k c)"), T[u][:, :]).then_inc(xgT_ready, 1)
                    for b, u, n in two(j):
                        act.wait_ge(gate_ps, b + 1)
                        nc.scalar.activation(hid[u], M[u][:, 0:512], ACT.Silu).then_inc(silu_ready, 1)
                        act.wait_ge(hidT_ps, b + 1)
                        nc.scalar.copy(hidT[u].rearrange("p k c -> p (k c)"), T[u][:, 0:512]).then_inc(hidT_ready, 1)
                        act.wait_ge(ye_ps, b + 3)
                        act.wait_ge(yo_free, j + 1)
                        nc.scalar.copy(yo[u], M[u][:, :]).then_inc(ye_rows, 1)

        @block.vector
        def _(dve):
            step = Count("dve")

            dve.sem_inc(o_done, 2)
            dve.sem_inc(pT_ready, 1)
            dve.sem_inc(ctx_done, 2)
            dve.sem_inc(logits_done, 2)
            for c in (0, 1):
                dve.wait_ge(memk_ps, c + 1)
                nc.vector.tensor_copy(memk[:, c, :], M[c][:, :]).then_inc(memk_rows, 1)
            for c in (0, 1):
                dve.wait_ge(memkT_ps, c + 1)
                nc.vector.tensor_copy(memkT[:, :, c * P:(c + 1) * P], M[c][:, :].rearrange("p (k c) -> p k c", k=KT)).then_inc(memkT_ready, 1)
            dve.wait_ge(consts_in, 16 * 10)
            dve.wait_ge(pads_zero, 1)

            def turn_rows(t, x, heads, rot):
                half = DR // 2
                cos = rope[:, ds(t, 1), 0:DR].to_broadcast([P, heads, DR])
                msin = rope[:, ds(t, 1), DR:DR + half].to_broadcast([P, heads, half])
                sin = rope[:, ds(t, 1), DR + half:].to_broadcast([P, heads, half])
                a, b = rot
                nc.vector.tensor_tensor(a, x, cos, ALU.mult)
                nc.vector.tensor_tensor(b[:, :, 0:half], x[:, :, half:], msin, ALU.mult)
                nc.vector.tensor_tensor(b[:, :, half:], x[:, :, 0:half], sin, ALU.mult).then_inc(dve_step, step.next())
                dve.wait_ge(dve_step, step.value())
                return a, b

            def project(tiles):
                for t, u, n in tiles:
                    dve.wait_ge(rrms_ready, t + 1)
                    nc.vector.scalar_tensor_tensor(cqn[u], M[u][:, 0:QL], rrms[u][:, 0:1], q_gain, ALU.mult, ALU.mult)
                    dve.wait_ge(lat_out[u], 32 * n + 32)
                    nc.vector.scalar_tensor_tensor(ckvn[u], M[u][:, QL:QL + KL], rrms[u][:, 1:2], kv_gain, ALU.mult, ALU.mult)
                    a, b = turn_rows(t, M[u][:, QL + KL:QL + KL + DR].rearrange("p (h c) -> p h c", h=1), 1, rot_k[u])
                    nc.vector.tensor_tensor(krpad[u][:, DN:].rearrange("p (h c) -> p h c", h=1), a, b, ALU.add).then_inc(norm_done, 1)
                for t, u, n in tiles:
                    dve.wait_ge(gv_ready, t + 1)
                    dve.wait_ge(u_out[u], 16 * n + 16)
                    nc.vector.tensor_tensor(us[u], T[u][:, 0:CW], gvs[u], ALU.mult).then_inc(u_ready, 1)
                for t, u, n in tiles:
                    dve.wait_ge(q_rows, t + 3)
                    x = qrow[u].rearrange("p (h c) -> p h c", h=H)[:, :, DN:]
                    a, b = turn_rows(t, x, H, rot_q[u])
                    nc.vector.tensor_tensor(x, a, b, ALU.add).then_inc(q_turned, 1)

            with dve.Fori(0, PT // 2) as j, step.loop(j, 4, PT // 2):
                project(two(j))
            project(LAST_TILE)

            dve.wait_ge(value_ready, 4)
            with dve.Fori(0, H // 2) as j, step.loop(j, 4 * PT, H // 2):
                for h, u, n in two(j):
                    dve.wait_ge(kT_ps, h + 3)
                    nc.vector.tensor_copy(kT[u][0:DN, :], M[1][0:DN, :]).then_inc(kT_ready, 1)

                    def row_max(i):
                        s, w = i % 2, (i + 1) * P
                        dve.wait_ge(s_ps, PT * h + i + 1)
                        nc.vector.memset(T[s][0:64, w - 64:w], FAR).then_inc(dve_step, step.next())
                        dve.wait_ge(dve_step, step.value())
                        nc.vector.tensor_reduce(negmax[s][:, 0:1], T[s][:, 0:w], AX.X, ALU.max, negate=True).then_inc(negmax_ready, 1)

                    row_max(0)
                    row_max(1)
                    for i in range(PT):
                        s, w = i % 2, (i + 1) * P
                        dve.wait_ge(pT_ps, PT * h + i + 1)
                        nc.vector.tensor_copy(prT[:, 0:i + 1, :].rearrange("p i c -> p (i c)"), M[0][:, 0:w]).then_inc(pT_ready, 1)
                        nc.vector.reciprocal(rinv[s][:, 0:1], rsum[s][:, 0:1]).then_inc(dve_step, step.next())
                        inverse_at = step.value()
                        if i + 2 < PT:
                            row_max(i + 2)
                        dve.wait_ge(o_ps, PT * h + i + 1)
                        dve.wait_ge(dve_step, inverse_at)
                        nc.vector.tensor_scalar(attn[:, i, ds(h * DV, DV)], M[1][:, s * 512:s * 512 + DV], rinv[s][:, 0:1], None,
                                                ALU.mult).then_inc(o_done, 1)

            dve.wait_ge(sqT_ps, 2)
            nc.vector.tensor_copy(wukT[0:DN, :, :].rearrange("p h c -> p (h c)"), T[0][0:DN, :]).then_inc(wukT_ready, 1)
            dve.wait_ge(qabs_ready, 1)
            dve.wait_ge(sqT_ready, 1)
            dve.wait_ge(sq_in, 32)
            with dve.Fori(0, NB // 2) as j, step.loop(j, 2, NB // 2):
                for b, u, n in two(j):
                    dve.wait_ge(ctx_ps, b + 1)
                    nc.vector.tensor_copy(qa_b[u], qabs[:, :, ds(b * ROWS, ROWS)])
                    nc.vector.tensor_copy(qr_b[u][0:HW], qTs[0:HW, :, ds(b * ROWS, ROWS)])
                    nc.vector.tensor_copy(latn_b[u][0:ROWS, :], lat_new[0:ROWS, ds(b, 1), :].rearrange("p a c -> p (a c)"))
                    nc.vector.tensor_copy(latTb[u][:, PAST:], latT[:, ds(PT * P + b * ROWS, ROWS)])
                    nc.vector.tensor_copy(krTb[u][DN:HW, PAST:], krTs[DN:HW, ds(b * ROWS, ROWS)]).then_inc(bq_ready, 1)
                for b, u, n in two(j):
                    dve.wait_ge(sb_ps, b + 1)
                    nc.vector.tensor_reduce(negmax[u][:, 0:1], M[u][:, 0:PAST + ROWS], AX.X, ALU.max, negate=True).then_inc(sb_negmax, 1)
                for b, u, n in two(j):
                    dve.wait_ge(sb_exp, b + 1)
                    nc.vector.reciprocal(rinv[u][:, 0:1], rsum[u][:, 0:1]).then_inc(dve_step, step.next())
                    dve.wait_ge(dve_step, step.value())
                    nc.vector.tensor_scalar(p_b[u], p_b[u], rinv[u][:, 0:1], None, ALU.mult).then_inc(sb_p, 1)
                for b, u, n in two(j):
                    dve.wait_ge(ctx_ps, b + 3)
                    nc.vector.tensor_copy(ctxT[:, :, ds(b * ROWS, ROWS)], M[u][:, 0:P].rearrange("p (h r) -> p h r", h=H)).then_inc(ctx_done, 1)

            dve.wait_ge(ln_in, 48)

            def add_norm(tiles, product_at, gain, shift, out_ready):
                for t, u, n in tiles:
                    dve.wait_ge(product_ps, product_at(u))
                    nc.vector.scalar_tensor_tensor(res[u], xr[u], ALPHA, M[u][:, :], ALU.mult, ALU.add).then_inc(dve_step, step.next())
                    dve.wait_ge(dve_step, step.value())
                    nc.vector.bn_stats(stats[u][:, 0:6], res[u][:, 0:512])
                    nc.vector.bn_stats(stats[u][:, 6:12], res[u][:, 512:]).then_inc(dve_step, step.next())
                    dve.wait_ge(dve_step, step.value())
                    dve.sem_inc(dve_waited, 1)
                    nc.vector.bn_aggr(moments[u][:, :], stats[u][:, :]).then_inc(var_ready, 1)
                for t, u, n in tiles:
                    dve.wait_ge(rstd_ready, norms[0] + u + 1)
                    nc.vector.tensor_scalar(res[u], res[u], moments[u][:, 0:1], rstd[u][:, 0:1], ALU.subtract, ALU.mult)\
                        .then_inc(dve_step, step.next())
                    dve.wait_ge(dve_step, step.value())
                    nc.vector.tensor_tensor(res[u], res[u], gain, ALU.mult).then_inc(dve_step, step.next())
                    dve.wait_ge(dve_step, step.value())
                    nc.vector.tensor_tensor(xr[u], res[u], shift, ALU.add).then_inc(out_ready, 1)

            with dve.Fori(0, PT // 2) as j, step.loop(j, 18, PT // 2):
                for t, u, n in two(j):
                    dve.wait_ge(xr_in[u], 16 * n + 16)
                norms = [4 * j]
                add_norm(two(j), lambda u: 12 * j + u + 1, gain1, shift1, x1_ready)
                for t, u, n in two(j):
                    dve.wait_ge(product_ps, 12 * j + 4 + u + 1)
                    nc.vector.tensor_reduce(xmax[u][:, :], M[u][:, :].rearrange("p (h m) -> p h m", h=XH), AX.X, ALU.max,
                                            negate=True).then_inc(xmax_ready, 1)
                for t, u, n in two(j):
                    dve.wait_ge(px_ready, t + 1)
                    nc.vector.reciprocal(xsum[u][:, :], xsum[u][:, :]).then_inc(dve_step, step.next())
                    dve.wait_ge(dve_step, step.value())
                    dve.wait_ge(product_ps, 12 * j + 6 + u + 1)
                    nc.vector.tensor_tensor(res[u].rearrange("p (h d) -> p h d", h=XH), M[u][:, :].rearrange("p (h d) -> p h d", h=XH),
                                            xsum[u][:, :].unsqueeze(2).to_broadcast([P, XH, XD]), ALU.mult).then_inc(ox_ready, 1)
                norms[0] = 4 * j + 2
                add_norm(two(j), lambda u: 12 * j + 8 + u + 1, gain2, shift2, x2_ready)
                for t, u, n in two(j):
                    dve.wait_ge(product_ps, 12 * j + 10 + u + 1)
                    nc.vector.tensor_tensor(logits[:, ds(t, 1), :].rearrange("p a c -> p (a c)"), M[u][:, 0:NG + NE], b_router[:, :],
                                            ALU.add).then_inc(logits_done, 1)

            E0 = 6 * PT
            norms = [2 * PT]
            dve.wait_ge(xr_in[0], 16 * 5)
            add_norm(LAST_TILE, lambda u: E0 + 1, gain1, shift1, x1_ready)
            dve.wait_ge(conv_ready, NT)
            nc.vector.memset(qx_b, 0.0).then_inc(dve_step, step.next())
            dve.wait_ge(dve_step, step.value())
            dve.wait_ge(rowsT_ready, E0 + 3)

            def evacuate_memory(b):
                dve.wait_ge(mkT_ps, b + 1)
                nc.vector.tensor_copy(mkT_b[:, :, P:], T[1][:, :].rearrange("p (k c) -> p k c", k=KT)).then_inc(mkT_hi, 1)

            def attend_memory(b, last):
                if not (isinstance(b, int) and b == 0):
                    dve.wait_ge(sx_ps, b)
                nc.vector.tensor_copy(qx_b[:, :, 0:ROWS], aT[0][:, :, ds(b * ROWS, ROWS)]).then_inc(qx_ready, 1)
                dve.wait_ge(sx_ps, b + 1)
                nc.vector.tensor_reduce(negmax[0][:, 0:1], M[0][:, 0:MEM], AX.X, ALU.max, negate=True).then_inc(sx_negmax, 1)
                dve.wait_ge(sx_exp, b + 1)
                nc.vector.reciprocal(rinv[0][:, 0:1], rsum[0][:, 0:1]).then_inc(dve_step, step.next())
                dve.wait_ge(dve_step, step.value())
                nc.vector.tensor_scalar(px_b, px_b, rinv[0][:, 0:1], None, ALU.mult).then_inc(sx_p, 1)
                if not last:
                    evacuate_memory(b + 1)

            evacuate_memory(0)
            attend_memory(0, False)
            attend_memory(1, False)
            with dve.Fori(1, NB // 2 - 1) as j, step.loop(j - 1, 2, NB // 2 - 2):
                for b, u, n in two(j):
                    attend_memory(b, False)
            for b, u, n in two(NB // 2 - 1):
                attend_memory(b, b == NB - 1)
            norms = [2 * PT + 1]
            add_norm(LAST_TILE, lambda u: E0 + 3, gain2, shift2, x2_ready)
            dve.wait_ge(product_ps, E0 + 4)
            nc.vector.tensor_tensor(logits[:, PT, :], M[0][:, 0:NG + NE], b_router[:, :], ALU.add).then_inc(logits_done, 1)

            def then(ins):
                ins.then_inc(dve_step, step.next())
                dve.wait_ge(dve_step, step.value())

            def wide(x, *shape):
                return x.unsqueeze(len(x.shape)).to_broadcast([P, *shape])

            def first_largest(values, n, best, scratch, pick):
                then(nc.vector.tensor_reduce(best, values, AX.X, ALU.max))
                then(nc.vector.tensor_tensor(scratch, values, wide(best, NT, n), ALU.is_equal))
                then(nc.vector.scalar_tensor_tensor(scratch, scratch, -64.0, iota[:, 0:n].unsqueeze(1).to_broadcast([P, NT, n]),
                                                    ALU.mult, ALU.add))
                then(nc.vector.tensor_reduce(r_first, scratch, AX.X, ALU.min))
                then(nc.vector.tensor_tensor(pick, scratch, wide(r_first, NT, n), ALU.is_equal))

            dve.wait_ge(logits_done, NT + 2)
            lg, le = logits[:, :, 0:NG], logits[:, :, NG:].rearrange("p t (g e) -> p t g e", g=NG)
            first_largest(lg, NG, r_best, r_s4, r_group)
            nc.vector.tensor_tensor(r_gd, lg, wide(r_best, NT, NG), ALU.subtract).then_inc(softmax_in, 1)
            then(nc.vector.tensor_tensor(r_all, le, wide(r_group, NT, NG, EG), ALU.mult))
            then(nc.vector.tensor_reduce(r_le, r_all.rearrange("p t g e -> p t e g"), AX.X, ALU.add))
            first_largest(r_le, EG, r_v1, r_s8, r_pick1)
            then(nc.vector.scalar_tensor_tensor(r_le, r_pick1, FAR, r_le, ALU.mult, ALU.add))
            first_largest(r_le, EG, r_v2, r_s8, r_pick2)
            nc.vector.tensor_tensor(r_d2, r_v2, r_v1, ALU.subtract).then_inc(softmax_in, 1)
            for k, pick in ((0, r_pick1), (1, r_pick2)):
                for g in range(NG):
                    got = nc.vector.tensor_tensor(r_hot[:, k, :, g * EG:(g + 1) * EG], pick,
                                                  r_group[:, :, g:g + 1].to_broadcast([P, NT, EG]), ALU.mult)
            then(got)
            nc.vector.tensor_tensor(picks.rearrange("p (t e) -> p t e", t=NT), r_hot[:, 0], r_hot[:, 1], ALU.add).then_inc(picks_ready, 1)
            dve.wait_ge(softmax_exp, 1)
            then(nc.vector.tensor_reduce(r_sum, r_eg, AX.X, ALU.add))
            dve.wait_ge(softmax_exp, 2)
            then(nc.vector.scalar_tensor_tensor(r_den, r_e2, 1.0, r_sum, ALU.add, ALU.mult))
            then(nc.vector.reciprocal(gates[:, 0, :], r_den))
            then(nc.vector.tensor_tensor(gates[:, 1, :], gates[:, 0, :], r_e2, ALU.mult))
            dve.wait_ge(rank_ps, 1)
            then(nc.vector.memset(r_before[:, 0, :], 0.0))
            then(nc.vector.tensor_copy(r_total, T[0][:, 512:512 + NT * NE].rearrange("p (t e) -> p t e", t=NT)))
            for t in range(NT):
                then(nc.vector.tensor_tensor(r_before[:, t + 1, :], r_before[:, t, :], r_total[:, t, :], ALU.add))
            then(nc.vector.tensor_tensor(r_rank, r_before[:, 0:NT, :], T[0][:, 0:NT * NE].rearrange("p (t e) -> p t e", t=NT), ALU.add))
            then(nc.vector.tensor_scalar(r_lim, iota[:, 0:NT], float(P), None, ALU.mult))
            then(nc.vector.tensor_tensor(r_cmp, wide(r_before[:, NT, :], NE, NT), r_lim.unsqueeze(1).to_broadcast([P, NE, NT]), ALU.is_gt))
            then(nc.vector.tensor_reduce(r_blocks, r_cmp, AX.X, ALU.add))
            then(nc.vector.tensor_tensor_scan(r_end, ones[:, 0:NE], r_blocks, 0.0, ALU.mult, ALU.add))
            then(nc.vector.tensor_tensor(r_start, r_end, r_blocks, ALU.subtract))
            then(nc.vector.scalar_tensor_tensor(r_rank, r_start.unsqueeze(1).to_broadcast([P, NT, NE]), float(P), r_rank, ALU.mult, ALU.add))
            for k in (0, 1):
                then(nc.vector.tensor_tensor(r_hot[:, k], r_hot[:, k], r_rank, ALU.mult))
                then(nc.vector.tensor_reduce(r_slot[:, :, k], r_hot[:, k], AX.X, ALU.add))
            then(nc.vector.tensor_copy(r_int, r_slot.rearrange("p t k -> p (t k)")))
            then(nc.vector.tensor_single_scalar(r_int2, r_int, 7, ALU.logical_shift_right))
            then(nc.vector.tensor_copy(r_blk, r_int2))
            then(nc.vector.tensor_single_scalar(r_int2, r_int, P - 1, ALU.bitwise_and))
            then(nc.vector.tensor_copy(r_pos, r_int2))
            for i in range(2 * NT):
                if i >= 2:
                    dve.wait_ge(map_ps, i - 1)
                nc.vector.tensor_scalar(sel_slot[i % 2], iota, r_pos[:, i:i + 1], None, ALU.is_equal)
                nc.vector.tensor_scalar(sel_blk[i % 2], iota[:, 0:NBLK], r_blk[:, i:i + 1], slot_id.rearrange("p t k -> p (t k)")[:, i:i + 1],
                                        ALU.is_equal, ALU.mult).then_inc(sel_ready, 1)
            then(nc.vector.tensor_tensor(r_plan[0:1], iota[0:1, 0:NBLK].unsqueeze(2).to_broadcast([1, NBLK, NE]),
                                         r_end[0:1, :].unsqueeze(1).to_broadcast([1, NBLK, NE]), ALU.is_ge))
            then(nc.vector.tensor_reduce(r_row[0:1, 0:NBLK], r_plan[0:1], AX.X, ALU.add))
            then(nc.vector.tensor_scalar(r_row[0:1, 0:NBLK], r_row[0:1, 0:NBLK], float(NE - 1), None, ALU.min))
            then(nc.vector.tensor_scalar(r_row[0:1, NBLK:NBLK + 1], r_end[0:1, NE - 1:NE], 1.0, None, ALU.add))
            then(nc.vector.tensor_copy(r_int3[0:1, :], r_row[0:1, 0:NBLK + 1]))
            then(nc.vector.tensor_single_scalar(plan[0:1, NBLK:NBLK + 1], r_int3[0:1, NBLK:NBLK + 1], 1, ALU.logical_shift_right))
            then(nc.vector.tensor_copy(plan[0:1, 0:NBLK], r_int3[0:1, 0:NBLK]))
            dve.wait_ge(map_ps, 2 * NT)
            then(nc.vector.tensor_scalar(r_map, M[1][:, 0:NBLK], 0.0, 8192.0, ALU.is_equal, ALU.mult))
            then(nc.vector.scalar_tensor_tensor(r_map, M[1][:, 0:NBLK], -1.0, r_map, ALU.add, ALU.add))
            then(nc.vector.tensor_copy(route_out[:, 0:NBLK], r_map))
            then(nc.vector.tensor_copy(r_mapi, r_map))
            then(nc.vector.tensor_single_scalar(r_mapi2, r_mapi, 1, ALU.logical_shift_right))
            then(nc.vector.memset(route_tok[:, NBLK:], 0))
            nc.vector.tensor_scalar(route_tok[:, 0:NBLK], r_mapi2, float(NT * P - 1), None, ALU.min).then_inc(plan_ready, 1)

            dve.wait_ge(plan_ready, 1)
            pairs = dve.value_load(plan[0:1, NBLK:NBLK + 1], min_val=1, max_val=NBLK // 2)
            with dve.Fori(0, NBLK // 2) as j:
                with dve.If(j < pairs):
                    for b, u, n in two(j):
                        dve.wait_ge(silu_ready, b + 1)
                        dve.wait_ge(up_ps, b + 3)
                        nc.vector.tensor_tensor(hid[u], hid[u], M[u][:, 512:1024], ALU.mult).then_inc(hid_ready, 1)

            dve.wait_ge(ln3_in, 32)

            def last(tiles, n0):
                for t, u, n in tiles:
                    dve.wait_ge(last_in[u], 32 * n + 32)
                    dve.wait_ge(y_out[u], 16 * n + 16)
                    g = gates[:, :, ds(t, 1)]
                    then(nc.vector.tensor_scalar(rl[u], yk[u][:, 0, :], gates[:, 0, ds(t, 1)], None, ALU.mult))
                    then(nc.vector.scalar_tensor_tensor(rl[u], yk[u][:, 1, :], gates[:, 1, ds(t, 1)], rl[u], ALU.mult, ALU.add))
                    then(nc.vector.scalar_tensor_tensor(rl[u], xl[u], ALPHA, rl[u], ALU.mult, ALU.add))
                    nc.vector.bn_stats(stats[u][:, 0:6], rl[u][:, 0:512])
                    then(nc.vector.bn_stats(stats[u][:, 6:12], rl[u][:, 512:]))
                    dve.sem_inc(dve_waited, 1)
                    nc.vector.bn_aggr(moments[u][:, :], stats[u][:, :]).then_inc(var3_ready, 1)
                for t, u, n in tiles:
                    dve.wait_ge(rstd3_ready, t + 1)
                    then(nc.vector.tensor_scalar(rl[u], rl[u], moments[u][:, 0:1], rstd[u][:, 0:1], ALU.subtract, ALU.mult))
                    then(nc.vector.tensor_tensor(rl[u], rl[u], gain3, ALU.mult))
                    nc.vector.tensor_tensor(rl[u], rl[u], shift3, ALU.add).then_inc(y_ready, 1)

            with dve.Fori(0, PT // 2) as j, step.loop(j, 12, PT // 2):
                last(two(j), 0)
            last(LAST_TILE, 0)

        @block.gpsimd
        def _(pool):
            step = Count("pool")
            pool.sem_inc(yo_free, 1)
            nc.gpsimd.memset(minus_half[:, :], -0.5)
            nc.gpsimd.memset(zero_row[:, :], 0.0)
            pool.wait_ge(memv_ps, 2)
            nc.gpsimd.memset(krpad[0][:, 0:DN], 0.0)
            nc.gpsimd.memset(krpad[1][:, 0:DN], 0.0).then_inc(pads_zero, 1)
            pool.wait_ge(pads_zero, 1)

            def inverse_root(out, x, eps):
                pool.sem_inc(pool_waited, 1)
                nc.gpsimd.tensor_scalar(x, x, eps, None, ALU.add).then_inc(pool_step, step.next())
                pool.wait_ge(pool_step, step.value())
                return nc.gpsimd.tensor_tensor(out, x, minus_half[:, 0:x.shape[1]], ALU.pow)

            def latents(tiles):
                for t, u, n in tiles:
                    pool.wait_ge(sumsq_ready, t + 1)
                    inverse_root(rrms[u][:, :], sumsq[u][:, :], RMS_EPS).then_inc(rrms_ready, 1)

            with pool.Fori(0, PT // 2) as j, step.loop(j, 2, PT // 2):
                latents(two(j))
            latents(LAST_TILE)

            pool.wait_ge(kT_ps, 2 + H)
            pool.wait_ge(o_done, 2 + PT * H)
            for u in (0, 1):
                nc.gpsimd.memset(kr_b[u][:, :, 0:DN], 0.0)
                got = nc.gpsimd.memset(krTb[u][0:DN, :], 0.0)
            got.then_inc(pads_zero, 1)

            pool.wait_ge(consts_in, 16 * 10)

            def convolve(u, loads, turned):
                pool.wait_ge(conv_in, loads)
                if turned is not None:
                    pool.wait_ge(rowsT_ps, turned)
                out = conv_rows[u]
                nc.gpsimd.tensor_tensor(cv[:, 0:3, :], cv[:, 0:3, :], conv_w[:, :, :], ALU.mult).then_inc(pool_step, step.next())
                pool.wait_ge(pool_step, step.value())
                nc.gpsimd.tensor_tensor(out, cv[:, 0, :], cv[:, 1, :], ALU.add).then_inc(pool_step, step.next())
                pool.wait_ge(pool_step, step.value())
                nc.gpsimd.tensor_tensor(out, out, cv[:, 2, :], ALU.add).then_inc(pool_step, step.next())
                pool.wait_ge(pool_step, step.value())
                nc.gpsimd.tensor_tensor(out, out, cv[:, 3, :], ALU.mult).then_inc(conv_ready, 1)

            def deviation(u, at):
                pool.wait_ge(var_ready, at)
                inverse_root(rstd[u][:, :], moments[u][:, 1:2], LN_EPS).then_inc(rstd_ready, 1)

            convolve(0, 64, None)
            convolve(1, 128, None)
            with pool.Fori(0, PT // 2 - 1) as j, step.loop(j, 10, PT // 2 - 1):
                deviation(0, 4 * j + 1)
                deviation(1, 4 * j + 2)
                convolve(0, 128 * j + 192, 12 * j + 1)
                convolve(1, 128 * j + 256, 12 * j + 2)
                deviation(0, 4 * j + 3)
                deviation(1, 4 * j + 4)
            deviation(0, 13)
            deviation(1, 14)
            convolve(0, 64 * PT + 16 * (3 * NB + 1), 37)
            for at in (15, 16, 17, 18):
                deviation(0 if at != 16 else 1, at)

            pool.wait_ge(x2_out[0], 16 + 16 * 5)
            pool.wait_ge(x2_out[1], 16 + 16 * 4)
            pool.wait_ge(plan_ready, 1)

            def gather(b, u, copied):
                nc.gpsimd.tensor_copy(tok_now[u][:, :], route_tok[:, ds(b, 1)]).then_inc(idx_ready, 1)
                pool.wait_ge(idx_ready, copied)
                pool.sem_inc(pool_waited, 1)
                nc.gpsimd.indirect_dma_start(out=xg[u], out_offset=None, in_=x2_dram,
                                             in_offset=bass.IndirectOffsetOnAxis(ap=tok_now[u][:, 0:1], axis=0)).then_inc(xg_in[u], 16)

            gather(0, 0, 1)
            gather(1, 1, 2)
            pairs = pool.value_load(plan[0:1, NBLK:NBLK + 1], min_val=1, max_val=NBLK // 2)
            with pool.Fori(0, NBLK // 2) as j:
                with pool.If(j < pairs):
                    for b, u, n in two(j):
                        pool.wait_ge(xgT_ps, b + 1)
                        gather(b + 2, u, 4 * j + 3 + u)
                    for b, u, n in two(j):
                        nc.gpsimd.tensor_copy(out_now[u][:, :], route_out[:, ds(b, 1)]).then_inc(idx_ready, 1)
                        pool.wait_ge(idx_ready, 4 * j + 5 + u)
                        pool.wait_ge(ye_rows, b + 3)
                        pool.sem_inc(pool_waited, 1)
                        nc.gpsimd.indirect_dma_start(out=ye_dram, out_offset=bass.IndirectOffsetOnAxis(ap=out_now[u][:, 0:1], axis=0),
                                                     in_=yo[u], in_offset=None, bounds_check=2 * NT * P - 1,
                                                     oob_is_err=False).then_inc(ye_out[u], 16)
                    for b, u, n in two(j):
                        pool.wait_ge(ye_out[u], 16 * n + 16)
                    pool.sem_inc(yo_free, 1)
            pool.sem_inc(experts_done, 1)

            def last(tiles):
                for t, u, n in tiles:
                    pool.wait_ge(var3_ready, t + 1)
                    inverse_root(rstd[u][:, :], moments[u][:, 1:2], LN_EPS).then_inc(rstd3_ready, 1)

            with pool.Fori(0, PT // 2) as j, step.loop(j, 2, PT // 2):
                last(two(j))
            last(LAST_TILE)


_INS = ['x_prompt', 'x_sample', 'cache_kv_latent', 'cache_k_rope', 'cache_conv', 'cache_mem_k', 'cache_mem_v',
        'mem_prompt', 'w_in', 'q_norm_g', 'kv_norm_g', 'w_uq', 'w_ukv', 'conv_w', 'w_out', 'ln1_g', 'ln1_b',
        'w_xq', 'w_xk', 'w_xv', 'w_xo', 'ln2_g', 'ln2_b', 'w_router_group', 'b_router_group',
        'w_router_expert', 'b_router_expert', 'w_exp_gate', 'w_exp_up', 'w_exp_down', 'ln3_g', 'ln3_b']
_OUTS = [('y_prompt', (1, 1024, 1024)), ('y_sample', (8, 16, 1024)), ('new_kv_latent_prompt', (1, 1, 1024, 128)),
         ('new_k_rope_prompt', (1, 1, 1024, 32)), ('new_conv_prompt', (1, 1, 2, 512)),
         ('new_mem_k_prompt', (1, 1, 256, 4, 256)), ('new_mem_v_prompt', (1, 1, 256, 4, 256)),
         ('new_kv_latent_sample', (1, 8, 16, 128)), ('new_k_rope_sample', (1, 8, 16, 32)),
         ('new_conv_sample', (1, 8, 2, 512))]


def kernel(**inputs):
    import numpy as _np
    import concourse.bacc as _bacc
    from concourse import mybir as _mybir
    from concourse.bass_utils import run_bass_kernel_spmd as _run

    nc = _bacc.Bacc("TRN2", target_bir_lowering=False, num_devices=1)
    arrays, ins, outs = {}, {}, {}
    for name in _INS:
        a = _np.ascontiguousarray(inputs[name])
        arrays[f"in_{name}"] = a
        ins[name] = nc.dram_tensor(f"in_{name}", a.shape, _mybir.dt.from_np(a.dtype), kind="ExternalInput").ap()
    arrays["in_tables"] = consts_table()
    ins["tables"] = nc.dram_tensor("in_tables", arrays["in_tables"].shape, _mybir.dt.float32, kind="ExternalInput").ap()
    for name, shape in _OUTS:
        outs[name] = nc.dram_tensor(f"out_{name}", shape, _mybir.dt.float32, kind="ExternalOutput").ap()
    encoder_layer_kernel(nc, ins, outs)
    r = _run(nc, [arrays], core_ids=[0])
    return tuple(r.results[0][f"out_{name}"] for name, _ in _OUTS)
```

```python
import concourse.bass as bass
from concourse import mybir
from contextlib import ExitStack, contextmanager


def consts_table():
    import numpy as np

    p = np.arange(128)
    ident = np.eye(128, dtype=np.float32)
    tri = (p[:, None] < p[None, :]).astype(np.float32)
    ones = np.ones((128, 128), np.float32)
    half = 16
    inv = (np.float32(10000.0) ** (-np.arange(half, dtype=np.float32) / np.float32(half))).astype(np.float32)
    rope = np.zeros((128, 9, 64), np.float32)
    for t in range(9):
        pos = (t * 128 + p if t < 8 else 512 + p % 16).astype(np.float32)
        ang = pos[:, None] * inv[None, :]
        c, s = np.cos(ang).astype(np.float32), np.sin(ang).astype(np.float32)
        rope[:, t] = np.concatenate([c, c, -s, s], 1)
    iota = np.broadcast_to(p.astype(np.float32), (128, 128))
    slot = 2 * (128 * np.arange(9)[None, :, None] + p[:, None, None]) + np.arange(2)[None, None, :] + 1
    return np.ascontiguousarray(np.concatenate(
        [ident, tri, ones, rope.reshape(128, -1), iota, slot.reshape(128, -1).astype(np.float32)], 1), np.float32)


class Count:

    def __init__(self, name):
        self.name, self.fixed, self.local, self.turn = name, 0, 0, None

    def next(self, by=1):
        self.local += by
        return by

    def value(self):
        own = self.fixed + self.local
        return own if self.turn is None else own + self.turn[0] * self.turn[1]

    @contextmanager
    def loop(self, j, per, turns):
        self.fixed, self.local, self.turn = self.fixed + self.local, 0, (j, per)
        yield
        assert self.local == per, (self.name, self.local, per)
        self.fixed, self.local, self.turn = self.fixed + turns * per, 0, None


def encoder_layer_kernel(nc, A, O):
    f32, f32r, i32, u32 = mybir.dt.float32, mybir.dt.float32r, mybir.dt.int32, mybir.dt.uint32
    ALU, ACT, AX = mybir.AluOpType, mybir.ActivationFunctionType, mybir.AxisListType
    ds = bass.ds

    P, D, NT, PT = 128, 1024, 9, 8
    NB, ROWS, PAST = 8, 16, 512
    H, DN, DR, DV = 8, 64, 32, 64
    HW = DN + DR
    QL, KL, CW = 256, 128, 512
    INW = QL + KL + DR + 3 * CW
    XH, XD, MEM = 4, 256, 256
    NG, EG, NE, FE = 4, 8, 32, 512
    NBLK = 50
    KT = D // P
    ALPHA = 2.0 ** 0.25
    MLA_SCALE, X_SCALE = float(HW) ** -0.5, float(XD) ** -0.5
    ORDER = (3, 4, 5, 6, 7, 2, 1, 0)
    NORMS = 2 * NT
    LN_EPS, RMS_EPS = 1e-5, 1e-6
    FAR = -1e30

    x_p = A["x_prompt"].rearrange("b s d -> (b s) d")
    x_s = A["x_sample"].rearrange("b s d -> (b s) d")
    y_p = O["y_prompt"].rearrange("b s d -> (b s) d")
    y_s = O["y_sample"].rearrange("b s d -> (b s) d")
    lat_p = O["new_kv_latent_prompt"].rearrange("l b s d -> (l b s) d")
    lat_s = O["new_kv_latent_sample"].rearrange("l b s d -> (l b s) d")
    kr_p = O["new_k_rope_prompt"].rearrange("l b s d -> (l b s) d")
    kr_s = O["new_k_rope_sample"].rearrange("l b s d -> (l b s) d")
    conv_p = O["new_conv_prompt"].rearrange("l b s d -> (l b s) d")
    conv_s = O["new_conv_sample"].rearrange("l b s d -> (l b) s d")
    mem_k_out = O["new_mem_k_prompt"].rearrange("l b (c p) h d -> p (l b c) (h d)", p=P)
    mem_v_out = O["new_mem_v_prompt"].rearrange("l b (c p) h d -> p (l b c) (h d)", p=P)
    mem_rows = A["mem_prompt"].rearrange("b (c p) d -> p (b c) d", p=P)
    cache_lat = A["cache_kv_latent"].rearrange("l b (c p) d -> (l b) p c d", p=P)
    cache_kr = A["cache_k_rope"].rearrange("l b (c p) d -> (l b) p c d", p=P)
    cache_conv = A["cache_conv"].rearrange("l b s d -> (l b) s d")
    cache_mk = A["cache_mem_k"].rearrange("l b (c p) h d -> (l b) p c (h d)", p=P)
    cache_mv = A["cache_mem_v"].rearrange("l b (c p) h d -> (l b) p c (h d)", p=P)

    def by_rows(name):
        return A[name].rearrange("l (k p) n -> p (l k) n", p=P)

    w_in_rows = by_rows("w_in")
    w_gate = A["w_exp_gate"].rearrange("l e (k p) n -> (l e) p k n", p=P)
    w_up = A["w_exp_up"].rearrange("l e (k p) n -> (l e) p k n", p=P)
    w_down = A["w_exp_down"].rearrange("l e (k p) n -> (l e) p k n", p=P)

    q_dram = nc.dram_tensor("q_rows", [NT * P, H * HW], f32).ap()
    u_dram = nc.dram_tensor("u_rows_prompt", [PT * P + 2, CW], f32).ap()
    us_dram = nc.dram_tensor("u_rows_sample", [NB, ROWS + 2, CW], f32).ap()
    gb_dram = nc.dram_tensor("gate_rows", [NT * P, CW], f32).ap()
    x2_dram = nc.dram_tensor("x2_rows", [NT * P, D], f32).ap()
    ye_dram = nc.dram_tensor("expert_rows", [2 * NT * P, D], f32).ap()
    ye_pairs = ye_dram.rearrange("(r k) d -> r k d", k=2)

    ctx = ExitStack()
    with ctx:
        def sb(name, shape, dt=f32):
            return ctx.enter_context(nc.sbuf_tensor(name, shape, dt))[tuple(slice(None) for _ in shape)]

        def sem(name):
            return ctx.enter_context(nc.semaphore(name))

        tables = sb("tables", [P, 3 * P + NT * 64 + P + 2 * NT])
        ident, tri, ones = (tables[:, i * P:(i + 1) * P] for i in range(3))
        rope = tables[:, 3 * P:3 * P + NT * 64].rearrange("p (t c) -> p t c", t=NT)
        iota = tables[:, 3 * P + NT * 64:4 * P + NT * 64]
        slot_id = tables[:, 4 * P + NT * 64:].rearrange("p (t k) -> p t k", k=2)
        conv_w = sb("conv_w_rows", [P, 3, CW])
        w_router = sb("w_router", [P, KT, NG + NE])
        b_router = sb("b_router", [P, NG + NE])
        logits = sb("logits", [P, NT, NG + NE])
        gates = sb("gates", [P, 2, NT])
        minus_half = sb("minus_half", [P, 2])
        minus_one = sb("minus_one", [P, 1])
        shift_by = [sb(f"shift_by{u}", [P, 1]) for u in (0, 1)]
        zero_row = sb("zero_row", [2, CW])
        shift2 = sb("shift2", [P, D])
        sumsq = [sb(f"sumsq{u}", [P, 2]) for u in (0, 1)]
        rrms = [sb(f"rrms{u}", [P, 2]) for u in (0, 1)]
        negmax = [sb(f"negmax{u}", [P, 1]) for u in (0, 1)]
        rsum = [sb(f"rsum{u}", [P, 1]) for u in (0, 1)]
        rinv = [sb(f"rinv{u}", [P, 1]) for u in (0, 1)]
        stats = [sb(f"stats{u}", [P, 12]) for u in (0, 1)]
        moments = [sb(f"moments{u}", [P, 2]) for u in (0, 1)]
        rstd = [sb(f"rstd{u}", [P, 1]) for u in (0, 1)]
        xmax = [sb(f"xmax{u}", [P, XH]) for u in (0, 1)]
        xsum = [sb(f"xsum{u}", [P, XH]) for u in (0, 1)]
        route_tok = sb("route_tok", [P, NBLK + 2], u32)
        route_out = sb("route_out", [P, NBLK + 2], u32)
        tok_now = [sb(f"tok_now{u}", [P, 1], u32) for u in (0, 1)]
        out_now = [sb(f"out_now{u}", [P, 1], u32) for u in (0, 1)]
        plan = sb("plan", [1, NBLK + 2], i32)

        ARENA, ROUNDED = 47912, 30720
        with nc.sbuf_tensor("arena", [P, ARENA], f32) as whole:
            arena = whole[:, :]
        rounded = sb("rounded", [P, ROUNDED], f32r)
        beside = sb("beside", [P, ARENA - ROUNDED])

        def area(at, *dims):
            n = 1
            for d in dims:
                n *= d
            assert at + n <= ARENA, (at, dims)
            got, names = arena[:, at:at + n], "abc"[:len(dims)]
            if len(dims) == 1:
                return got
            return got.rearrange(f"p ({' '.join(names)}) -> p {' '.join(names)}",
                                 **{c: d for c, d in zip(names, dims)})

        def pair(at, *dims):
            n = 1
            for d in dims:
                n *= d
            return [area(at + u * n, *dims) for u in (0, 1)]

        WA, KEEP = 0, 3 * KT * D
        w_ukv = area(KEEP, H, DN + DV)
        latT = area(KEEP + 1024, NT * P)
        krTs = area(KEEP + 2176, P)
        memkT = area(KEEP + 2304, KT, MEM)
        memv = area(KEEP + 4352, 2, D)
        ATT = KEEP + 6400
        attn = area(ATT, PT, H * DV)
        VAL = ATT + 4096
        value = area(VAL, PT, H * DV)
        WORK = VAL + 4096
        mixTs = area(46336, 4, P)

        mem, memT, memk = area(VAL, 2, D), area(VAL + 2048, 2, KT, P), area(ATT + 2 * D, 2, D)
        w_xk, w_xv = area(WA, KT, D), area(WA + 8192, KT, D)
        w_in = [area(WA + 16384 + k * INW if k < 4 else WA + (k - 4) * INW, INW) for k in range(KT)]
        x_a, xT_a = pair(ATT, D), pair(ATT + 2 * D, KT, P)
        w_uq, sq_junk = area(VAL, 2, H * HW), area(VAL + 1536, QL)
        rot_q = [(area(o, H, DR), area(o + H * DR, H, DR)) for o in (VAL + 1792, WORK + 7040)]
        rot_k = [(area(o, 1, DR), area(o + DR, 1, DR)) for o in (VAL + 3776, VAL + 3840)]
        cqn, ckvn, krpad, cqT = pair(VAL + 2304, QL), pair(VAL + 2816, KL), pair(VAL + 3072, HW), pair(VAL + 3264, 2, P)
        kT = pair(WORK, D)
        gbs, gvs, us = pair(WORK + 2048, CW), pair(WORK + 3072, CW), pair(WORK + 4096, CW)
        qrow = pair(WORK + 5120, H * HW)
        q_gain, kv_gain = area(WORK + 6656, QL), area(WORK + 6912, KL)
        qh, wk = pair(WA + 16384, PT, HW), pair(WA + 17920, DN)
        qT, pr, prT = pair(WORK + 2048, D), pair(WORK + 4096, D), pair(WORK + 6144, PT, P)
        lat_b, kr_b = pair(WA + 16384, 4, KL), pair(WA + 17408, 4, HW)
        lat_new, q_s = area(WA + 18176, NB, KL), area(WA + 19200, H, HW)
        wukT, qabs, ctxT = area(VAL, H, P), area(VAL + 1024, H, P), area(VAL + 2048, H, P)
        qTs = area(VAL + 3072, H, P)
        latTb, krTb, p_b = pair(WORK, PAST + ROWS), pair(WORK + 1056, PAST + ROWS), pair(WORK + 2112, PAST + ROWS)
        pT_b = pair(WORK + 3168, 5, P)
        qa_b, qr_b, latn_b = pair(WORK + 4448, H, ROWS), pair(WORK + 4704, H, ROWS), pair(WORK + 4960, KL)
        w_out, w_xq, w_xo = area(WA, KT, D), area(WA + 8192, KT, D), area(WA + 16384, KT, D)
        xr, aT = [area(VAL + u * 4096, D) for u in (0, 1)], [area(VAL + u * 4096 + 1024, KT, P) for u in (0, 1)]
        mix, res = [area(VAL + u * 4096 + 2048, D) for u in (0, 1)], [area(VAL + u * 4096 + 3072, D) for u in (0, 1)]
        cv = area(VAL + 8192, 4, CW)
        conv_rows = pair(46848, CW)
        gain1, shift1, gain2 = area(KEEP, D), area(KEEP + D, D), area(VAL + 10240, D)
        mk_b, mv_b = [area(ATT, 2, D), area(VAL + 4096, 2, D)], [area(ATT + 2048, 2, D), area(VAL + 6144, 2, D)]
        mkT_b = memkT
        qx_b, px_b, pxT_b = area(VAL + 8192, KT, 32), area(VAL + 8448, MEM), area(VAL + 8704, 2, P)
        oxT = mix[0].rearrange("p (k c) -> p k c", k=KT)
        CH = 12
        w_raw = [beside[:, g * 4 * D:(g + 1) * 4 * D].rearrange("p (k n) -> p k n", k=4) for g in range(3)]

        def high(c):
            return rounded[:, c * 2 * D:c * 2 * D + D]

        def low(c):
            return rounded[:, c * 2 * D + D:(c + 1) * 2 * D]

        def halves(at, n):
            return [[rounded[:, at + (2 * u + s) * n:at + (2 * u + s + 1) * n] for s in (0, 1)] for u in (0, 1)]

        xT_parts, hidT_parts = halves(CH * 2 * D, D), halves(CH * 2 * D + 4 * D, FE)
        xg, yo = ([beside[:, at + u * D:at + (u + 1) * D] for u in (0, 1)] for at in (12 * D, 14 * D))
        hid = [conv_w[:, u, :] for u in (0, 1)]
        at = [WA]

        def route(*dims, dt=f32):
            got = area(at[0], *dims)
            size = 1
            for d in dims:
                size *= d
            at[0] += size
            return got if dt is f32 else got.bitcast(dt)

        r_best, r_first, r_v1, r_v2, r_d2, r_e2, r_sum, r_den, r_lim = (route(NT) for _ in range(9))
        r_s4, r_group, r_gd, r_eg = (route(NT, NG) for _ in range(4))
        r_le, r_s8, r_pick1, r_pick2 = (route(NT, EG) for _ in range(4))
        r_all, r_hot, picks = route(NT * NE), route(2, NT, NE), route(NT * NE)
        r_all = r_all.rearrange("p (t g e) -> p t g e", t=NT, g=NG)
        r_before, r_total, r_rank, r_cmp = route(NT + 1, NE), route(NT, NE), route(NT, NE), route(NE, NT)
        r_blocks, r_end, r_start = (route(NE) for _ in range(3))
        r_slot, r_int, r_int2 = route(NT, 2), route(2 * NT, dt=i32), route(2 * NT, dt=i32)
        r_blk, r_pos, r_plan, r_row, r_int3 = route(2 * NT), route(2 * NT), route(NBLK, NE), route(NBLK + 1), route(NBLK + 1, dt=i32)
        r_map, r_mapi, r_mapi2 = route(NBLK), route(NBLK, dt=i32), route(NBLK, dt=i32)
        sel_slot, sel_blk = (route(P), route(P)), (route(NBLK), route(NBLK))
        LAST = WA
        yk, xl, rl = pair(LAST, 2, D), pair(LAST + 4096, D), pair(LAST + 6144, D)
        gain3, shift3 = area(LAST + 8192, D), area(LAST + 9216, D)

        T = [ctx.enter_context(nc.psum_tensor(f"T{u}", [P, 1024], f32)) for u in (0, 1)]
        M = [ctx.enter_context(nc.psum_tensor(f"M{u}", [P, 1024], f32)) for u in (0, 1)]

        tables_in, consts_in, mem_in = sem("tables_in"), sem("consts_in"), sem("mem_in")
        wxk_in, wxv_in, win_lo_in, win_hi_in = sem("wxk_in"), sem("wxv_in"), sem("win_lo_in"), sem("win_hi_in")
        mem_ps, mem_act, mem_dve, mem_out = sem("mem_ps"), sem("mem_act"), sem("mem_dve"), sem("mem_out")
        dve_step, pool_step = sem("dve_step"), sem("pool_step")
        dve_waited, pool_waited = sem("dve_waited"), sem("pool_waited")
        pads_zero = sem("pads_zero")
        x_in = [sem(f"x_in{u}") for u in (0, 1)]
        xT_ps, xT_ready = sem("xT_ps"), sem("xT_ready")
        latent_ps, conv_ps = sem("latent_ps"), sem("conv_ps")
        sumsq_ready, rrms_ready, gb_ready, gv_ready = (sem(n) for n in ("sumsq_ready", "rrms_ready", "gb_ready", "gv_ready"))
        norm_done, u_ready, cT_ps, cqT_ready = (sem(n) for n in ("norm_done", "u_ready", "cT_ps", "cqT_ready"))
        latT_ready, q_ps, q_rows, q_turned = (sem(n) for n in ("latT_ready", "q_ps", "q_rows", "q_turned"))
        gb_out, lat_out, u_out, q_out = ([sem(f"{n}{u}") for u in (0, 1)] for n in ("gb_out", "lat_out", "u_out", "q_out"))
        edge_out = sem("edge_out")
        value_ps, value_ready = sem("value_ps"), sem("value_ready")
        head_in = [sem(f"head_in{u}") for u in (0, 1)]
        qT_ps, kT_ps, qT_ready, kT_ready = (sem(n) for n in ("qT_ps", "kT_ps", "qT_ready", "kT_ready"))
        s_ps, negmax_ready, exp_done, pT_ps, pT_ready, o_ps, o_done = (
            sem(n) for n in ("s_ps", "negmax_ready", "exp_done", "pT_ps", "pT_ready", "o_ps", "o_done"))
        sq_in, sq_ps, sq_ready, wukT_ready = (sem(n) for n in ("sq_in", "sq_ps", "sq_ready", "wukT_ready"))
        cache_in = [sem(f"cache_in{u}") for u in (0, 1)]
        bq_ready, latb_ps, latb_ready, sb_ps, sb_negmax, sb_exp, sb_p, pTb_ps, pTb_ready, ctx_ps, ctx_done = (
            sem(n) for n in ("bq_ready", "latb_ps", "latb_ready", "sb_ps", "sb_negmax", "sb_exp", "sb_p",
                             "pTb_ps", "pTb_ready", "ctx_ps", "ctx_done"))
        mixTs_ps, mixTs_ready = sem("mixTs_ps"), sem("mixTs_ready")
        woq_in, wxo_in, ln_in = sem("woq_in"), sem("wxo_in"), sem("ln_in")
        conv_in, conv_ready, attn_copied = sem("conv_in"), sem("conv_ready"), sem("attn_copied")
        xr_in = [sem(f"xr_in{u}") for u in (0, 1)]
        rowsT_ps, rowsT_ready, product_ps = sem("rowsT_ps"), sem("rowsT_ready"), sem("product_ps")
        var_ready, rstd_ready, x1_ready, xq_rows, xmax_ready, px_ready, ox_ready, x2_ready, logits_done = (
            sem(n) for n in ("var_ready", "rstd_ready", "x1_ready", "xq_rows", "xmax_ready", "px_ready", "ox_ready",
                             "x2_ready", "logits_done"))
        x2_out = [sem(f"x2_out{u}") for u in (0, 1)]
        mkv_in = [sem(f"mkv_in{u}") for u in (0, 1)]
        qx_ready, mkT_ps, mkT_lo, mkT_hi, sx_ps, sx_negmax, sx_exp, sx_p, sxT_ps, sxT_ready, sxo_ps, sxo_done = (
            sem(n) for n in ("qx_ready", "mkT_ps", "mkT_lo", "mkT_hi", "sx_ps", "sx_negmax", "sx_exp", "sx_p",
                             "sxT_ps", "sxT_ready", "sxo_ps", "sxo_done"))
        softmax_in, softmax_exp = sem("softmax_in"), sem("softmax_exp")
        picks_ready, rank_ps, sel_ready, map_ps, plan_ready = (
            sem(n) for n in ("picks_ready", "rank_ps", "sel_ready", "map_ps", "plan_ready"))
        raw_in = [sem(f"raw_in{g}") for g in range(3)]
        xg_in, ye_out = ([sem(f"{n}{u}") for u in (0, 1)] for n in ("xg_in", "ye_out"))
        gu_high, gu_low, gu_used, down_high, down_low, down_used = (
            sem(n) for n in ("gu_high", "gu_low", "gu_used", "down_high", "down_low", "down_used"))
        xgT_ps, xgT_high, xgT_low, silu_ready, hid_ready, hidT_ps, hidT_high, hidT_low, ye_rows = (
            sem(n) for n in ("xgT_ps", "xgT_high", "xgT_low", "silu_ready", "hid_ready", "hidT_ps", "hidT_high",
                             "hidT_low", "ye_rows"))
        yo_free, idx_ready, experts_done, ln3_in = sem("yo_free"), sem("idx_ready"), sem("experts_done"), sem("ln3_in")
        last_in = [sem(f"last_in{u}") for u in (0, 1)]
        y_ready = sem("y_ready")
        xl_scaled, normed3, gain3_done = sem("xl_scaled"), sem("normed3"), sem("gain3_done")
        y_out = [sem(f"y_out{u}") for u in (0, 1)]

        block = ctx.enter_context(nc.Block())

        def tokens(p, s, t):
            return s if isinstance(t, int) and t == PT else p[ds(t * P, P), :]

        def two(j):
            return [(2 * j, 0, j), (2 * j + 1, 1, j)]

        LAST_TILE = [(PT, 0, PT // 2)]
        GB, GC, GV = QL + KL + DR, QL + KL + DR + CW, QL + KL + DR + 2 * CW

        @block.sync
        def _(sp):
            for u in (0, 1):
                sp.sem_inc(gb_out[u], 16)
                sp.sem_inc(lat_out[u], 32)
                sp.sem_inc(u_out[u], 16)
                sp.sem_inc(q_out[u], 16)
                sp.sem_inc(x2_out[u], 16)
                sp.sem_inc(y_out[u], 16)
            sp.dma_start(tables, A["tables"]).then_inc(tables_in, 16)
            sp.dma_start(mem, mem_rows).then_inc(mem_in, 16)
            sp.dma_start(w_xk, by_rows("w_xk")).then_inc(wxk_in, 16)
            sp.dma_start(w_xv, by_rows("w_xv")).then_inc(wxv_in, 16)
            for u in (0, 1):
                sp.dma_start(x_a[u], x_p[u * P:(u + 1) * P, :]).then_inc(x_in[u], 16)
            for k in range(4):
                sp.dma_start(w_in[k], w_in_rows[:, k, :]).then_inc(win_lo_in, 16)
            for dst, src in ((q_gain, A["q_norm_g"]), (kv_gain, A["kv_norm_g"]), (b_router[:, 0:NG], A["b_router_group"]),
                             (b_router[:, NG:], A["b_router_expert"].rearrange("l g e -> l (g e)")),
                             (shift2, A["ln2_b"])):
                sp.dma_start(dst, src.to_broadcast([P, dst.shape[1]])).then_inc(consts_in, 16)
            for k in range(3):
                sp.dma_start(conv_w[:, k, :], A["conv_w"][0, k:k + 1, :].to_broadcast([P, CW])).then_inc(consts_in, 16)
            sp.dma_start(w_router[:, :, 0:NG], by_rows("w_router_group")).then_inc(consts_in, 16)
            sp.dma_start(w_router[:, :, NG:], by_rows("w_router_expert")).then_inc(consts_in, 16)
            sp.dma_start(w_ukv, A["w_ukv"].rearrange("l p (h c) -> p (l h) c", h=H)).then_inc(win_hi_in, 16)
            sp.wait_ge(mem_ps, 2)
            sp.dma_start(w_uq, by_rows("w_uq")).then_inc(win_hi_in, 16)
            sp.wait_ge(mem_ps, 4)
            for k in range(4, KT):
                sp.dma_start(w_in[k], w_in_rows[:, k, :]).then_inc(win_hi_in, 16)
            sp.wait_ge(mem_dve, 2)
            sp.dma_start(mem_k_out, memk).then_inc(mem_out, 16)
            sp.wait_ge(mem_act, 4)
            sp.dma_start(mem_v_out, memv).then_inc(mem_out, 16)
            sp.wait_ge(pads_zero, 1)
            sp.dma_start(u_dram[0:2, :], zero_row).then_inc(edge_out, 16)
            sp.dma_start(us_dram[:, 0:2, :], cache_conv).then_inc(edge_out, 16)

            def store_rows(tiles):
                for t, u, n in tiles:
                    sp.wait_ge(gb_ready, t + 1)
                    sp.dma_start(gb_dram[ds(t * P, P), :], gbs[u]).then_inc(gb_out[u], 16)
                for t, u, n in tiles:
                    sp.wait_ge(norm_done, t + 1)
                    sp.dma_start(tokens(lat_p, lat_s, t), ckvn[u]).then_inc(lat_out[u], 16)
                    sp.dma_start(tokens(kr_p, kr_s, t), krpad[u][:, DN:]).then_inc(lat_out[u], 16)
                for t, u, n in tiles:
                    sp.wait_ge(u_ready, t + 1)
                    if isinstance(t, int) and t == PT:
                        for b in range(NB):
                            sp.dma_start(us_dram[b, 2:, :], us[u][b * ROWS:(b + 1) * ROWS, :]).then_inc(edge_out, 16)
                        sp.sem_inc(u_out[u], 16)
                    else:
                        sp.dma_start(u_dram[ds(t * P + 2, P), :], us[u]).then_inc(u_out[u], 16)
                for t, u, n in tiles:
                    sp.wait_ge(q_turned, t + 1)
                    sp.dma_start(q_dram[ds(t * P, P), :], qrow[u]).then_inc(q_out[u], 16)

            with sp.Fori(0, 3) as j:
                for t, u, n in two(j):
                    sp.wait_ge(xT_ps, t + 1)
                    sp.dma_start(x_a[u], x_p[ds((t + 2) * P, P), :]).then_inc(x_in[u], 16)
                store_rows(two(j))
            sp.wait_ge(xT_ps, 7)
            sp.dma_start(x_a[0], x_s).then_inc(x_in[0], 16)
            store_rows(two(3))
            store_rows(LAST_TILE)

            for u, uses in ((0, 5), (1, 4)):
                sp.wait_ge(q_out[u], 16 + 16 * uses)
                sp.wait_ge(lat_out[u], 32 + 32 * uses)
                sp.wait_ge(u_out[u], 16 + 16 * uses)
                sp.wait_ge(gb_out[u], 16 + 16 * uses)
            sp.wait_ge(conv_ps, NT)
            q_heads = q_dram[0:PT * P, :].rearrange("(i p) c -> p i c", p=P)
            w_ukv_cols = A["w_ukv"].rearrange("l p c -> (l p) c")

            def load_head(h, u):
                sp.dma_start(qh[u], q_heads[:, :, ds(h * HW, HW)]).then_inc(head_in[u], 16)
                sp.dma_start(wk[u], w_ukv_cols[:, ds(h * (DN + DV), DN)]).then_inc(head_in[u], 16)

            load_head(0, 0)
            load_head(1, 1)
            sp.dma_start(w_out, by_rows("w_out")).then_inc(woq_in, 16)
            sp.dma_start(w_xq, by_rows("w_xq")).then_inc(woq_in, 16)
            sp.dma_start(q_s, q_dram[PT * P:, :].rearrange("p (h c) -> p h c", h=H)).then_inc(sq_in, 16)
            sp.dma_start(lat_new[0:ROWS, :, :], lat_s.rearrange("(b r) c -> r b c", r=ROWS)).then_inc(sq_in, 16)
            sp.wait_ge(edge_out, 16 * (2 + NB))
            sp.dma_start(conv_p, u_dram[PT * P:PT * P + 2, :]).then_inc(edge_out, 16)
            sp.dma_start(conv_s, us_dram[:, ROWS:, :]).then_inc(edge_out, 16)
            with sp.Fori(0, 3) as j:
                for h, u, n in two(j):
                    sp.wait_ge(kT_ps, h + 3)
                    load_head(h + 2, u)
            sp.wait_ge(kT_ps, 2 + H)

            with sp.Fori(0, NB // 2) as j:
                for b, u, n in two(j):
                    sp.wait_ge(ctx_ps, b + 1)
                    sp.dma_start(lat_b[u], cache_lat[ds(b, 1), :, :, :].rearrange("b p c d -> p (b c) d")).then_inc(cache_in[u], 16)
                    sp.dma_start(kr_b[u][:, :, DN:], cache_kr[ds(b, 1), :, :, :].rearrange("b p c d -> p (b c) d")).then_inc(cache_in[u], 16)

            sp.wait_ge(mixTs_ps, 1)

            def load_conv(t):
                if isinstance(t, int) and t == PT:
                    for k in range(3):
                        for b in range(NB):
                            sp.dma_start(cv[b * ROWS:(b + 1) * ROWS, k, :], us_dram[b, k:k + ROWS, :]).then_inc(conv_in, 16)
                else:
                    for k in range(3):
                        sp.dma_start(cv[:, k, :], u_dram[ds(t * P + k, P), :]).then_inc(conv_in, 16)
                sp.dma_start(cv[:, 3, :], gb_dram[ds(t * P, P), :]).then_inc(conv_in, 16)

            load_conv(0)
            for dst, name in ((gain1, "ln1_g"), (shift1, "ln1_b"), (gain2, "ln2_g")):
                sp.dma_start(dst, A[name].to_broadcast([P, D])).then_inc(ln_in, 16)
            sp.wait_ge(conv_ready, 1)
            load_conv(1)
            sp.dma_start(w_xo, by_rows("w_xo")).then_inc(wxo_in, 16)

            def load_x(tiles):
                for t, u, n in tiles:
                    sp.wait_ge(logits_done, t + 1)
                    sp.wait_ge(x2_out[u], 16 * n + 16)
                    sp.dma_start(xr[u], tokens(x_p, x_s, t)).then_inc(xr_in[u], 16)

            def store_x2(tiles):
                for t, u, n in tiles:
                    sp.wait_ge(x2_ready, t + 1)
                    sp.dma_start(x2_dram[ds(t * P, P), :], xr[u]).then_inc(x2_out[u], 16)

            with sp.Fori(0, 3) as j:
                load_x(two(j))
                for t, u, n in two(j):
                    sp.wait_ge(conv_ready, t + 2)
                    load_conv(t + 2)
                store_x2(two(j))
            load_x(two(3))
            sp.wait_ge(conv_ready, PT)
            load_conv(PT)
            store_x2(two(3))
            load_x(LAST_TILE)

            sp.wait_ge(x2_out[1], 16 + 16 * 4)
            with sp.Fori(0, NB // 2) as j:
                for b, u, n in two(j):
                    sp.wait_ge(sxo_ps, b + 1)
                    if u == 0:
                        sp.wait_ge(attn_copied, PT)
                    else:
                        sp.wait_ge(logits_done, PT + 2)
                    sp.dma_start(mk_b[u], cache_mk[ds(b, 1), :, :, :].rearrange("b p c d -> p (b c) d")).then_inc(mkv_in[u], 16)
                    sp.dma_start(mv_b[u], cache_mv[ds(b, 1), :, :, :].rearrange("b p c d -> p (b c) d")).then_inc(mkv_in[u], 16)
            store_x2(LAST_TILE)

            sp.wait_ge(logits_done, NT + 2)
            sp.wait_ge(x2_out[0], 16 + 16 * 5)
            sp.wait_ge(plan_ready, 1)
            pairs = sp.value_load(plan[0:1, NBLK:NBLK + 1], min_val=1, max_val=NBLK // 2)
            pairs_less_1 = sp.value_load(plan[0:1, NBLK + 1:NBLK + 2], min_val=0, max_val=NBLK // 2 - 1)

            def load_gate_up(b, e):
                for g in (0, 1):
                    sp.wait_ge(gu_low, 8 * b + 4 * (g + 1))
                    for src, c in ((w_gate, 0), (w_up, FE)):
                        sp.dma_start(w_raw[g][:, :, c:c + FE],
                                     src[ds(e, 1), :, 4 * g:4 * g + 4, :].rearrange("e p k n -> p (e k) n")).then_inc(raw_in[g], 16)

            def load_down(b, e):
                sp.wait_ge(down_low, 4 * b + 4)
                sp.dma_start(w_raw[2], w_down[ds(e, 1), :, :, :].rearrange("e p k n -> p (e k) n")).then_inc(raw_in[2], 16)

            def expert(b):
                return sp.value_load(plan[0:1, ds(b, 1)], min_val=0, max_val=NE - 1)

            load_gate_up(0, expert(0))
            with sp.Fori(0, NBLK // 2) as j:
                with sp.If(j < pairs):
                    b0, b1 = 2 * j, 2 * j + 1
                    e1 = expert(b1)
                    load_gate_up(b1, e1)
                    load_down(b0, expert(b0))
                    with sp.If(j < pairs_less_1):
                        load_gate_up(b1 + 1, expert(b1 + 1))
                    load_down(b1, e1)

            sp.wait_ge(experts_done, 1)
            sp.dma_start(gain3, A["ln3_g"].to_broadcast([P, D])).then_inc(ln3_in, 16)
            sp.dma_start(shift3, A["ln3_b"].to_broadcast([P, D])).then_inc(ln3_in, 16)

            def load_last(tiles):
                for t, u, n in tiles:
                    if not (isinstance(t, int) and t < 2):
                        sp.wait_ge(var_ready, NORMS + t - 1)
                    sp.dma_start(yk[u], ye_pairs[ds(t * P, P), :, :]).then_inc(last_in[u], 16)
                    sp.dma_start(xl[u], x2_dram[ds(t * P, P), :]).then_inc(last_in[u], 16)

            def store_y(tiles):
                for t, u, n in tiles:
                    sp.wait_ge(y_ready, t + 1)
                    sp.dma_start(tokens(y_p, y_s, t), rl[u]).then_inc(y_out[u], 16)

            load_last(two(0))
            with sp.Fori(0, PT // 2 - 1) as j:
                load_last(two(j + 1))
                store_y(two(j))
            load_last(LAST_TILE)
            store_y(two(PT // 2 - 1))
            store_y(LAST_TILE)
            sp.wait_ge(y_out[0], 16 + 16 * 5)
            sp.wait_ge(y_out[1], 16 + 16 * 4)
            sp.wait_ge(mem_out, 32)
            sp.wait_ge(edge_out, 16 * (4 + NB))
            sp.wait_ge(lat_out[0], 32 + 32 * 5)
            sp.wait_ge(lat_out[1], 32 + 32 * 4)
            sp.wait_ge(x2_out[0], 16 + 16 * 5)

        @block.tensor
        def _(pe):
            for two_ahead in (kT_ps, ctx_ps, sxo_ps):
                pe.sem_inc(two_ahead, 2)
            pe.sem_inc(gu_used, 8)
            pe.sem_inc(down_used, 4)

            def transposes(out, rows, n, width=P):
                for k in range(n):
                    got = nc.tensor.transpose(out[:, k * P:(k + 1) * P] if width == P else out[0:width, k * P:(k + 1) * P],
                                              rows[:, k * width:(k + 1) * width], ident)
                return got

            def product(out, lhsT, w, cols):
                for half, (c0, c1) in enumerate(cols):
                    for k in range(KT):
                        w_k = w[k] if isinstance(w, list) else w[:, k, :]
                        got = nc.tensor.matmul(out[:, half * 512:half * 512 + c1 - c0], lhsT[:, k, :], w_k[:, c0:c1],
                                               start=(k == 0), stop=(k == KT - 1))
                return got

            BOTH = [(0, 512), (512, 1024)]
            pe.wait_ge(tables_in, 16)
            pe.wait_ge(mem_in, 16)
            for c in (0, 1):
                transposes(T[c], mem[:, c, :], KT).then_inc(mem_ps, 1)
            pe.wait_ge(wxk_in, 16)
            for c in (0, 1):
                pe.wait_ge(mem_act, c + 1)
                product(M[c], memT[:, c, :, :], w_xk, BOTH).then_inc(mem_ps, 1)
            pe.wait_ge(wxv_in, 16)
            for c in (0, 1):
                product(T[c], memT[:, c, :, :], w_xv, BOTH).then_inc(mem_ps, 1)
            for c in (0, 1):
                pe.wait_ge(mem_dve, c + 1)
                transposes(M[c], memk[:, c, :], KT).then_inc(mem_ps, 1)
            pe.wait_ge(mem_act, 4)
            pe.wait_ge(mem_dve, 4)
            pe.wait_ge(win_lo_in, 64)
            pe.wait_ge(win_hi_in, 96)
            pe.wait_ge(pads_zero, 1)

            def project(tiles):
                for t, u, n in tiles:
                    pe.wait_ge(x_in[u], 16 * n + 16)
                    pe.wait_ge(q_rows, t + 1)
                    transposes(T[u], x_a[u], KT).then_inc(xT_ps, 1)
                for t, u, n in tiles:
                    pe.wait_ge(xT_ready, t + 1)
                    product(M[u], xT_a[u], w_in, [(0, GB), (GB, GC)]).then_inc(latent_ps, 1)
                for t, u, n in tiles:
                    product(T[u], xT_a[u], w_in, [(GC, GV), (GV, INW)]).then_inc(conv_ps, 1)
                for t, u, n in tiles:
                    pe.wait_ge(norm_done, t + 1)
                    transposes(M[u], cqn[u], 2)
                    nc.tensor.transpose(M[u][:, 2 * P:3 * P], ckvn[u], ident)
                    nc.tensor.transpose(M[u][0:HW, 3 * P:4 * P], krpad[u], ident).then_inc(cT_ps, 1)
                for t, u, n in tiles:
                    pe.wait_ge(cqT_ready, t + 1)
                    pe.wait_ge(u_ready, t + 1)
                    for dst, c in ((M[u][:, 512:896], 0), (T[u][:, 0:384], 384)):
                        for k in (0, 1):
                            got = nc.tensor.matmul(dst, cqT[u][:, k, :], w_uq[:, k, c:c + 384], start=(k == 0), stop=(k == 1))
                    got.then_inc(q_ps, 1)

            with pe.Fori(0, PT // 2) as j:
                project(two(j))
            project(LAST_TILE)

            pe.wait_ge(latT_ready, NT)
            pe.wait_ge(q_rows, 2 + NT)
            for c, dst in enumerate((T[0], T[1], M[0], M[1])):
                for i in (0, 1):
                    got = nc.tensor.matmul(dst[:, i * 512:(i + 1) * 512], latT[:, (2 * c + i) * P:(2 * c + i + 1) * P],
                                           w_ukv[:, :, DN:], start=True, stop=True)
                got.then_inc(value_ps, 1)
            pe.wait_ge(value_ready, 4)
            with pe.Fori(0, H // 2) as j:
                for h, u, n in two(j):
                    pe.wait_ge(head_in[u], 32 * n + 32)
                    pe.wait_ge(pT_ready, PT * h + 1)
                    for i in range(PT):
                        got = nc.tensor.transpose(M[0][0:HW, i * P:(i + 1) * P], qh[u][:, i, :], ident)
                    got.then_inc(qT_ps, 1)
                    pe.wait_ge(o_done, PT * h + 2)
                    for c in (0, 1):
                        got = nc.tensor.matmul(M[1][0:DN, c * 512:(c + 1) * 512], wk[u], latT[:, c * 512:(c + 1) * 512],
                                               start=True, stop=True)
                    got.then_inc(kT_ps, 1)
                    pe.wait_ge(qT_ready, h + 1)
                    pe.wait_ge(kT_ready, h + 1)

                    def scores(n):
                        i = ORDER[n]
                        pe.wait_ge(exp_done, PT * h + n + 1)
                        for c in range(0, (i + 1) * P, 512):
                            c1 = min(c + 512, (i + 1) * P)
                            got = nc.tensor.matmul(T[n % 2][:, c:c1], qT[u][0:HW, i * P:(i + 1) * P], kT[u][0:HW, c:c1],
                                                   start=True, stop=True)
                        got.then_inc(s_ps, 1)

                    def weigh_values(n):
                        i = ORDER[n]
                        pe.wait_ge(pT_ready, PT * h + n + 2)
                        pe.wait_ge(o_done, PT * h + n + 1)
                        o = M[1][:, (n % 2) * 512:(n % 2) * 512 + DV]
                        for c in range(i + 1):
                            got = nc.tensor.matmul(o, prT[n % 2][:, c, :], value[:, c, ds(h * DV, DV)], start=(c == 0), stop=(c == i))
                        got.then_inc(o_ps, 1)

                    scores(0)
                    scores(1)
                    for n in range(PT):
                        pe.wait_ge(exp_done, PT * h + n + 3)
                        pe.wait_ge(pT_ready, PT * h + n + 1)
                        transposes(M[0], pr[n % 2], ORDER[n] + 1).then_inc(pT_ps, 1)
                        if n + 2 < PT:
                            scores(n + 2)
                        if n > 0:
                            weigh_values(n - 1)
                    weigh_values(PT - 1)

            pe.wait_ge(sq_in, 32)
            pe.wait_ge(pT_ready, PT * H + 1)
            for h in range(H):
                got = nc.tensor.transpose(M[0][0:HW, h * P:(h + 1) * P], q_s[:, h, :], ident)
            got.then_inc(sq_ps, 1)
            for h in range(H):
                got = nc.tensor.transpose(T[0][0:DN, h * P:(h + 1) * P], w_ukv[:, h, 0:DN], ident)
            got.then_inc(sq_ps, 1)
            pe.wait_ge(sq_ready, 1)
            pe.wait_ge(wukT_ready, 1)
            pe.wait_ge(o_done, 2 + PT * H)
            for h in range(H):
                got = nc.tensor.matmul(M[1][:, h * P:(h + 1) * P], wukT[0:DN, h, :], qTs[0:DN, h, :], start=True, stop=True)
            got.then_inc(sq_ps, 1)
            pe.wait_ge(sq_ready, 2)
            pe.wait_ge(pads_zero, 2)
            N_KEYS = PAST + ROWS
            with pe.Fori(0, NB // 2) as j:
                for b, u, n in two(j):
                    pe.wait_ge(cache_in[u], 32 * n + 32)
                    for c in range(4):
                        nc.tensor.transpose(T[u][:, c * P:(c + 1) * P], lat_b[u][:, c, :], ident)
                    for c in range(4):
                        got = nc.tensor.transpose(T[u][0:HW, 512 + c * P:512 + (c + 1) * P], kr_b[u][:, c, :], ident)
                    got.then_inc(latb_ps, 1)
                for b, u, n in two(j):
                    pe.wait_ge(latb_ready, b + 1)
                    pe.wait_ge(bq_ready, b + 1)
                    pe.wait_ge(ctx_done, b + 1)
                    for c0, c1 in ((0, 512), (512, N_KEYS)):
                        nc.tensor.matmul(M[u][:, c0:c1], qa_b[u].rearrange("p h r -> p (h r)"), latTb[u][:, c0:c1], start=True, stop=False)
                        got = nc.tensor.matmul(M[u][:, c0:c1], qr_b[u][0:HW].rearrange("p h r -> p (h r)"), krTb[u][0:HW, c0:c1],
                                               start=False, stop=True)
                    got.then_inc(sb_ps, 1)
                for b, u, n in two(j):
                    pe.wait_ge(sb_p, b + 1)
                    transposes(T[u], p_b[u], 4)
                    nc.tensor.transpose(T[u][0:ROWS, 512:512 + P], p_b[u][:, PAST:], ident).then_inc(pTb_ps, 1)
                for b, u, n in two(j):
                    pe.wait_ge(pTb_ready, b + 1)
                    for c in range(4):
                        nc.tensor.matmul(M[u][:, 0:P], lat_b[u][:, c, :], pT_b[u][:, c, :], start=(c == 0), stop=False)
                    nc.tensor.matmul(M[u][:, 0:P], latn_b[u][0:ROWS, :], pT_b[u][0:ROWS, 4, :], start=False, stop=True).then_inc(ctx_ps, 1)
            pe.wait_ge(ctx_done, 2 + NB)
            for h in range(H):
                r = (h % 2) * DV
                got = nc.tensor.matmul(T[0][r:r + DV, (h // 2) * P:(h // 2 + 1) * P], w_ukv[:, h, DN:], ctxT[:, h, :],
                                       start=True, stop=True)
            got.then_inc(mixTs_ps, 1)

            pe.wait_ge(mixTs_ready, 1)
            pe.wait_ge(woq_in, 32)
            with pe.Fori(0, PT // 2) as j:
                def event(stage, u):
                    return 12 * j + 2 * stage + u + 1

                for t, u, n in two(j):
                    pe.wait_ge(attn_copied, t + 1)
                    pe.wait_ge(conv_ready, t + 1)
                    pe.wait_ge(logits_done, t + 1)
                    transposes(T[u], mix[u], 4)
                    transposes(T[u][:, 512:], conv_rows[u], 4).then_inc(rowsT_ps, 1)
                for t, u, n in two(j):
                    pe.wait_ge(rowsT_ready, event(0, u))
                    product(M[u], aT[u], w_out, BOTH).then_inc(product_ps, 1)
                for t, u, n in two(j):
                    pe.wait_ge(x1_ready, t + 1)
                    transposes(T[u], xr[u], KT).then_inc(rowsT_ps, 1)
                for t, u, n in two(j):
                    pe.wait_ge(rowsT_ready, event(1, u))
                    product(M[u], aT[u], w_xq, BOTH).then_inc(product_ps, 1)
                for t, u, n in two(j):
                    pe.wait_ge(xq_rows, t + 1)
                    transposes(T[u], res[u], KT).then_inc(rowsT_ps, 1)
                for t, u, n in two(j):
                    pe.wait_ge(rowsT_ready, event(2, u))
                    for h in range(XH):
                        for c in (0, 1):
                            got = nc.tensor.matmul(M[u][:, h * MEM:(h + 1) * MEM], aT[u][:, 2 * h + c, :], memkT[:, 2 * h + c, :],
                                                   start=(c == 0), stop=(c == 1))
                    got.then_inc(product_ps, 1)
                for t, u, n in two(j):
                    pe.wait_ge(px_ready, t + 1)
                    transposes(T[u], mix[u], KT).then_inc(rowsT_ps, 1)
                for t, u, n in two(j):
                    pe.wait_ge(rowsT_ready, event(3, u))
                    for h in range(XH):
                        for c in (0, 1):
                            got = nc.tensor.matmul(M[u][:, h * XD:(h + 1) * XD], aT[u][:, 2 * h + c, :], memv[:, c, h * XD:(h + 1) * XD],
                                                   start=(c == 0), stop=(c == 1))
                    got.then_inc(product_ps, 1)
                for t, u, n in two(j):
                    pe.wait_ge(ox_ready, t + 1)
                    transposes(T[u], res[u], KT).then_inc(rowsT_ps, 1)
                pe.wait_ge(wxo_in, 16)
                for t, u, n in two(j):
                    pe.wait_ge(rowsT_ready, event(4, u))
                    product(M[u], aT[u], w_xo, BOTH).then_inc(product_ps, 1)
                for t, u, n in two(j):
                    pe.wait_ge(x2_ready, t + 1)
                    transposes(T[u], xr[u], KT).then_inc(rowsT_ps, 1)
                for t, u, n in two(j):
                    pe.wait_ge(rowsT_ready, event(5, u))
                    for k in range(KT):
                        got = nc.tensor.matmul(M[u][:, 0:NG + NE], aT[u][:, k, :], w_router[:, k, :], start=(k == 0), stop=(k == KT - 1))
                    got.then_inc(product_ps, 1)

            E0 = 6 * PT
            pe.wait_ge(conv_ready, NT)
            pe.wait_ge(logits_done, NT)
            transposes(T[0][:, 512:], conv_rows[0], 4).then_inc(rowsT_ps, 1)
            pe.wait_ge(rowsT_ready, E0 + 1)
            product(M[0], aT[0], w_out, BOTH).then_inc(product_ps, 1)
            pe.wait_ge(x1_ready, NT)
            transposes(T[0], xr[0], KT).then_inc(rowsT_ps, 1)
            pe.wait_ge(rowsT_ready, E0 + 2)
            product(M[0], aT[0], w_xq, BOTH).then_inc(product_ps, 1)
            pe.wait_ge(xq_rows, NT)
            transposes(T[0], res[0], KT).then_inc(rowsT_ps, 1)
            pe.wait_ge(rowsT_ready, E0 + 3)

            def turn_memory(u, n):
                pe.wait_ge(mkv_in[u], 32 * n + 32)
                for c in (0, 1):
                    got = transposes(T[c], mk_b[u][:, c, :], KT)
                got.then_inc(mkT_ps, 1)

            def attend_memory(b, u, n, last):
                pe.wait_ge(mkT_lo, b + 1)
                pe.wait_ge(mkT_hi, b + 1)
                pe.wait_ge(qx_ready, b + 1)
                for h in range(XH):
                    for c in (0, 1):
                        got = nc.tensor.matmul(M[0][h * 32:(h + 1) * 32, 0:MEM], qx_b[:, 2 * h + c, :], mkT_b[:, 2 * h + c, :],
                                               start=(c == 0), stop=(c == 1))
                got.then_inc(sx_ps, 1)
                if not last:
                    turn_memory(1 - u, n + u)
                pe.wait_ge(sx_p, b + 1)
                transposes(M[0][:, 512:], px_b, 2).then_inc(sxT_ps, 1)
                pe.wait_ge(sxT_ready, b + 1)
                pe.wait_ge(sxo_done, b + 1)
                for h in range(XH):
                    for d in (0, 1):
                        for c in (0, 1):
                            got = nc.tensor.matmul(M[1][:, (2 * h + d) * ROWS:(2 * h + d + 1) * ROWS],
                                                   mv_b[u][:, c, h * XD + d * P:h * XD + (d + 1) * P],
                                                   pxT_b[:, c, h * 32:h * 32 + ROWS], start=(c == 0), stop=(c == 1))
                got.then_inc(sxo_ps, 1)

            turn_memory(0, 0)
            with pe.Fori(0, NB // 2 - 1) as j:
                for b, u, n in two(j):
                    attend_memory(b, u, n, False)
            for b, u, n in two(NB // 2 - 1):
                attend_memory(b, u, n, b == NB - 1)
            pe.wait_ge(sxo_done, NB + 1)
            product(M[0], oxT, w_xo, BOTH).then_inc(product_ps, 1)
            pe.wait_ge(x2_ready, NT)
            transposes(T[0], xr[0], KT).then_inc(rowsT_ps, 1)
            pe.wait_ge(rowsT_ready, E0 + 4)
            for k in range(KT):
                got = nc.tensor.matmul(M[0][:, 0:NG + NE], aT[0][:, k, :], w_router[:, k, :], start=(k == 0), stop=(k == KT - 1))
            got.then_inc(product_ps, 1)

            pe.wait_ge(picks_ready, 1)
            nc.tensor.matmul(T[0][:, 0:NT * NE], tri, picks, start=True, stop=True)
            nc.tensor.matmul(T[0][:, 512:512 + NT * NE], ones, picks, start=True, stop=True).then_inc(rank_ps, 1)
            for i in range(2 * NT):
                pe.wait_ge(sel_ready, i + 1)
                nc.tensor.matmul(M[1][:, 0:NBLK], sel_slot[i % 2], sel_blk[i % 2], start=(i == 0), stop=(i == 2 * NT - 1)).then_inc(map_ps, 1)

            def split_product(out, x, w, c, first, last):
                for n, (xs, ws) in enumerate(((0, 0), (0, 1), (1, 0))):
                    got = nc.tensor.matmul(out, x[xs], (high, low)[ws](w)[:, c:c + 512], start=(first and n == 0), stop=(last and n == 2))
                return got

            def gate_up(b, u):
                pe.wait_ge(xgT_high, b + 1)
                pe.wait_ge(xgT_low, b + 1)
                pe.wait_ge(hid_ready, b + 1)
                for k in range(KT):
                    pe.wait_ge(gu_low, 8 * b + 8 + k + 1)
                    x = [xT_parts[u][s][:, k * P:(k + 1) * P] for s in (0, 1)]
                    for c in (0, FE):
                        got = split_product(M[0][:, c:c + 512], x, k, c, k == 0, k == KT - 1)
                    got.then_inc(gu_used, 1)

            def down(b, u):
                pe.wait_ge(hidT_high, b + 1)
                pe.wait_ge(hidT_low, b + 1)
                pe.wait_ge(ye_rows, b + 1)
                for k in range(4):
                    pe.wait_ge(down_low, 4 * b + 4 + k + 1)
                    x = [hidT_parts[u][s][:, k * P:(k + 1) * P] for s in (0, 1)]
                    for c in (0, 512):
                        got = split_product(M[1][:, c:c + 512], x, 8 + k, c, k == 0, k == 3)
                    got.then_inc(down_used, 1)

            def turn_rows(b, u, uses):
                pe.wait_ge(xg_in[u], 16 * uses + 16)
                if not (isinstance(b, int) and b == 0):
                    pe.wait_ge(xgT_low, b)
                    pe.wait_ge(xgT_high, b)
                transposes(T[0], xg[u], KT).then_inc(xgT_ps, 1)

            def turn_hidden(b, u):
                pe.wait_ge(hid_ready, b + 2)
                if u == 1:
                    pe.wait_ge(hidT_low, b)
                transposes(T[1], hid[u], 4).then_inc(hidT_ps, 1)

            pe.wait_ge(plan_ready, 1)
            pairs = pe.value_load(plan[0:1, NBLK:NBLK + 1], min_val=1, max_val=NBLK // 2)
            turn_rows(0, 0, 0)
            with pe.Fori(0, NBLK // 2) as j:
                with pe.If(j < pairs):
                    b0, b1 = 2 * j, 2 * j + 1
                    gate_up(b0, 0)
                    turn_rows(b1, 1, j)
                    turn_hidden(b0, 0)
                    gate_up(b1, 1)
                    down(b0, 0)
                    turn_hidden(b1, 1)
                    turn_rows(b1 + 1, 0, j + 1)
                    down(b1, 1)

        @block.scalar
        def _(act):
            act.sem_inc(q_rows, 2)
            act.sem_inc(exp_done, 2)
            act.sem_inc(sxo_done, 1)
            act.sem_inc(ye_rows, 1)
            for c in (0, 1):
                act.wait_ge(mem_ps, c + 1)
                nc.scalar.copy(memT[:, c, :, :].rearrange("p k c -> p (k c)"), T[c][:, :]).then_inc(mem_act, 1)
            for c in (0, 1):
                act.wait_ge(mem_ps, 4 + c + 1)
                nc.scalar.copy(memv[:, c, :], T[c][:, :]).then_inc(mem_act, 1)
            act.wait_ge(mem_out, 32)

            def project(tiles):
                for t, u, n in tiles:
                    act.wait_ge(xT_ps, t + 1)
                    nc.scalar.copy(xT_a[u].rearrange("p k c -> p (k c)"), T[u][:, :]).then_inc(xT_ready, 1)
                for t, u, n in tiles:
                    act.wait_ge(latent_ps, t + 1)
                    nc.scalar.activation(cqn[u], M[u][:, 0:QL], ACT.Square, scale=float(QL) ** -0.5, accum_out=sumsq[u][:, 0:1])
                    nc.scalar.activation(sq_junk[:, u * KL:(u + 1) * KL], M[u][:, QL:QL + KL], ACT.Square, scale=float(KL) ** -0.5,
                                         accum_out=sumsq[u][:, 1:2]).then_inc(sumsq_ready, 1)
                    act.wait_ge(gb_out[u], 16 * n + 16)
                    nc.scalar.copy(gbs[u], M[u][:, 512:1024]).then_inc(gb_ready, 1)
                for t, u, n in tiles:
                    act.wait_ge(conv_ps, t + 1)
                    nc.scalar.copy(gvs[u], T[u][:, 512:1024]).then_inc(gv_ready, 1)
                for t, u, n in tiles:
                    act.wait_ge(cT_ps, t + 1)
                    nc.scalar.copy(cqT[u].rearrange("p k c -> p (k c)"), M[u][:, 0:2 * P]).then_inc(cqT_ready, 1)
                    if isinstance(t, int) and t == PT:
                        nc.scalar.copy(latT[:, PT * P:], M[u][:, 2 * P:3 * P])
                        nc.scalar.copy(krTs[DN:HW, :], M[u][DN:HW, 3 * P:4 * P]).then_inc(latT_ready, 1)
                    else:
                        nc.scalar.copy(latT[:, ds(t * P, P)], M[u][:, 2 * P:3 * P])
                        nc.scalar.copy(kT[0][DN:HW, ds(t * P, P)], M[u][DN:HW, 3 * P:4 * P])
                        nc.scalar.copy(kT[1][DN:HW, ds(t * P, P)], M[u][DN:HW, 3 * P:4 * P]).then_inc(latT_ready, 1)
                for t, u, n in tiles:
                    act.wait_ge(q_ps, t + 1)
                    act.wait_ge(q_out[u], 16 * n + 16)
                    nc.scalar.copy(qrow[u][:, 0:384], M[u][:, 512:896])
                    nc.scalar.copy(qrow[u][:, 384:768], T[u][:, 0:384]).then_inc(q_rows, 1)

            with act.Fori(0, PT // 2) as j:
                project(two(j))
            project(LAST_TILE)

            act.wait_ge(q_turned, NT)
            for u, uses in ((0, 5), (1, 4)):
                act.wait_ge(q_out[u], 16 + 16 * uses)
                act.wait_ge(lat_out[u], 32 + 32 * uses)
                act.wait_ge(u_out[u], 16 + 16 * uses)
                act.wait_ge(gb_out[u], 16 + 16 * uses)
            act.wait_ge(edge_out, 16 * (2 + NB))
            for c, src in enumerate((T[0], T[1], M[0], M[1])):
                act.wait_ge(value_ps, c + 1)
                nc.scalar.copy(value[:, 2 * c:2 * c + 2, :].rearrange("p i c -> p (i c)"), src[:, :]).then_inc(value_ready, 1)
            with act.Fori(0, H // 2) as j:
                for h, u, n in two(j):
                    act.wait_ge(qT_ps, h + 1)
                    nc.scalar.mul(qT[u][0:HW, :], M[0][0:HW, :], MLA_SCALE).then_inc(qT_ready, 1)
                    for n in range(PT):
                        w = (ORDER[n] + 1) * P
                        act.wait_ge(negmax_ready, PT * h + n + 1)
                        nc.scalar.activation(pr[n % 2][:, 0:w], T[n % 2][:, 0:w], ACT.Exp, bias=negmax[n % 2][:, 0:1],
                                             scale=1.0, accum_out=rsum[n % 2][:, 0:1]).then_inc(exp_done, 1)

            act.wait_ge(sq_ps, 1)
            nc.scalar.mul(qTs[0:HW, :, :].rearrange("p h c -> p (h c)"), M[0][0:HW, :], MLA_SCALE).then_inc(sq_ready, 1)
            act.wait_ge(sq_ps, 3)
            nc.scalar.copy(qabs.rearrange("p h c -> p (h c)"), M[1][:, :]).then_inc(sq_ready, 1)
            with act.Fori(0, NB // 2) as j:
                for b, u, n in two(j):
                    act.wait_ge(latb_ps, b + 1)
                    nc.scalar.copy(latTb[u][:, 0:PAST], T[u][:, 0:512])
                    nc.scalar.copy(krTb[u][DN:HW, 0:PAST], T[u][DN:HW, 512:1024]).then_inc(latb_ready, 1)
                for b, u, n in two(j):
                    act.wait_ge(sb_negmax, b + 1)
                    nc.scalar.activation(p_b[u], M[u][:, 0:PAST + ROWS], ACT.Exp, bias=negmax[u][:, 0:1], scale=1.0,
                                         accum_out=rsum[u][:, 0:1]).then_inc(sb_exp, 1)
                for b, u, n in two(j):
                    act.wait_ge(pTb_ps, b + 1)
                    nc.scalar.copy(pT_b[u][:, 0:4, :].rearrange("p c q -> p (c q)"), T[u][:, 0:512])
                    nc.scalar.copy(pT_b[u][0:ROWS, 4, :], T[u][0:ROWS, 512:512 + P]).then_inc(pTb_ready, 1)
            act.wait_ge(mixTs_ps, 1)
            nc.scalar.copy(mixTs.rearrange("p k c -> p (k c)"), T[0][:, 0:512]).then_inc(mixTs_ready, 1)

            def turn(stage, u, base):
                act.wait_ge(rowsT_ps, base + 2 * stage + u + 1)
                nc.scalar.copy(aT[u].rearrange("p k c -> p (k c)"), T[u][:, :]).then_inc(rowsT_ready, 1)

            with act.Fori(0, PT // 2) as j:
                for t, u, n in two(j):
                    nc.scalar.copy(mix[u][:, 0:512], attn[:, ds(t, 1), :].rearrange("p a c -> p (a c)")).then_inc(attn_copied, 1)
                for t, u, n in two(j):
                    turn(0, u, 12 * j)
                for t, u, n in two(j):
                    turn(1, u, 12 * j)
                for t, u, n in two(j):
                    act.wait_ge(product_ps, 12 * j + 2 + u + 1)
                    nc.scalar.mul(res[u], M[u][:, :], X_SCALE).then_inc(xq_rows, 1)
                for t, u, n in two(j):
                    turn(2, u, 12 * j)
                for t, u, n in two(j):
                    act.wait_ge(xmax_ready, t + 1)
                    for h in range(XH):
                        got = nc.scalar.activation(mix[u][:, h * MEM:(h + 1) * MEM], M[u][:, h * MEM:(h + 1) * MEM], ACT.Exp,
                                                   bias=xmax[u][:, h:h + 1], scale=1.0, accum_out=xsum[u][:, h:h + 1])
                    got.then_inc(px_ready, 1)
                for stage in (3, 4, 5):
                    for t, u, n in two(j):
                        turn(stage, u, 12 * j)
            E0 = 6 * PT
            act.wait_ge(product_ps, E0)
            nc.scalar.copy(aT[0][:, 0:4, :].rearrange("p k c -> p (k c)"), mixTs.rearrange("p k c -> p (k c)"))
            act.wait_ge(rowsT_ps, E0 + 1)
            nc.scalar.copy(aT[0][:, 4:8, :].rearrange("p k c -> p (k c)"), T[0][:, 512:]).then_inc(rowsT_ready, 1)
            act.wait_ge(rowsT_ps, E0 + 2)
            nc.scalar.copy(aT[0].rearrange("p k c -> p (k c)"), T[0][:, :]).then_inc(rowsT_ready, 1)
            act.wait_ge(product_ps, E0 + 2)
            nc.scalar.mul(res[0], M[0][:, :], X_SCALE).then_inc(xq_rows, 1)
            act.wait_ge(rowsT_ps, E0 + 3)
            nc.scalar.copy(aT[0].rearrange("p k c -> p (k c)"), T[0][:, :]).then_inc(rowsT_ready, 1)

            def evacuate_memory(b):
                act.wait_ge(mkT_ps, b + 1)
                nc.scalar.copy(mkT_b[:, :, 0:P], T[0][:, :].rearrange("p (k c) -> p k c", k=KT)).then_inc(mkT_lo, 1)

            def attend_memory(b, last):
                act.wait_ge(sx_negmax, b + 1)
                nc.scalar.activation(px_b, M[0][:, 0:MEM], ACT.Exp, bias=negmax[0][:, 0:1], scale=1.0,
                                     accum_out=rsum[0][:, 0:1]).then_inc(sx_exp, 1)
                if not last:
                    evacuate_memory(b + 1)
                act.wait_ge(sxT_ps, b + 1)
                nc.scalar.copy(pxT_b.rearrange("p c q -> p (c q)"), M[0][:, 512:768]).then_inc(sxT_ready, 1)
                act.wait_ge(sxo_ps, b + 3)
                nc.scalar.copy(oxT[:, :, ds(b * ROWS, ROWS)], M[1][:, 0:P].rearrange("p (k r) -> p k r", k=KT)).then_inc(sxo_done, 1)

            evacuate_memory(0)
            with act.Fori(0, NB // 2 - 1) as j:
                for b, u, n in two(j):
                    attend_memory(b, False)
            for b, u, n in two(NB // 2 - 1):
                attend_memory(b, b == NB - 1)
            act.wait_ge(rowsT_ps, E0 + 4)
            nc.scalar.copy(aT[0].rearrange("p k c -> p (k c)"), T[0][:, :]).then_inc(rowsT_ready, 1)

            act.wait_ge(softmax_in, 1)
            nc.scalar.activation(r_eg, r_gd, ACT.Exp).then_inc(softmax_exp, 1)
            act.wait_ge(softmax_in, 2)
            nc.scalar.activation(r_e2, r_d2, ACT.Exp).then_inc(softmax_exp, 1)

            act.wait_ge(plan_ready, 1)
            pairs = act.value_load(plan[0:1, NBLK:NBLK + 1], min_val=1, max_val=NBLK // 2)
            pairs_less_1 = act.value_load(plan[0:1, NBLK + 1:NBLK + 2], min_val=0, max_val=NBLK // 2 - 1)

            def split_gate_up(b, chunks):
                for c in chunks:
                    if c % 4 == 0:
                        act.wait_ge(raw_in[c // 4], 32 * b + 32)
                    act.wait_ge(gu_used, 8 * b + c + 1)
                    nc.scalar.copy(high(c), w_raw[c // 4][:, c % 4, :]).then_inc(gu_high, 1)

            def split_down(b, chunks):
                for c in chunks:
                    if c == 0:
                        act.wait_ge(raw_in[2], 16 * b + 16)
                    act.wait_ge(down_used, 4 * b + c + 1)
                    nc.scalar.copy(high(8 + c), w_raw[2][:, c, :]).then_inc(down_high, 1)

            def silu(b, u):
                act.wait_ge(gu_used, 8 * b + 16)
                nc.scalar.activation(hid[u], M[0][:, 0:512], ACT.Silu).then_inc(silu_ready, 1)

            def rows_high(b, u):
                act.wait_ge(xgT_ps, b + 1)
                nc.scalar.copy(xT_parts[u][0], T[0][:, :]).then_inc(xgT_high, 1)

            def hidden_high(b, u):
                act.wait_ge(hidT_ps, b + 1)
                nc.scalar.copy(hidT_parts[u][0], T[1][:, 0:512]).then_inc(hidT_high, 1)

            def results(b, u):
                act.wait_ge(yo_free, j + 1)
                act.wait_ge(down_used, 4 * b + 8)
                nc.scalar.copy(yo[u], M[1][:, :]).then_inc(ye_rows, 1)

            rows_high(0, 0)
            split_gate_up(0, range(8))
            with act.Fori(0, NBLK // 2) as j:
                with act.If(j < pairs):
                    b0, b1 = 2 * j, 2 * j + 1
                    split_gate_up(b1, range(7))
                    silu(b0, 0)
                    split_gate_up(b1, range(7, 8))
                    rows_high(b1, 1)
                    hidden_high(b0, 0)
                    split_down(b0, range(4))
                    with act.If(j < pairs_less_1):
                        split_gate_up(b1 + 1, range(7))
                    silu(b1, 1)
                    with act.If(j < pairs_less_1):
                        split_gate_up(b1 + 1, range(7, 8))
                    split_down(b1, range(2))
                    hidden_high(b1, 1)
                    results(b0, 0)
                    split_down(b1, range(2, 4))
                    rows_high(b1 + 1, 0)
                    results(b1, 1)

            def last(tiles):
                for t, u, n in tiles:
                    act.wait_ge(last_in[u], 32 * n + 32)
                    nc.scalar.mul(xl[u], xl[u], ALPHA).then_inc(xl_scaled, 1)
                for t, u, n in tiles:
                    act.wait_ge(rstd_ready, NORMS + t + 1)
                    nc.scalar.activation(rl[u], rl[u], ACT.Identity, scale=rstd[u][:, 0:1], bias=shift_by[u][:, 0:1]).then_inc(normed3, 1)

            with act.Fori(0, PT // 2) as j:
                last(two(j))
            last(LAST_TILE)

        @block.vector
        def _(dve):
            step = Count("dve")

            dve.sem_inc(o_done, 2)
            dve.sem_inc(pT_ready, 1)
            dve.sem_inc(ctx_done, 2)
            dve.sem_inc(logits_done, 2)
            dve.sem_inc(gu_low, 8)
            dve.sem_inc(down_low, 4)
            dve.sem_inc(hid_ready, 1)
            for c in (0, 1):
                dve.wait_ge(mem_ps, 2 + c + 1)
                nc.vector.tensor_copy(memk[:, c, :], M[c][:, :]).then_inc(mem_dve, 1)
            for c in (0, 1):
                dve.wait_ge(mem_ps, 6 + c + 1)
                nc.vector.tensor_copy(memkT[:, :, c * P:(c + 1) * P], M[c][:, :].rearrange("p (k c) -> p k c", k=KT)).then_inc(mem_dve, 1)
            dve.wait_ge(consts_in, 16 * 10)
            dve.wait_ge(pads_zero, 1)

            def turn_rows(t, x, heads, rot):
                half = DR // 2
                cos = rope[:, ds(t, 1), 0:DR].to_broadcast([P, heads, DR])
                msin = rope[:, ds(t, 1), DR:DR + half].to_broadcast([P, heads, half])
                sin = rope[:, ds(t, 1), DR + half:].to_broadcast([P, heads, half])
                a, b = rot
                nc.vector.tensor_tensor(a, x, cos, ALU.mult)
                nc.vector.tensor_tensor(b[:, :, 0:half], x[:, :, half:], msin, ALU.mult)
                nc.vector.tensor_tensor(b[:, :, half:], x[:, :, 0:half], sin, ALU.mult).then_inc(dve_step, step.next())
                dve.wait_ge(dve_step, step.value())
                return a, b

            def project(tiles):
                for t, u, n in tiles:
                    dve.wait_ge(rrms_ready, t + 1)
                    nc.vector.scalar_tensor_tensor(cqn[u], M[u][:, 0:QL], rrms[u][:, 0:1], q_gain, ALU.mult, ALU.mult)
                    dve.wait_ge(lat_out[u], 32 * n + 32)
                    nc.vector.scalar_tensor_tensor(ckvn[u], M[u][:, QL:QL + KL], rrms[u][:, 1:2], kv_gain, ALU.mult, ALU.mult)
                    a, b = turn_rows(t, M[u][:, QL + KL:QL + KL + DR].rearrange("p (h c) -> p h c", h=1), 1, rot_k[u])
                    nc.vector.tensor_tensor(krpad[u][:, DN:].rearrange("p (h c) -> p h c", h=1), a, b, ALU.add).then_inc(norm_done, 1)
                for t, u, n in tiles:
                    dve.wait_ge(gv_ready, t + 1)
                    dve.wait_ge(u_out[u], 16 * n + 16)
                    nc.vector.tensor_tensor(us[u], T[u][:, 0:CW], gvs[u], ALU.mult).then_inc(u_ready, 1)
                for t, u, n in tiles:
                    dve.wait_ge(q_rows, t + 3)
                    x = qrow[u].rearrange("p (h c) -> p h c", h=H)[:, :, DN:]
                    a, b = turn_rows(t, x, H, rot_q[u])
                    nc.vector.tensor_tensor(x, a, b, ALU.add).then_inc(q_turned, 1)

            with dve.Fori(0, PT // 2) as j, step.loop(j, 4, PT // 2):
                project(two(j))
            project(LAST_TILE)

            dve.wait_ge(value_ready, 4)
            with dve.Fori(0, H // 2) as j, step.loop(j, 4 * PT, H // 2):
                for h, u, n in two(j):
                    dve.wait_ge(kT_ps, h + 3)
                    nc.vector.tensor_copy(kT[u][0:DN, :], M[1][0:DN, :]).then_inc(kT_ready, 1)

                    def row_max(n):
                        s, w = n % 2, (ORDER[n] + 1) * P
                        dve.wait_ge(s_ps, PT * h + n + 1)
                        nc.vector.memset(T[s][0:64, w - 64:w], FAR).then_inc(dve_step, step.next())
                        dve.wait_ge(dve_step, step.value())
                        nc.vector.tensor_reduce(negmax[s][:, 0:1], T[s][:, 0:w], AX.X, ALU.max, negate=True).then_inc(negmax_ready, 1)

                    row_max(0)
                    row_max(1)
                    def scale_rows(n):
                        s = n % 2
                        dve.wait_ge(o_ps, PT * h + n + 1)
                        nc.vector.tensor_scalar(attn[:, ORDER[n], ds(h * DV, DV)], M[1][:, s * 512:s * 512 + DV], rinv[s][:, 0:1],
                                                None, ALU.mult).then_inc(o_done, 1)

                    for n in range(PT):
                        s, i = n % 2, ORDER[n]
                        dve.wait_ge(pT_ps, PT * h + n + 1)
                        nc.vector.tensor_copy(prT[s][:, 0:i + 1, :].rearrange("p i c -> p (i c)"), M[0][:, 0:(i + 1) * P]).then_inc(pT_ready, 1)
                        dve.wait_ge(o_done, PT * h + n + 1)
                        nc.vector.reciprocal(rinv[s][:, 0:1], rsum[s][:, 0:1]).then_inc(dve_step, step.next())
                        if n > 0:
                            scale_rows(n - 1)
                        if n + 2 < PT:
                            row_max(n + 2)
                    dve.wait_ge(dve_step, step.value())
                    scale_rows(PT - 1)

            dve.wait_ge(sq_ps, 2)
            nc.vector.tensor_copy(wukT[0:DN, :, :].rearrange("p h c -> p (h c)"), T[0][0:DN, :]).then_inc(wukT_ready, 1)
            dve.wait_ge(sq_ready, 2)
            dve.wait_ge(sq_in, 32)
            with dve.Fori(0, NB // 2) as j, step.loop(j, 2, NB // 2):
                for b, u, n in two(j):
                    dve.wait_ge(ctx_ps, b + 1)
                    nc.vector.tensor_copy(qa_b[u], qabs[:, :, ds(b * ROWS, ROWS)])
                    nc.vector.tensor_copy(qr_b[u][0:HW], qTs[0:HW, :, ds(b * ROWS, ROWS)])
                    nc.vector.tensor_copy(latn_b[u][0:ROWS, :], lat_new[0:ROWS, ds(b, 1), :].rearrange("p a c -> p (a c)"))
                    nc.vector.tensor_copy(latTb[u][:, PAST:], latT[:, ds(PT * P + b * ROWS, ROWS)])
                    nc.vector.tensor_copy(krTb[u][DN:HW, PAST:], krTs[DN:HW, ds(b * ROWS, ROWS)]).then_inc(bq_ready, 1)
                for b, u, n in two(j):
                    dve.wait_ge(sb_ps, b + 1)
                    nc.vector.tensor_reduce(negmax[u][:, 0:1], M[u][:, 0:PAST + ROWS], AX.X, ALU.max, negate=True).then_inc(sb_negmax, 1)
                for b, u, n in two(j):
                    dve.wait_ge(sb_exp, b + 1)
                    nc.vector.reciprocal(rinv[u][:, 0:1], rsum[u][:, 0:1]).then_inc(dve_step, step.next())
                    dve.wait_ge(dve_step, step.value())
                    nc.vector.tensor_scalar(p_b[u], p_b[u], rinv[u][:, 0:1], None, ALU.mult).then_inc(sb_p, 1)
                for b, u, n in two(j):
                    dve.wait_ge(ctx_ps, b + 3)
                    nc.vector.tensor_copy(ctxT[:, :, ds(b * ROWS, ROWS)], M[u][:, 0:P].rearrange("p (h r) -> p h r", h=H)).then_inc(ctx_done, 1)

            dve.wait_ge(ln_in, 48)

            def add_norm(tiles, product_at, gain, shift, out_ready):
                for t, u, n in tiles:
                    dve.wait_ge(product_ps, product_at(u))
                    nc.vector.scalar_tensor_tensor(res[u], xr[u], ALPHA, M[u][:, :], ALU.mult, ALU.add).then_inc(dve_step, step.next())
                    dve.wait_ge(dve_step, step.value())
                    nc.vector.bn_stats(stats[u][:, 0:6], res[u][:, 0:512])
                    nc.vector.bn_stats(stats[u][:, 6:12], res[u][:, 512:]).then_inc(dve_step, step.next())
                    dve.wait_ge(dve_step, step.value())
                    dve.sem_inc(dve_waited, 1)
                    nc.vector.bn_aggr(moments[u][:, :], stats[u][:, :]).then_inc(var_ready, 1)
                for t, u, n in tiles:
                    dve.wait_ge(rstd_ready, norms[0] + u + 1)
                    nc.vector.tensor_scalar(res[u], res[u], moments[u][:, 0:1], rstd[u][:, 0:1], ALU.subtract, ALU.mult)\
                        .then_inc(dve_step, step.next())
                    dve.wait_ge(dve_step, step.value())
                    nc.vector.tensor_tensor(res[u], res[u], gain, ALU.mult).then_inc(dve_step, step.next())
                    dve.wait_ge(dve_step, step.value())
                    nc.vector.tensor_tensor(xr[u], res[u], shift, ALU.add).then_inc(out_ready, 1)

            with dve.Fori(0, PT // 2) as j, step.loop(j, 18, PT // 2):
                for t, u, n in two(j):
                    dve.wait_ge(xr_in[u], 16 * n + 16)
                norms = [4 * j]
                add_norm(two(j), lambda u: 12 * j + u + 1, gain1, shift1, x1_ready)
                for t, u, n in two(j):
                    dve.wait_ge(product_ps, 12 * j + 4 + u + 1)
                    nc.vector.tensor_reduce(xmax[u][:, :], M[u][:, :].rearrange("p (h m) -> p h m", h=XH), AX.X, ALU.max,
                                            negate=True).then_inc(xmax_ready, 1)
                for t, u, n in two(j):
                    dve.wait_ge(px_ready, t + 1)
                    nc.vector.reciprocal(xsum[u][:, :], xsum[u][:, :]).then_inc(dve_step, step.next())
                    dve.wait_ge(dve_step, step.value())
                    dve.wait_ge(product_ps, 12 * j + 6 + u + 1)
                    nc.vector.tensor_tensor(res[u].rearrange("p (h d) -> p h d", h=XH), M[u][:, :].rearrange("p (h d) -> p h d", h=XH),
                                            xsum[u][:, :].unsqueeze(2).to_broadcast([P, XH, XD]), ALU.mult).then_inc(ox_ready, 1)
                norms[0] = 4 * j + 2
                add_norm(two(j), lambda u: 12 * j + 8 + u + 1, gain2, shift2, x2_ready)
                for t, u, n in two(j):
                    dve.wait_ge(product_ps, 12 * j + 10 + u + 1)
                    nc.vector.tensor_tensor(logits[:, ds(t, 1), :].rearrange("p a c -> p (a c)"), M[u][:, 0:NG + NE], b_router[:, :],
                                            ALU.add).then_inc(logits_done, 1)

            E0 = 6 * PT
            norms = [2 * PT]
            dve.wait_ge(xr_in[0], 16 * 5)
            add_norm(LAST_TILE, lambda u: E0 + 1, gain1, shift1, x1_ready)
            dve.wait_ge(conv_ready, NT)
            nc.vector.memset(qx_b, 0.0).then_inc(dve_step, step.next())
            dve.wait_ge(dve_step, step.value())
            dve.wait_ge(rowsT_ready, E0 + 3)

            def evacuate_memory(b):
                dve.wait_ge(mkT_ps, b + 1)
                nc.vector.tensor_copy(mkT_b[:, :, P:], T[1][:, :].rearrange("p (k c) -> p k c", k=KT)).then_inc(mkT_hi, 1)

            def attend_memory(b, last):
                if not (isinstance(b, int) and b == 0):
                    dve.wait_ge(sx_ps, b)
                nc.vector.tensor_copy(qx_b[:, :, 0:ROWS], aT[0][:, :, ds(b * ROWS, ROWS)]).then_inc(qx_ready, 1)
                dve.wait_ge(sx_ps, b + 1)
                nc.vector.tensor_reduce(negmax[0][:, 0:1], M[0][:, 0:MEM], AX.X, ALU.max, negate=True).then_inc(sx_negmax, 1)
                dve.wait_ge(sx_exp, b + 1)
                nc.vector.reciprocal(rinv[0][:, 0:1], rsum[0][:, 0:1]).then_inc(dve_step, step.next())
                dve.wait_ge(dve_step, step.value())
                nc.vector.tensor_scalar(px_b, px_b, rinv[0][:, 0:1], None, ALU.mult).then_inc(sx_p, 1)
                if not last:
                    evacuate_memory(b + 1)

            evacuate_memory(0)
            attend_memory(0, False)
            attend_memory(1, False)
            with dve.Fori(1, NB // 2 - 1) as j, step.loop(j - 1, 2, NB // 2 - 2):
                for b, u, n in two(j):
                    attend_memory(b, False)
            for b, u, n in two(NB // 2 - 1):
                attend_memory(b, b == NB - 1)
            norms = [2 * PT + 1]
            add_norm(LAST_TILE, lambda u: E0 + 3, gain2, shift2, x2_ready)
            dve.wait_ge(product_ps, E0 + 4)
            nc.vector.tensor_tensor(logits[:, PT, :], M[0][:, 0:NG + NE], b_router[:, :], ALU.add).then_inc(logits_done, 1)

            def then(ins):
                ins.then_inc(dve_step, step.next())
                dve.wait_ge(dve_step, step.value())

            def wide(x, *shape):
                return x.unsqueeze(len(x.shape)).to_broadcast([P, *shape])

            def first_largest(values, n, best, scratch, pick):
                then(nc.vector.tensor_reduce(best, values, AX.X, ALU.max))
                then(nc.vector.tensor_tensor(scratch, values, wide(best, NT, n), ALU.is_equal))
                then(nc.vector.scalar_tensor_tensor(scratch, scratch, -64.0, iota[:, 0:n].unsqueeze(1).to_broadcast([P, NT, n]),
                                                    ALU.mult, ALU.add))
                then(nc.vector.tensor_reduce(r_first, scratch, AX.X, ALU.min))
                then(nc.vector.tensor_tensor(pick, scratch, wide(r_first, NT, n), ALU.is_equal))

            dve.wait_ge(logits_done, NT + 2)
            lg, le = logits[:, :, 0:NG], logits[:, :, NG:].rearrange("p t (g e) -> p t g e", g=NG)
            first_largest(lg, NG, r_best, r_s4, r_group)
            nc.vector.tensor_tensor(r_gd, lg, wide(r_best, NT, NG), ALU.subtract).then_inc(softmax_in, 1)
            then(nc.vector.tensor_tensor(r_all, le, wide(r_group, NT, NG, EG), ALU.mult))
            then(nc.vector.tensor_reduce(r_le, r_all.rearrange("p t g e -> p t e g"), AX.X, ALU.add))
            first_largest(r_le, EG, r_v1, r_s8, r_pick1)
            then(nc.vector.scalar_tensor_tensor(r_le, r_pick1, FAR, r_le, ALU.mult, ALU.add))
            first_largest(r_le, EG, r_v2, r_s8, r_pick2)
            nc.vector.tensor_tensor(r_d2, r_v2, r_v1, ALU.subtract).then_inc(softmax_in, 1)
            for k, pick in ((0, r_pick1), (1, r_pick2)):
                for g in range(NG):
                    got = nc.vector.tensor_tensor(r_hot[:, k, :, g * EG:(g + 1) * EG], pick,
                                                  r_group[:, :, g:g + 1].to_broadcast([P, NT, EG]), ALU.mult)
            then(got)
            nc.vector.tensor_tensor(picks.rearrange("p (t e) -> p t e", t=NT), r_hot[:, 0], r_hot[:, 1], ALU.add).then_inc(picks_ready, 1)
            dve.wait_ge(softmax_exp, 1)
            then(nc.vector.tensor_reduce(r_sum, r_eg, AX.X, ALU.add))
            dve.wait_ge(softmax_exp, 2)
            then(nc.vector.scalar_tensor_tensor(r_den, r_e2, 1.0, r_sum, ALU.add, ALU.mult))
            then(nc.vector.reciprocal(gates[:, 0, :], r_den))
            then(nc.vector.tensor_tensor(gates[:, 1, :], gates[:, 0, :], r_e2, ALU.mult))
            dve.wait_ge(rank_ps, 1)
            then(nc.vector.memset(r_before[:, 0, :], 0.0))
            then(nc.vector.tensor_copy(r_total, T[0][:, 512:512 + NT * NE].rearrange("p (t e) -> p t e", t=NT)))
            for t in range(NT):
                then(nc.vector.tensor_tensor(r_before[:, t + 1, :], r_before[:, t, :], r_total[:, t, :], ALU.add))
            then(nc.vector.tensor_tensor(r_rank, r_before[:, 0:NT, :], T[0][:, 0:NT * NE].rearrange("p (t e) -> p t e", t=NT), ALU.add))
            then(nc.vector.tensor_scalar(r_lim, iota[:, 0:NT], float(P), None, ALU.mult))
            then(nc.vector.tensor_tensor(r_cmp, wide(r_before[:, NT, :], NE, NT), r_lim.unsqueeze(1).to_broadcast([P, NE, NT]), ALU.is_gt))
            then(nc.vector.tensor_reduce(r_blocks, r_cmp, AX.X, ALU.add))
            then(nc.vector.tensor_tensor_scan(r_end, ones[:, 0:NE], r_blocks, 0.0, ALU.mult, ALU.add))
            then(nc.vector.tensor_tensor(r_start, r_end, r_blocks, ALU.subtract))
            then(nc.vector.scalar_tensor_tensor(r_rank, r_start.unsqueeze(1).to_broadcast([P, NT, NE]), float(P), r_rank, ALU.mult, ALU.add))
            for k in (0, 1):
                then(nc.vector.tensor_tensor(r_hot[:, k], r_hot[:, k], r_rank, ALU.mult))
                then(nc.vector.tensor_reduce(r_slot[:, :, k], r_hot[:, k], AX.X, ALU.add))
            then(nc.vector.tensor_copy(r_int, r_slot.rearrange("p t k -> p (t k)")))
            then(nc.vector.tensor_single_scalar(r_int2, r_int, 7, ALU.logical_shift_right))
            then(nc.vector.tensor_copy(r_blk, r_int2))
            then(nc.vector.tensor_single_scalar(r_int2, r_int, P - 1, ALU.bitwise_and))
            then(nc.vector.tensor_copy(r_pos, r_int2))
            for i in range(2 * NT):
                if i >= 2:
                    dve.wait_ge(map_ps, i - 1)
                nc.vector.tensor_scalar(sel_slot[i % 2], iota, r_pos[:, i:i + 1], None, ALU.is_equal)
                nc.vector.tensor_scalar(sel_blk[i % 2], iota[:, 0:NBLK], r_blk[:, i:i + 1], slot_id.rearrange("p t k -> p (t k)")[:, i:i + 1],
                                        ALU.is_equal, ALU.mult).then_inc(sel_ready, 1)
            then(nc.vector.tensor_tensor(r_plan[0:1], iota[0:1, 0:NBLK].unsqueeze(2).to_broadcast([1, NBLK, NE]),
                                         r_end[0:1, :].unsqueeze(1).to_broadcast([1, NBLK, NE]), ALU.is_ge))
            then(nc.vector.tensor_reduce(r_row[0:1, 0:NBLK], r_plan[0:1], AX.X, ALU.add))
            then(nc.vector.tensor_scalar(r_row[0:1, 0:NBLK], r_row[0:1, 0:NBLK], float(NE - 1), None, ALU.min))
            then(nc.vector.tensor_scalar(r_row[0:1, NBLK:NBLK + 1], r_end[0:1, NE - 1:NE], 1.0, None, ALU.add))
            then(nc.vector.tensor_copy(r_int3[0:1, :], r_row[0:1, 0:NBLK + 1]))
            then(nc.vector.tensor_single_scalar(plan[0:1, NBLK:NBLK + 1], r_int3[0:1, NBLK:NBLK + 1], 1, ALU.logical_shift_right))
            then(nc.vector.tensor_copy(plan[0:1, 0:NBLK], r_int3[0:1, 0:NBLK]))
            then(nc.vector.tensor_single_scalar(plan[0:1, NBLK + 1:NBLK + 2], plan[0:1, NBLK:NBLK + 1], 1, ALU.subtract))
            dve.wait_ge(map_ps, 2 * NT)
            then(nc.vector.tensor_scalar(r_map, M[1][:, 0:NBLK], 0.0, 8192.0, ALU.is_equal, ALU.mult))
            then(nc.vector.scalar_tensor_tensor(r_map, M[1][:, 0:NBLK], -1.0, r_map, ALU.add, ALU.add))
            then(nc.vector.tensor_copy(route_out[:, 0:NBLK], r_map))
            then(nc.vector.tensor_copy(r_mapi, r_map))
            then(nc.vector.tensor_single_scalar(r_mapi2, r_mapi, 1, ALU.logical_shift_right))
            then(nc.vector.memset(route_tok[:, NBLK:], 0))
            nc.vector.tensor_scalar(route_tok[:, 0:NBLK], r_mapi2, float(NT * P - 1), None, ALU.min).then_inc(plan_ready, 1)

            dve.wait_ge(plan_ready, 1)
            pairs = dve.value_load(plan[0:1, NBLK:NBLK + 1], min_val=1, max_val=NBLK // 2)
            pairs_less_1 = dve.value_load(plan[0:1, NBLK + 1:NBLK + 2], min_val=0, max_val=NBLK // 2 - 1)

            def take_low(out, x, highs):
                return nc.vector.tensor_tensor(out, x, highs.bitcast(f32), ALU.subtract)

            def split_gate_up(b, chunks):
                for c in chunks:
                    dve.wait_ge(gu_high, 8 * b + c + 1)
                    take_low(low(c), w_raw[c // 4][:, c % 4, :], high(c)).then_inc(gu_low, 1)

            def split_down(b, chunks):
                for c in chunks:
                    dve.wait_ge(down_high, 4 * b + c + 1)
                    take_low(low(8 + c), w_raw[2][:, c, :], high(8 + c)).then_inc(down_low, 1)

            def hidden(b, u):
                dve.wait_ge(silu_ready, b + 1)
                nc.vector.tensor_tensor(hid[u], hid[u], M[0][:, 512:1024], ALU.mult).then_inc(hid_ready, 1)

            def rows_low(b, u):
                dve.wait_ge(xgT_high, b + 1)
                take_low(xT_parts[u][1], T[0][:, :], xT_parts[u][0]).then_inc(xgT_low, 1)

            def hidden_low(b, u):
                dve.wait_ge(hidT_high, b + 1)
                take_low(hidT_parts[u][1], T[1][:, 0:512], hidT_parts[u][0]).then_inc(hidT_low, 1)

            rows_low(0, 0)
            split_gate_up(0, range(8))
            with dve.Fori(0, NBLK // 2) as j:
                with dve.If(j < pairs):
                    b0, b1 = 2 * j, 2 * j + 1
                    split_gate_up(b1, range(7))
                    hidden(b0, 0)
                    split_gate_up(b1, range(7, 8))
                    rows_low(b1, 1)
                    hidden_low(b0, 0)
                    split_down(b0, range(4))
                    with dve.If(j < pairs_less_1):
                        split_gate_up(b1 + 1, range(7))
                    hidden(b1, 1)
                    with dve.If(j < pairs_less_1):
                        split_gate_up(b1 + 1, range(7, 8))
                    split_down(b1, range(2))
                    hidden_low(b1, 1)
                    split_down(b1, range(2, 4))
                    rows_low(b1 + 1, 0)

            dve.wait_ge(ln3_in, 32)

            def last(tiles):
                for t, u, n in tiles:
                    dve.wait_ge(last_in[u], 32 * n + 32)
                    dve.wait_ge(xl_scaled, t + 1)
                    dve.wait_ge(y_out[u], 16 * n + 16)
                    then(nc.vector.scalar_tensor_tensor(rl[u], yk[u][:, 0, :], gates[:, 0, ds(t, 1)], xl[u], ALU.mult, ALU.add))
                    then(nc.vector.scalar_tensor_tensor(rl[u], yk[u][:, 1, :], gates[:, 1, ds(t, 1)], rl[u], ALU.mult, ALU.add))
                    nc.vector.bn_stats(stats[u][:, 0:6], rl[u][:, 0:512])
                    then(nc.vector.bn_stats(stats[u][:, 6:12], rl[u][:, 512:]))
                    dve.sem_inc(dve_waited, 1)
                    nc.vector.bn_aggr(moments[u][:, :], stats[u][:, :]).then_inc(var_ready, 1)
                for t, u, n in tiles:
                    dve.wait_ge(gain3_done, t + 1)
                    nc.vector.tensor_tensor(rl[u], rl[u], shift3, ALU.add).then_inc(y_ready, 1)

            with dve.Fori(0, PT // 2) as j, step.loop(j, 6, PT // 2):
                last(two(j))
            last(LAST_TILE)

        @block.gpsimd
        def _(pool):
            step = Count("pool")
            pool.sem_inc(yo_free, 1)
            nc.gpsimd.memset(minus_half[:, :], -0.5)
            nc.gpsimd.memset(minus_one[:, :], -1.0)
            nc.gpsimd.memset(zero_row[:, :], 0.0)
            pool.wait_ge(mem_ps, 6)
            nc.gpsimd.memset(krpad[0][:, 0:DN], 0.0)
            nc.gpsimd.memset(krpad[1][:, 0:DN], 0.0).then_inc(pads_zero, 1)
            pool.wait_ge(pads_zero, 1)

            def inverse_root(out, x, eps):
                pool.sem_inc(pool_waited, 1)
                nc.gpsimd.tensor_scalar(x, x, eps, None, ALU.add).then_inc(pool_step, step.next())
                pool.wait_ge(pool_step, step.value())
                return nc.gpsimd.tensor_tensor(out, x, minus_half[:, 0:x.shape[1]], ALU.pow)

            def latents(tiles):
                for t, u, n in tiles:
                    pool.wait_ge(sumsq_ready, t + 1)
                    inverse_root(rrms[u][:, :], sumsq[u][:, :], RMS_EPS).then_inc(rrms_ready, 1)

            with pool.Fori(0, PT // 2) as j, step.loop(j, 2, PT // 2):
                latents(two(j))
            latents(LAST_TILE)

            pool.wait_ge(kT_ps, 2 + H)
            pool.wait_ge(o_done, 2 + PT * H)
            for u in (0, 1):
                nc.gpsimd.memset(kr_b[u][:, :, 0:DN], 0.0)
                got = nc.gpsimd.memset(krTb[u][0:DN, :], 0.0)
            got.then_inc(pads_zero, 1)

            pool.wait_ge(consts_in, 16 * 10)

            def convolve(u, loads, turned):
                pool.wait_ge(conv_in, loads)
                if turned is not None:
                    pool.wait_ge(rowsT_ps, turned)
                out = conv_rows[u]
                nc.gpsimd.tensor_tensor(cv[:, 0:3, :], cv[:, 0:3, :], conv_w[:, :, :], ALU.mult).then_inc(pool_step, step.next())
                pool.wait_ge(pool_step, step.value())
                nc.gpsimd.tensor_tensor(out, cv[:, 0, :], cv[:, 1, :], ALU.add).then_inc(pool_step, step.next())
                pool.wait_ge(pool_step, step.value())
                nc.gpsimd.tensor_tensor(out, out, cv[:, 2, :], ALU.add).then_inc(pool_step, step.next())
                pool.wait_ge(pool_step, step.value())
                nc.gpsimd.tensor_tensor(out, out, cv[:, 3, :], ALU.mult).then_inc(conv_ready, 1)

            def deviation(u, at):
                pool.wait_ge(var_ready, at)
                inverse_root(rstd[u][:, :], moments[u][:, 1:2], LN_EPS).then_inc(rstd_ready, 1)

            convolve(0, 64, None)
            convolve(1, 128, None)
            with pool.Fori(0, PT // 2 - 1) as j, step.loop(j, 10, PT // 2 - 1):
                deviation(0, 4 * j + 1)
                deviation(1, 4 * j + 2)
                convolve(0, 128 * j + 192, 12 * j + 1)
                convolve(1, 128 * j + 256, 12 * j + 2)
                deviation(0, 4 * j + 3)
                deviation(1, 4 * j + 4)
            deviation(0, 13)
            deviation(1, 14)
            convolve(0, 64 * PT + 16 * (3 * NB + 1), 37)
            for at in (15, 16, 17, 18):
                deviation(0 if at != 16 else 1, at)

            pool.wait_ge(x2_out[0], 16 + 16 * 5)
            pool.wait_ge(x2_out[1], 16 + 16 * 4)
            pool.wait_ge(plan_ready, 1)

            def gather(b, u, copied):
                nc.gpsimd.tensor_copy(tok_now[u][:, :], route_tok[:, ds(b, 1)]).then_inc(idx_ready, 1)
                pool.wait_ge(idx_ready, copied)
                pool.sem_inc(pool_waited, 1)
                nc.gpsimd.indirect_dma_start(out=xg[u], out_offset=None, in_=x2_dram,
                                             in_offset=bass.IndirectOffsetOnAxis(ap=tok_now[u][:, 0:1], axis=0)).then_inc(xg_in[u], 16)

            gather(0, 0, 1)
            gather(1, 1, 2)
            pairs = pool.value_load(plan[0:1, NBLK:NBLK + 1], min_val=1, max_val=NBLK // 2)
            with pool.Fori(0, NBLK // 2) as j:
                with pool.If(j < pairs):
                    for b, u, n in two(j):
                        pool.wait_ge(xgT_ps, b + 1)
                        gather(b + 2, u, 4 * j + 3 + u)
                    for b, u, n in two(j):
                        nc.gpsimd.tensor_copy(out_now[u][:, :], route_out[:, ds(b, 1)]).then_inc(idx_ready, 1)
                        pool.wait_ge(idx_ready, 4 * j + 5 + u)
                        pool.wait_ge(ye_rows, b + 2)
                        pool.sem_inc(pool_waited, 1)
                        nc.gpsimd.indirect_dma_start(out=ye_dram, out_offset=bass.IndirectOffsetOnAxis(ap=out_now[u][:, 0:1], axis=0),
                                                     in_=yo[u], in_offset=None, bounds_check=2 * NT * P - 1,
                                                     oob_is_err=False).then_inc(ye_out[u], 16)
                    for b, u, n in two(j):
                        pool.wait_ge(ye_out[u], 16 * n + 16)
                    pool.sem_inc(yo_free, 1)
            pool.sem_inc(experts_done, 1)

            def last(tiles):
                for t, u, n in tiles:
                    pool.wait_ge(var_ready, NORMS + t + 1)
                    nc.gpsimd.tensor_tensor(moments[u][:, 0:1], moments[u][:, 0:1], minus_one[:, :], ALU.mult)
                    inverse_root(rstd[u][:, :], moments[u][:, 1:2], LN_EPS).then_inc(pool_step, step.next())
                    pool.wait_ge(pool_step, step.value())
                    nc.gpsimd.tensor_tensor(shift_by[u][:, :], moments[u][:, 0:1], rstd[u][:, :], ALU.mult).then_inc(rstd_ready, 1)
                for t, u, n in tiles:
                    pool.wait_ge(normed3, t + 1)
                    nc.gpsimd.tensor_tensor(rl[u], rl[u], gain3, ALU.mult).then_inc(gain3_done, 1)

            pool.wait_ge(ln3_in, 32)
            with pool.Fori(0, PT // 2) as j, step.loop(j, 4, PT // 2):
                last(two(j))
            last(LAST_TILE)


_INS = ['x_prompt', 'x_sample', 'cache_kv_latent', 'cache_k_rope', 'cache_conv', 'cache_mem_k', 'cache_mem_v',
        'mem_prompt', 'w_in', 'q_norm_g', 'kv_norm_g', 'w_uq', 'w_ukv', 'conv_w', 'w_out', 'ln1_g', 'ln1_b',
        'w_xq', 'w_xk', 'w_xv', 'w_xo', 'ln2_g', 'ln2_b', 'w_router_group', 'b_router_group',
        'w_router_expert', 'b_router_expert', 'w_exp_gate', 'w_exp_up', 'w_exp_down', 'ln3_g', 'ln3_b']
_OUTS = [('y_prompt', (1, 1024, 1024)), ('y_sample', (8, 16, 1024)), ('new_kv_latent_prompt', (1, 1, 1024, 128)),
         ('new_k_rope_prompt', (1, 1, 1024, 32)), ('new_conv_prompt', (1, 1, 2, 512)),
         ('new_mem_k_prompt', (1, 1, 256, 4, 256)), ('new_mem_v_prompt', (1, 1, 256, 4, 256)),
         ('new_kv_latent_sample', (1, 8, 16, 128)), ('new_k_rope_sample', (1, 8, 16, 32)),
         ('new_conv_sample', (1, 8, 2, 512))]


def kernel(**inputs):
    import numpy as _np
    import concourse.bacc as _bacc
    from concourse import mybir as _mybir
    from concourse.bass_utils import run_bass_kernel_spmd as _run

    nc = _bacc.Bacc("TRN2", target_bir_lowering=False, num_devices=1)
    arrays, ins, outs = {}, {}, {}
    for name in _INS:
        a = _np.ascontiguousarray(inputs[name])
        arrays[f"in_{name}"] = a
        ins[name] = nc.dram_tensor(f"in_{name}", a.shape, _mybir.dt.from_np(a.dtype), kind="ExternalInput").ap()
    arrays["in_tables"] = consts_table()
    ins["tables"] = nc.dram_tensor("in_tables", arrays["in_tables"].shape, _mybir.dt.float32, kind="ExternalInput").ap()
    for name, shape in _OUTS:
        outs[name] = nc.dram_tensor(f"out_{name}", shape, _mybir.dt.float32, kind="ExternalOutput").ap()
    encoder_layer_kernel(nc, ins, outs)
    r = _run(nc, [arrays], core_ids=[0])
    return tuple(r.results[0][f"out_{name}"] for name, _ in _OUTS)
```

```python
import concourse.bass as bass
from concourse import mybir
from contextlib import ExitStack, contextmanager


def consts_table():
    import numpy as np

    p = np.arange(128)
    ident = np.eye(128, dtype=np.float32)
    tri = (p[:, None] < p[None, :]).astype(np.float32)
    ones = np.ones((128, 128), np.float32)
    half = 16
    inv = (np.float32(10000.0) ** (-np.arange(half, dtype=np.float32) / np.float32(half))).astype(np.float32)
    rope = np.zeros((128, 9, 64), np.float32)
    for t in range(9):
        pos = (t * 128 + p if t < 8 else 512 + p % 16).astype(np.float32)
        ang = pos[:, None] * inv[None, :]
        c, s = np.cos(ang).astype(np.float32), np.sin(ang).astype(np.float32)
        rope[:, t] = np.concatenate([c, c, -s, s], 1)
    iota = np.broadcast_to(p.astype(np.float32), (128, 128))
    slot = 2 * (128 * np.arange(9)[None, :, None] + p[:, None, None]) + np.arange(2)[None, None, :] + 1
    return np.ascontiguousarray(np.concatenate(
        [ident, tri, ones, rope.reshape(128, -1), iota, slot.reshape(128, -1).astype(np.float32)], 1), np.float32)


class Count:

    def __init__(self, name):
        self.name, self.fixed, self.local, self.turn = name, 0, 0, None

    def next(self, by=1):
        self.local += by
        return by

    def value(self):
        own = self.fixed + self.local
        return own if self.turn is None else own + self.turn[0] * self.turn[1]

    @contextmanager
    def loop(self, j, per, turns):
        self.fixed, self.local, self.turn = self.fixed + self.local, 0, (j, per)
        yield
        assert self.local == per, (self.name, self.local, per)
        self.fixed, self.local, self.turn = self.fixed + turns * per, 0, None


def encoder_layer_kernel(nc, A, O):
    f32, f32r, i32, u32 = mybir.dt.float32, mybir.dt.float32r, mybir.dt.int32, mybir.dt.uint32
    ALU, ACT, AX = mybir.AluOpType, mybir.ActivationFunctionType, mybir.AxisListType
    ds = bass.ds

    P, D, NT, PT = 128, 1024, 9, 8
    NB, ROWS, PAST = 8, 16, 512
    H, DN, DR, DV = 8, 64, 32, 64
    HW = DN + DR
    QL, KL, CW = 256, 128, 512
    INW = QL + KL + DR + 3 * CW
    XH, XD, MEM = 4, 256, 256
    NG, EG, NE, FE = 4, 8, 32, 512
    NBLK = 50
    KT = D // P
    ALPHA = 2.0 ** 0.25
    MLA_SCALE, X_SCALE = float(HW) ** -0.5, float(XD) ** -0.5
    ORDER = (2, 4, 6, 7, 5, 3, 1, 0)
    NORMS = 2 * NT
    LN_EPS, RMS_EPS = 1e-5, 1e-6
    FAR = -1e30

    x_p = A["x_prompt"].rearrange("b s d -> (b s) d")
    x_s = A["x_sample"].rearrange("b s d -> (b s) d")
    y_p = O["y_prompt"].rearrange("b s d -> (b s) d")
    y_s = O["y_sample"].rearrange("b s d -> (b s) d")
    lat_p = O["new_kv_latent_prompt"].rearrange("l b s d -> (l b s) d")
    lat_s = O["new_kv_latent_sample"].rearrange("l b s d -> (l b s) d")
    kr_p = O["new_k_rope_prompt"].rearrange("l b s d -> (l b s) d")
    kr_s = O["new_k_rope_sample"].rearrange("l b s d -> (l b s) d")
    conv_p = O["new_conv_prompt"].rearrange("l b s d -> (l b s) d")
    conv_s = O["new_conv_sample"].rearrange("l b s d -> (l b) s d")
    mem_k_out = O["new_mem_k_prompt"].rearrange("l b (c p) h d -> p (l b c) (h d)", p=P)
    mem_v_out = O["new_mem_v_prompt"].rearrange("l b (c p) h d -> p (l b c) (h d)", p=P)
    mem_rows = A["mem_prompt"].rearrange("b (c p) d -> p (b c) d", p=P)
    cache_lat = A["cache_kv_latent"].rearrange("l b (c p) d -> (l b) p c d", p=P)
    cache_kr = A["cache_k_rope"].rearrange("l b (c p) d -> (l b) p c d", p=P)
    cache_conv = A["cache_conv"].rearrange("l b s d -> (l b) s d")
    cache_mk = A["cache_mem_k"].rearrange("l b (c p) h d -> (l b) p c (h d)", p=P)
    cache_mv = A["cache_mem_v"].rearrange("l b (c p) h d -> (l b) p c (h d)", p=P)

    def by_rows(name):
        return A[name].rearrange("l (k p) n -> p (l k) n", p=P)

    w_in_rows = by_rows("w_in")
    w_gate = A["w_exp_gate"].rearrange("l e (k p) n -> (l e) p k n", p=P)
    w_up = A["w_exp_up"].rearrange("l e (k p) n -> (l e) p k n", p=P)
    w_down = A["w_exp_down"].rearrange("l e (k p) n -> (l e) p k n", p=P)

    q_dram = nc.dram_tensor("q_rows", [NT * P, H * HW], f32).ap()
    u_dram = nc.dram_tensor("u_rows_prompt", [PT * P + 2, CW], f32).ap()
    us_dram = nc.dram_tensor("u_rows_sample", [NB, ROWS + 2, CW], f32).ap()
    gb_dram = nc.dram_tensor("gate_rows", [NT * P, CW], f32).ap()
    x2_dram = nc.dram_tensor("x2_rows", [NT * P, D], f32).ap()
    ye_dram = nc.dram_tensor("expert_rows", [2 * NT * P, D], f32).ap()
    ye_pairs = ye_dram.rearrange("(r k) d -> r k d", k=2)

    ctx = ExitStack()
    with ctx:
        def sb(name, shape, dt=f32):
            return ctx.enter_context(nc.sbuf_tensor(name, shape, dt))[tuple(slice(None) for _ in shape)]

        def sem(name):
            return ctx.enter_context(nc.semaphore(name))

        tables = sb("tables", [P, 3 * P + NT * 64 + P + 2 * NT])
        ident, tri, ones = (tables[:, i * P:(i + 1) * P] for i in range(3))
        rope = tables[:, 3 * P:3 * P + NT * 64].rearrange("p (t c) -> p t c", t=NT)
        iota = tables[:, 3 * P + NT * 64:4 * P + NT * 64]
        slot_id = tables[:, 4 * P + NT * 64:].rearrange("p (t k) -> p t k", k=2)
        with nc.sbuf_tensor("x_high0", [P, D], f32r) as first:
            x_high = [first[:, :]]
        conv_w = sb("conv_w_rows", [P, 3, CW])
        w_router = sb("w_router", [P, KT, NG + NE])
        b_router = sb("b_router", [P, NG + NE])
        logits = sb("logits", [P, NT, NG + NE])
        gates = sb("gates", [P, 2, NT])
        minus_half = sb("minus_half", [P, 2])
        minus_one = sb("minus_one", [P, 1])
        shift_by = [sb(f"shift_by{u}", [P, 1]) for u in (0, 1)]
        zero_row = sb("zero_row", [2, CW])
        with nc.sbuf_tensor("x_high1", [P, D], f32r) as second:
            x_high.append(second[:, :])
        shift2 = sb("shift2", [P, D])
        sumsq = [sb(f"sumsq{u}", [P, 2]) for u in (0, 1)]
        rrms = [sb(f"rrms{u}", [P, 2]) for u in (0, 1)]
        negmax = [sb(f"negmax{u}", [P, 1]) for u in (0, 1)]
        rsum = [sb(f"rsum{u}", [P, 1]) for u in (0, 1)]
        rinv = [sb(f"rinv{u}", [P, 1]) for u in (0, 1)]
        stats = [sb(f"stats{u}", [P, 12]) for u in (0, 1)]
        moments = [sb(f"moments{u}", [P, 2]) for u in (0, 1)]
        rstd = [sb(f"rstd{u}", [P, 1]) for u in (0, 1)]
        xmax = [sb(f"xmax{u}", [P, XH]) for u in (0, 1)]
        xsum = [sb(f"xsum{u}", [P, XH]) for u in (0, 1)]
        route_tok = sb("route_tok", [P, NBLK + 2], u32)
        route_out = sb("route_out", [P, NBLK + 2], u32)
        tok_now = [sb(f"tok_now{u}", [P, 1], u32) for u in (0, 1)]
        out_now = [sb(f"out_now{u}", [P, 1], u32) for u in (0, 1)]
        plan = sb("plan", [1, NBLK + 2], i32)

        ARENA, ROUNDED = 47912, 30720
        with nc.sbuf_tensor("arena", [P, ARENA], f32) as whole:
            arena = whole[:, :]
        LOWS = 39168 + 3 * D, 39168 + 7552
        x_low = []
        with nc.sbuf_tensor("below_lows", [P, LOWS[0]], f32), nc.sbuf_tensor("x_low0", [P, D], f32r) as first, \
                nc.sbuf_tensor("between_lows", [P, LOWS[1] - LOWS[0] - D], f32), nc.sbuf_tensor("x_low1", [P, D], f32r) as second:
            x_low += [first[:, :], second[:, :]]
        rounded = sb("rounded", [P, ROUNDED], f32r)
        beside = sb("beside", [P, ARENA - ROUNDED])

        def area(at, *dims):
            n = 1
            for d in dims:
                n *= d
            assert at + n <= ARENA, (at, dims)
            got, names = arena[:, at:at + n], "abc"[:len(dims)]
            if len(dims) == 1:
                return got
            return got.rearrange(f"p ({' '.join(names)}) -> p {' '.join(names)}",
                                 **{c: d for c, d in zip(names, dims)})

        def pair(at, *dims):
            n = 1
            for d in dims:
                n *= d
            return [area(at + u * n, *dims) for u in (0, 1)]

        WA, KEEP = 0, 3 * KT * D
        w_ukv = area(KEEP, H, DN + DV)
        latT = area(KEEP + 1024, NT * P)
        krTs = area(KEEP + 2176, P)
        memkT = area(KEEP + 2304, KT, MEM)
        memv = area(KEEP + 4352, 2, D)
        ATT = KEEP + 6400
        attn = area(ATT, PT, H * DV)
        VAL = ATT + 4096
        value = area(VAL, PT, H * DV)
        WORK = VAL + 4096
        mixTs = area(46336, 4, P)

        mem, memT, memk = area(VAL, 2, D), area(VAL + 2048, 2, KT, P), area(ATT + 2 * D, 2, D)
        w_xk, w_xv = area(WA, KT, D), area(WA + 8192, KT, D)
        def high(c):
            return rounded[:, c * 2 * D:c * 2 * D + D]

        def low(c):
            return rounded[:, c * 2 * D + D:(c + 1) * 2 * D]

        w_lat = [area(WA + 16384 + k * (INW - 2 * CW), INW - 2 * CW) for k in range(KT)]
        w_stage = [beside[:, WORK - ROUNDED + o * D:WORK - ROUNDED + (o + 1) * D] for o in (0, 1, 2, 4, 5, 6, 0, 1)]
        assert (LOWS[0], LOWS[1]) == (WORK + 3 * D, WORK + 7552)
        x_a, xT_a = pair(ATT, D), pair(ATT + 2 * D, KT, P)
        w_uq, sq_junk = area(VAL, 2, H * HW), area(VAL + 1536, QL)
        rot_q = [(area(o, H, DR), area(o + H * DR, H, DR)) for o in (VAL + 1792, WORK + 7040)]
        rot_k = [(area(o, 1, DR), area(o + DR, 1, DR)) for o in (VAL + 3776, VAL + 3840)]
        cqn, ckvn, krpad, cqT = pair(VAL + 2304, QL), pair(VAL + 2816, KL), pair(VAL + 3072, HW), pair(VAL + 3264, 2, P)
        kT = pair(WORK, D)
        gbs, us = pair(WORK + 2048, CW), pair(WORK + 4096, CW)
        qrow = pair(WORK + 5120, H * HW)
        q_gain, kv_gain = area(WA + 23808, QL), area(WA + 23808 + QL, KL)
        qh, wk = pair(WA + 16384, PT, HW), pair(WA + 17920, DN)
        qT, pr, prT = pair(WORK + 2048, D), pair(WORK + 4096, D), pair(WORK + 6144, PT, P)
        lat_b, kr_b = pair(WA + 16384, 4, KL), pair(WA + 17408, 4, HW)
        lat_new, q_s = area(WA + 18176, NB, KL), area(WA + 19200, H, HW)
        wukT, qabs, ctxT = area(VAL, H, P), area(VAL + 1024, H, P), area(VAL + 2048, H, P)
        qTs = area(VAL + 3072, H, P)
        latTb, krTb, p_b = pair(WORK, PAST + ROWS), pair(WORK + 1056, PAST + ROWS), pair(WORK + 2112, PAST + ROWS)
        pT_b = pair(WA + 20224, 5, P)
        qa_b, qr_b, latn_b = pair(WA + 21504, H, ROWS), pair(WA + 21760, H, ROWS), pair(WA + 22016, KL)
        w_out, w_xq, w_xo = area(WA, KT, D), area(WA + 8192, KT, D), area(WA + 16384, KT, D)
        xr, aT = [area(VAL + u * 4096, D) for u in (0, 1)], [area(VAL + u * 4096 + 1024, KT, P) for u in (0, 1)]
        mix, res = [area(VAL + u * 4096 + 2048, D) for u in (0, 1)], [area(VAL + u * 4096 + 3072, D) for u in (0, 1)]
        cv = area(VAL + 8192, 4, CW)
        conv_rows = pair(46848, CW)
        gain1, shift1, gain2 = area(KEEP, D), area(KEEP + D, D), area(VAL + 10240, D)
        mk_b, mv_b = [area(ATT, 2, D), area(VAL + 4096, 2, D)], [area(ATT + 2048, 2, D), area(VAL + 6144, 2, D)]
        mkT_b = memkT
        qx_b, px_b, pxT_b = area(VAL + 8192, KT, 32), area(VAL + 8448, MEM), area(VAL + 8704, 2, P)
        oxT = mix[0].rearrange("p (k c) -> p k c", k=KT)
        CH = 12
        w_raw = [beside[:, o:o + 4 * D].rearrange("p (k n) -> p k n", k=4) for o in (0, 8448, 12544)]

        def halves(at, n):
            return [[rounded[:, at + (2 * u + s) * n:at + (2 * u + s + 1) * n] for s in (0, 1)] for u in (0, 1)]

        xT_parts, hidT_parts = halves(CH * 2 * D, D), halves(CH * 2 * D + 4 * D, FE)
        xg, yo = ([beside[:, at + u * D:at + (u + 1) * D] for u in (0, 1)] for at in (4 * D, 6 * D))
        hid = [conv_w[:, u, :] for u in (0, 1)]
        at = [KEEP]

        def route(*dims, dt=f32):
            got = area(at[0], *dims)
            size = 1
            for d in dims:
                size *= d
            at[0] += size
            return got if dt is f32 else got.bitcast(dt)

        r_best, r_first, r_v1, r_v2, r_d2, r_e2, r_sum, r_den, r_lim = (route(NT) for _ in range(9))
        r_s4, r_group, r_gd, r_eg = (route(NT, NG) for _ in range(4))
        r_le, r_s8, r_pick1, r_pick2 = (route(NT, EG) for _ in range(4))
        r_all, r_hot, picks = route(NT * NE), route(2, NT, NE), route(NT * NE)
        r_all = r_all.rearrange("p (t g e) -> p t g e", t=NT, g=NG)
        r_before, r_total, r_rank, r_cmp = route(NT + 1, NE), route(NT, NE), route(NT, NE), route(NE, NT)
        r_blocks, r_end, r_start = (route(NE) for _ in range(3))
        r_slot, r_int, r_int2 = route(NT, 2), route(2 * NT, dt=i32), route(2 * NT, dt=i32)
        r_blk, r_pos, r_plan, r_row, r_int3 = route(2 * NT), route(2 * NT), route(NBLK, NE), route(NBLK + 1), route(NBLK + 1, dt=i32)
        r_map, r_mapi, r_mapi2 = route(NBLK), route(NBLK, dt=i32), route(NBLK, dt=i32)
        SEL = 6
        sel_slot, sel_blk = [route(P) for _ in range(SEL)], [route(NBLK) for _ in range(SEL)]
        assert at[0] <= ROUNDED
        gain3, shift3 = area(WA, D), area(WA + D, D)
        xl, rl = ([area(WA + (at + i) * D, D) for i in range(4)] for at in (2, 6))
        yk = [area(WA + 16384 + i * 2 * D, 2, D) for i in range(4)]

        T = [ctx.enter_context(nc.psum_tensor(f"T{u}", [P, 1024], f32)) for u in (0, 1)]
        M = [ctx.enter_context(nc.psum_tensor(f"M{u}", [P, 1024], f32)) for u in (0, 1)]

        tables_in, consts_in, mem_in = sem("tables_in"), sem("consts_in"), sem("mem_in")
        wxk_in, wxv_in, win_lo_in, win_hi_in = sem("wxk_in"), sem("wxv_in"), sem("win_lo_in"), sem("win_hi_in")
        mem_ps, mem_act, mem_dve, mem_out = sem("mem_ps"), sem("mem_act"), sem("mem_dve"), sem("mem_out")
        dve_step, pool_step = sem("dve_step"), sem("pool_step")
        waited = sem("waited")
        pads_zero = sem("pads_zero")
        x_in = [sem(f"x_in{u}") for u in (0, 1)]
        xT_ps, xT_ready = sem("xT_ps"), sem("xT_ready")
        latent_ps, conv_ps = sem("latent_ps"), sem("conv_ps")
        sumsq_ready, rrms_ready, gates_ready = (sem(n) for n in ("sumsq_ready", "rrms_ready", "gates_ready"))
        win_high, win_low, xT_low = (sem(n) for n in ("win_high", "win_low", "xT_low"))
        norm_done, u_ready, cT_ps, cqT_ready = (sem(n) for n in ("norm_done", "u_ready", "cT_ps", "cqT_ready"))
        q_ps, q_rows, q_turned = (sem(n) for n in ("q_ps", "q_rows", "q_turned"))
        gb_out, lat_out, u_out, q_out = ([sem(f"{n}{u}") for u in (0, 1)] for n in ("gb_out", "lat_out", "u_out", "q_out"))
        edge_out = sem("edge_out")
        value_ps, value_ready = sem("value_ps"), sem("value_ready")
        head_in = [sem(f"head_in{u}") for u in (0, 1)]
        qT_ps, kT_ps, qT_ready, kT_ready = (sem(n) for n in ("qT_ps", "kT_ps", "qT_ready", "kT_ready"))
        s_ps, negmax_ready, exp_done, pT_ps, pT_ready, o_ps, o_done = (
            sem(n) for n in ("s_ps", "negmax_ready", "exp_done", "pT_ps", "pT_ready", "o_ps", "o_done"))
        sq_in, sq_ps, sq_ready, wukT_ready = (sem(n) for n in ("sq_in", "sq_ps", "sq_ready", "wukT_ready"))
        cache_in = [sem(f"cache_in{u}") for u in (0, 1)]
        bq_ready, latb_ps, latb_ready, sb_ps, sb_negmax, sb_exp, sb_p, pTb_ps, pTb_ready, ctx_ps, ctx_done = (
            sem(n) for n in ("bq_ready", "latb_ps", "latb_ready", "sb_ps", "sb_negmax", "sb_exp", "sb_p",
                             "pTb_ps", "pTb_ready", "ctx_ps", "ctx_done"))
        mixTs_ps = sem("mixTs_ps")
        woq_in, wxo_in, ln_in = sem("woq_in"), sem("wxo_in"), sem("ln_in")
        conv_in, conv_ready, attn_copied = sem("conv_in"), sem("conv_ready"), sem("attn_copied")
        xr_in = [sem(f"xr_in{u}") for u in (0, 1)]
        rowsT_ps, rowsT_ready, product_ps = sem("rowsT_ps"), sem("rowsT_ready"), sem("product_ps")
        var_ready, rstd_ready, x1_ready, xq_rows, xmax_ready, px_ready, ox_ready, x2_ready, logits_done = (
            sem(n) for n in ("var_ready", "rstd_ready", "x1_ready", "xq_rows", "xmax_ready", "px_ready", "ox_ready",
                             "x2_ready", "logits_done"))
        x2_out = [sem(f"x2_out{u}") for u in (0, 1)]
        mk_in, mv_in = [sem(f"mk_in{u}") for u in (0, 1)], [sem(f"mv_in{u}") for u in (0, 1)]
        qx_ready, mkT_ps, mkT_lo, mkT_hi, sx_ps, sx_negmax, sx_exp, sx_p, sxT_ps, sxT_ready, sxo_ps, sxo_done = (
            sem(n) for n in ("qx_ready", "mkT_ps", "mkT_lo", "mkT_hi", "sx_ps", "sx_negmax", "sx_exp", "sx_p",
                             "sxT_ps", "sxT_ready", "sxo_ps", "sxo_done"))
        softmax_in, softmax_exp = sem("softmax_in"), sem("softmax_exp")
        sel_ready, map_ps, plan_ready, routes_ready = (
            sem(n) for n in ("sel_ready", "map_ps", "plan_ready", "routes_ready"))
        raw_in = [sem(f"raw_in{g}") for g in range(3)]
        xg_in, ye_out = ([sem(f"{n}{u}") for u in (0, 1)] for n in ("xg_in", "ye_out"))
        gu_high, gu_low, gu_used, down_high, down_low, down_used = (
            sem(n) for n in ("gu_high", "gu_low", "gu_used", "down_high", "down_low", "down_used"))
        xgT_ps, xgT_high, xgT_low, silu_ready, hid_ready, hidT_ps, hidT_high, hidT_low, ye_rows = (
            sem(n) for n in ("xgT_ps", "xgT_high", "xgT_low", "silu_ready", "hid_ready", "hidT_ps", "hidT_high",
                             "hidT_low", "ye_rows"))
        yo_free, idx_ready, ln3_in = sem("yo_free"), sem("idx_ready"), sem("ln3_in")
        last_in = [sem(f"last_in{i}") for i in range(4)]
        y_ready = sem("y_ready")
        xl_scaled, normed3, gain3_done = sem("xl_scaled"), sem("normed3"), sem("gain3_done")
        y_out = [sem(f"y_out{i}") for i in range(4)]

        block = ctx.enter_context(nc.Block())

        def tokens(p, s, t):
            return s if isinstance(t, int) and t == PT else p[ds(t * P, P), :]

        def two(j):
            return [(2 * j, 0, j), (2 * j + 1, 1, j)]

        def four(g):
            return [(4 * g + i, i, g) for i in range(4)]

        LAST_TILE = [(PT, 0, PT // 2)]
        LAST_OF_FOURS = [(PT, 0, PT // 4)]
        GB, GC, GV = QL + KL + DR, QL + KL + DR + CW, QL + KL + DR + 2 * CW

        def in_turn(tiles, first, second):
            for n, tile in enumerate(tiles):
                first(*tile)
                if n > 0:
                    second(*tiles[n - 1])
            second(*tiles[-1])

        @block.sync
        def _(sp):
            for u in (0, 1):
                sp.sem_inc(gb_out[u], 16)
                sp.sem_inc(lat_out[u], 32)
                sp.sem_inc(u_out[u], 16)
                sp.sem_inc(q_out[u], 16)
                sp.sem_inc(x2_out[u], 16)
            for i in range(4):
                sp.sem_inc(y_out[i], 16)
            sp.dma_start(tables, A["tables"]).then_inc(tables_in, 16)
            sp.dma_start(mem, mem_rows).then_inc(mem_in, 16)
            sp.dma_start(w_xk, by_rows("w_xk")).then_inc(wxk_in, 16)
            sp.dma_start(w_xv, by_rows("w_xv")).then_inc(wxv_in, 16)
            for u in (0, 1):
                sp.dma_start(x_a[u], x_p[u * P:(u + 1) * P, :]).then_inc(x_in[u], 16)
            w_gates = w_in_rows[:, :, GC:INW]
            for k in range(6):
                sp.dma_start(w_stage[k], w_gates[:, k, :]).then_inc(raw_in[2], 16)
            for k in range(KT):
                sp.dma_start(w_lat[k], w_in_rows[:, k, 0:GC]).then_inc(win_lo_in, 16)
            for dst, src in ((q_gain, A["q_norm_g"]), (kv_gain, A["kv_norm_g"]), (b_router[:, 0:NG], A["b_router_group"]),
                             (b_router[:, NG:], A["b_router_expert"].rearrange("l g e -> l (g e)"))):
                sp.dma_start(dst, src.to_broadcast([P, dst.shape[1]])).then_inc(consts_in, 16)
            sp.dma_start(w_router[:, :, 0:NG], by_rows("w_router_group")).then_inc(consts_in, 16)
            sp.dma_start(w_router[:, :, NG:], by_rows("w_router_expert")).then_inc(consts_in, 16)
            sp.dma_start(w_ukv, A["w_ukv"].rearrange("l p (h c) -> p (l h) c", h=H)).then_inc(win_hi_in, 16)
            sp.wait_ge(mem_ps, 2)
            sp.dma_start(w_uq, by_rows("w_uq")).then_inc(win_hi_in, 16)
            for k in (6, 7):
                sp.wait_ge(win_low, k - 5)
                sp.dma_start(w_stage[k], w_gates[:, k, :]).then_inc(raw_in[2], 16)
            sp.wait_ge(mem_dve, 2)
            sp.dma_start(mem_k_out, memk).then_inc(mem_out, 16)
            sp.wait_ge(mem_act, 4)
            sp.dma_start(mem_v_out, memv).then_inc(mem_out, 16)
            sp.wait_ge(pads_zero, 1)
            sp.dma_start(u_dram[0:2, :], zero_row).then_inc(edge_out, 16)
            sp.dma_start(us_dram[:, 0:2, :], cache_conv).then_inc(edge_out, 16)

            def store_rows(tiles):
                for t, u, n in tiles:
                    sp.wait_ge(gates_ready, t + 1)
                    sp.dma_start(gb_dram[ds(t * P, P), :], gbs[u]).then_inc(gb_out[u], 16)
                for t, u, n in tiles:
                    sp.wait_ge(norm_done, t + 1)
                    sp.dma_start(tokens(lat_p, lat_s, t), ckvn[u]).then_inc(lat_out[u], 16)
                    sp.dma_start(tokens(kr_p, kr_s, t), krpad[u][:, DN:]).then_inc(lat_out[u], 16)
                for t, u, n in tiles:
                    sp.wait_ge(u_ready, t + 1)
                    if isinstance(t, int) and t == PT:
                        for b in range(NB):
                            sp.dma_start(us_dram[b, 2:, :], us[u][b * ROWS:(b + 1) * ROWS, :]).then_inc(edge_out, 16)
                        sp.sem_inc(u_out[u], 16)
                    else:
                        sp.dma_start(u_dram[ds(t * P + 2, P), :], us[u]).then_inc(u_out[u], 16)
                for t, u, n in tiles:
                    sp.wait_ge(q_turned, t + 1)
                    sp.dma_start(q_dram[ds(t * P, P), :], qrow[u]).then_inc(q_out[u], 16)

            with sp.Fori(0, 3) as j:
                for t, u, n in two(j):
                    sp.wait_ge(xT_ps, t + 1)
                    sp.dma_start(x_a[u], x_p[ds((t + 2) * P, P), :]).then_inc(x_in[u], 16)
                store_rows(two(j))
            sp.wait_ge(xT_ps, 7)
            sp.dma_start(x_a[0], x_s).then_inc(x_in[0], 16)
            store_rows(two(3))
            store_rows(LAST_TILE)

            for u, uses in ((0, 5), (1, 4)):
                sp.wait_ge(q_out[u], 16 + 16 * uses)
                sp.wait_ge(lat_out[u], 32 + 32 * uses)
                sp.wait_ge(u_out[u], 16 + 16 * uses)
                sp.wait_ge(gb_out[u], 16 + 16 * uses)
            sp.wait_ge(conv_ps, NT)
            sp.dma_start(shift2, A["ln2_b"].to_broadcast([P, D])).then_inc(consts_in, 16)
            for k in range(3):
                sp.dma_start(conv_w[:, k, :], A["conv_w"][0, k:k + 1, :].to_broadcast([P, CW])).then_inc(consts_in, 16)
            q_heads = q_dram[0:PT * P, :].rearrange("(i p) c -> p i c", p=P)
            w_ukv_cols = A["w_ukv"].rearrange("l p c -> (l p) c")

            def load_head(h, u):
                sp.dma_start(qh[u], q_heads[:, :, ds(h * HW, HW)]).then_inc(head_in[u], 16)
                sp.dma_start(wk[u], w_ukv_cols[:, ds(h * (DN + DV), DN)]).then_inc(head_in[u], 16)

            load_head(0, 0)
            load_head(1, 1)
            sp.dma_start(w_out, by_rows("w_out")).then_inc(woq_in, 16)
            sp.dma_start(w_xq, by_rows("w_xq")).then_inc(woq_in, 16)
            sp.dma_start(q_s, q_dram[PT * P:, :].rearrange("p (h c) -> p h c", h=H)).then_inc(sq_in, 16)
            sp.dma_start(lat_new[0:ROWS, :, :], lat_s.rearrange("(b r) c -> r b c", r=ROWS)).then_inc(sq_in, 16)
            sp.wait_ge(edge_out, 16 * (2 + NB))
            sp.dma_start(conv_p, u_dram[PT * P:PT * P + 2, :]).then_inc(edge_out, 16)
            sp.dma_start(conv_s, us_dram[:, ROWS:, :]).then_inc(edge_out, 16)
            with sp.Fori(0, 3) as j:
                for h, u, n in two(j):
                    sp.wait_ge(kT_ps, h + 3)
                    load_head(h + 2, u)
            sp.wait_ge(kT_ps, 2 + H)

            def load_cache(tiles):
                for b, u, n in tiles:
                    sp.wait_ge(ctx_ps, b + 1)
                    sp.dma_start(lat_b[u], cache_lat[ds(b, 1), :, :, :].rearrange("b p c d -> p (b c) d")).then_inc(cache_in[u], 16)
                    sp.dma_start(kr_b[u][:, :, DN:], cache_kr[ds(b, 1), :, :, :].rearrange("b p c d -> p (b c) d")).then_inc(cache_in[u], 16)

            load_cache(two(0))
            def load_conv(t):
                if isinstance(t, int) and t == PT:
                    for k in range(3):
                        for b in range(NB):
                            sp.dma_start(cv[b * ROWS:(b + 1) * ROWS, k, :], us_dram[b, k:k + ROWS, :]).then_inc(conv_in, 16)
                else:
                    for k in range(3):
                        sp.dma_start(cv[:, k, :], u_dram[ds(t * P + k, P), :]).then_inc(conv_in, 16)
                sp.dma_start(cv[:, 3, :], gb_dram[ds(t * P, P), :]).then_inc(conv_in, 16)

            sp.wait_ge(o_done, 2 + PT * H)
            load_conv(0)
            sp.dma_start(gain2, A["ln2_g"].to_broadcast([P, D])).then_inc(ln_in, 16)
            load_cache(two(1))
            sp.wait_ge(conv_ready, 1)
            load_conv(1)
            with sp.Fori(2, NB // 2) as j:
                load_cache(two(j))

            sp.wait_ge(mixTs_ps, 1)
            for dst, name in ((gain1, "ln1_g"), (shift1, "ln1_b")):
                sp.dma_start(dst, A[name].to_broadcast([P, D])).then_inc(ln_in, 16)
            sp.dma_start(w_xo, by_rows("w_xo")).then_inc(wxo_in, 16)

            def load_x(tiles):
                for t, u, n in tiles:
                    sp.wait_ge(logits_done, t + 1)
                    sp.wait_ge(x2_out[u], 16 * n + 16)
                    sp.dma_start(xr[u], tokens(x_p, x_s, t)).then_inc(xr_in[u], 16)

            def store_x2(tiles):
                for t, u, n in tiles:
                    sp.wait_ge(x2_ready, t + 1)
                    sp.dma_start(x2_dram[ds(t * P, P), :], xr[u]).then_inc(x2_out[u], 16)

            with sp.Fori(0, 3) as j:
                load_x(two(j))
                for t, u, n in two(j):
                    sp.wait_ge(conv_ready, t + 2)
                    load_conv(t + 2)
                store_x2(two(j))
            load_x(two(3))
            sp.wait_ge(conv_ready, PT)
            load_conv(PT)
            store_x2(two(3))
            load_x(LAST_TILE)

            sp.wait_ge(x2_out[1], 16 + 16 * 4)
            def load_mk(b, u):
                sp.dma_start(mk_b[u], cache_mk[ds(b, 1), :, :, :].rearrange("b p c d -> p (b c) d")).then_inc(mk_in[u], 16)

            def load_mv(b, u):
                sp.dma_start(mv_b[u], cache_mv[ds(b, 1), :, :, :].rearrange("b p c d -> p (b c) d")).then_inc(mv_in[u], 16)

            sp.wait_ge(attn_copied, PT)
            load_mk(0, 0)
            load_mv(0, 0)
            sp.wait_ge(logits_done, PT + 2)
            load_mk(1, 1)
            load_mv(1, 1)
            with sp.Fori(1, NB // 2) as j:
                for b, u, n in two(j):
                    sp.wait_ge(mkT_ps, b - 1)
                    load_mk(b, u)
                    sp.wait_ge(sxo_ps, b + 1)
                    load_mv(b, u)

            def load_gate_up(b, e):
                for g in (0, 1):
                    sp.wait_ge(gu_low, 8 * b + 4 * (g + 1))
                    for src, c in ((w_gate, 0), (w_up, FE)):
                        sp.dma_start(w_raw[g][:, :, c:c + FE],
                                     src[ds(e, 1), :, 4 * g:4 * g + 4, :].rearrange("e p k n -> p (e k) n")).then_inc(raw_in[g], 16)

            def load_down(b, e):
                sp.wait_ge(down_low, 4 * b + 4)
                sp.dma_start(w_raw[2], w_down[ds(e, 1), :, :, :].rearrange("e p k n -> p (e k) n")).then_inc(raw_in[2], 16)

            sp.wait_ge(sxo_ps, 2 + NB)
            load_gate_up(0, 0)
            store_x2(LAST_TILE)

            sp.wait_ge(logits_done, NT + 2)
            load_down(0, 0)
            sp.wait_ge(plan_ready, 1)
            pairs = sp.value_load(plan[0:1, NBLK:NBLK + 1], min_val=1, max_val=NBLK // 2)
            pairs_less_1 = sp.value_load(plan[0:1, NBLK + 1:NBLK + 2], min_val=0, max_val=NBLK // 2 - 1)

            def expert(b):
                return sp.value_load(plan[0:1, ds(b, 1)], min_val=0, max_val=NE - 1)

            with sp.Fori(0, NBLK // 2) as j:
                with sp.If(j < pairs):
                    b0, b1 = 2 * j, 2 * j + 1
                    e1 = expert(b1)
                    load_gate_up(b1, e1)
                    with sp.If(j > 0):
                        load_down(b0, expert(b0))
                    with sp.If(j < pairs_less_1):
                        load_gate_up(b1 + 1, expert(b1 + 1))
                    load_down(b1, e1)

            def load_x2(tiles):
                for t, i, n in tiles:
                    sp.dma_start(xl[i], x2_dram[ds(t * P, P), :]).then_inc(last_in[i], 16)

            def load_picks(tiles):
                for t, i, n in tiles:
                    sp.dma_start(yk[i], ye_pairs[ds(t * P, P), :, :]).then_inc(last_in[i], 16)

            def store_y(tiles):
                for t, i, n in tiles:
                    sp.wait_ge(y_ready, t + 1)
                    sp.dma_start(tokens(y_p, y_s, t), rl[i]).then_inc(y_out[i], 16)

            sp.wait_ge(gu_used, 16 * pairs + 8)
            sp.dma_start(gain3, A["ln3_g"].to_broadcast([P, D])).then_inc(ln3_in, 16)
            sp.dma_start(shift3, A["ln3_b"].to_broadcast([P, D])).then_inc(ln3_in, 16)
            load_x2(four(0))
            sp.wait_ge(yo_free, pairs + 1)
            load_picks(four(0))
            for tile in four(1) + LAST_OF_FOURS:
                sp.wait_ge(var_ready, NORMS + tile[0] - 3)
                load_x2([tile])
                load_picks([tile])
                store_y([(tile[0] - 4, tile[0] % 4, 0)])
            for t in range(PT - 3, NT):
                store_y([(t, t % 4, 0)])
            for i in range(4):
                sp.wait_ge(y_out[i], 16 + 16 * (3 if i == 0 else 2))
            sp.wait_ge(mem_out, 32)
            sp.wait_ge(edge_out, 16 * (4 + NB))
            sp.wait_ge(lat_out[0], 32 + 32 * 5)
            sp.wait_ge(lat_out[1], 32 + 32 * 4)
            sp.wait_ge(x2_out[0], 16 + 16 * 5)

        @block.tensor
        def _(pe):
            for two_ahead in (kT_ps, ctx_ps, sxo_ps):
                pe.sem_inc(two_ahead, 2)
            pe.sem_inc(gu_used, 8)
            pe.sem_inc(down_used, 4)

            def transposes(out, rows, n, width=P):
                for k in range(n):
                    got = nc.tensor.transpose(out[:, k * P:(k + 1) * P] if width == P else out[0:width, k * P:(k + 1) * P],
                                              rows[:, k * width:(k + 1) * width], ident)
                return got

            def product(out, lhsT, w, cols, halves=(0, 1)):
                for half, (c0, c1) in zip(halves, cols):
                    for k in range(KT):
                        w_k = w[k] if isinstance(w, list) else w[:, k, :]
                        got = nc.tensor.matmul(out[:, half * 512:half * 512 + c1 - c0], lhsT[:, k, :], w_k[:, c0:c1],
                                               start=(k == 0), stop=(k == KT - 1))
                return got

            BOTH = [(0, 512), (512, 1024)]
            pe.wait_ge(tables_in, 16)
            pe.wait_ge(mem_in, 16)
            for c in (0, 1):
                transposes(T[c], mem[:, c, :], KT).then_inc(mem_ps, 1)
            pe.wait_ge(wxk_in, 16)
            for c in (0, 1):
                pe.wait_ge(mem_act, c + 1)
                product(M[c], memT[:, c, :, :], w_xk, BOTH).then_inc(mem_ps, 1)
            pe.wait_ge(wxv_in, 16)
            for c in (0, 1):
                product(T[c], memT[:, c, :, :], w_xv, BOTH).then_inc(mem_ps, 1)
            for c in (0, 1):
                pe.wait_ge(mem_dve, c + 1)
                transposes(M[c], memk[:, c, :], KT).then_inc(mem_ps, 1)
            pe.wait_ge(mem_act, 4)
            pe.wait_ge(mem_dve, 4)
            pe.wait_ge(win_lo_in, 16 * KT)
            pe.wait_ge(win_hi_in, 32)
            pe.wait_ge(pads_zero, 1)

            def project(tiles):
                for t, u, n in tiles:
                    pe.wait_ge(x_in[u], 16 * n + 16)
                    pe.wait_ge(q_rows, t + 1)
                    transposes(T[u], x_a[u], KT).then_inc(xT_ps, 1)
                for t, u, n in tiles:
                    pe.wait_ge(xT_ready, 2 * t + 1)
                    product(M[u], xT_a[u], w_lat, [(0, GB), (GB, GC)]).then_inc(latent_ps, 1)
                for t, u, n in tiles:
                    pe.wait_ge(win_low, KT)
                    pe.wait_ge(xT_low, t + 1)
                    for c in (0, CW):
                        for x, parts in ((x_high[u], (high, low)), (x_low[u], (high,))):
                            for k in range(KT):
                                for part in parts:
                                    got = nc.tensor.matmul(T[u][:, c:c + CW], x[:, k * P:(k + 1) * P], part(k)[:, c:c + CW],
                                                           start=(k == 0 and part is high and x is x_high[u]),
                                                           stop=(k == KT - 1 and x is x_low[u]))
                    got.then_inc(conv_ps, 1)
                for t, u, n in tiles:
                    pe.wait_ge(norm_done, t + 1)
                    transposes(M[u], cqn[u], 2)
                    nc.tensor.transpose(M[u][:, 2 * P:3 * P], ckvn[u], ident)
                    nc.tensor.transpose(M[u][0:HW, 3 * P:4 * P], krpad[u], ident).then_inc(cT_ps, 1)
                for t, u, n in tiles:
                    pe.wait_ge(cqT_ready, t + 1)
                    pe.wait_ge(u_ready, t + 1)
                    for dst, c in ((M[u][:, 512:896], 0), (T[u][:, 0:384], 384)):
                        for k in (0, 1):
                            got = nc.tensor.matmul(dst, cqT[u][:, k, :], w_uq[:, k, c:c + 384], start=(k == 0), stop=(k == 1))
                    got.then_inc(q_ps, 1)

            with pe.Fori(0, PT // 2) as j:
                project(two(j))
            project(LAST_TILE)

            pe.wait_ge(q_rows, 2 + NT)
            for c, dst in enumerate((T[0], T[1], M[0], M[1])):
                for i in (0, 1):
                    got = nc.tensor.matmul(dst[:, i * 512:(i + 1) * 512], latT[:, (2 * c + i) * P:(2 * c + i + 1) * P],
                                           w_ukv[:, :, DN:], start=True, stop=True)
                got.then_inc(value_ps, 1)
            pe.wait_ge(value_ready, 4)
            with pe.Fori(0, H // 2) as j:
                for h, u, n in two(j):
                    pe.wait_ge(head_in[u], 32 * n + 32)
                    pe.wait_ge(pT_ready, PT * h + 1)
                    for i in range(PT):
                        got = nc.tensor.transpose(M[0][0:HW, i * P:(i + 1) * P], qh[u][:, i, :], ident)
                    got.then_inc(qT_ps, 1)
                    pe.wait_ge(o_done, PT * h + 2)
                    for c in (0, 1):
                        got = nc.tensor.matmul(M[1][0:DN, c * 512:(c + 1) * 512], wk[u], latT[:, c * 512:(c + 1) * 512],
                                               start=True, stop=True)
                    got.then_inc(kT_ps, 1)
                    pe.wait_ge(qT_ready, h + 1)
                    pe.wait_ge(kT_ready, h + 1)

                    def scores(n):
                        i = ORDER[n]
                        pe.wait_ge(exp_done, PT * h + n + 1)
                        for c in range(0, (i + 1) * P, 512):
                            c1 = min(c + 512, (i + 1) * P)
                            got = nc.tensor.matmul(T[n % 2][:, c:c1], qT[u][0:HW, i * P:(i + 1) * P], kT[u][0:HW, c:c1],
                                                   start=True, stop=True)
                        got.then_inc(s_ps, 1)

                    def weigh_values(n):
                        i = ORDER[n]
                        pe.wait_ge(pT_ready, PT * h + n + 2)
                        pe.wait_ge(o_done, PT * h + n + 1)
                        o = M[1][:, (n % 2) * 512:(n % 2) * 512 + DV]
                        for c in range(i + 1):
                            got = nc.tensor.matmul(o, prT[n % 2][:, c, :], value[:, c, ds(h * DV, DV)], start=(c == 0), stop=(c == i))
                        got.then_inc(o_ps, 1)

                    scores(0)
                    scores(1)
                    for n in range(PT):
                        pe.wait_ge(exp_done, PT * h + n + 3)
                        pe.wait_ge(pT_ready, PT * h + n + 1)
                        transposes(M[0], pr[n % 2], ORDER[n] + 1).then_inc(pT_ps, 1)
                        if n + 2 < PT:
                            scores(n + 2)
                        if n > 0:
                            weigh_values(n - 1)
                    weigh_values(PT - 1)

            pe.wait_ge(sq_in, 32)
            pe.wait_ge(pT_ready, PT * H + 1)
            for h in range(H):
                got = nc.tensor.transpose(M[0][0:HW, h * P:(h + 1) * P], q_s[:, h, :], ident)
            got.then_inc(sq_ps, 1)
            for h in range(H):
                got = nc.tensor.transpose(T[0][0:DN, h * P:(h + 1) * P], w_ukv[:, h, 0:DN], ident)
            got.then_inc(sq_ps, 1)
            pe.wait_ge(sq_ready, 1)
            pe.wait_ge(wukT_ready, 1)
            pe.wait_ge(o_done, 2 + PT * H)
            for h in range(H):
                got = nc.tensor.matmul(M[1][:, h * P:(h + 1) * P], wukT[0:DN, h, :], qTs[0:DN, h, :], start=True, stop=True)
            got.then_inc(sq_ps, 1)
            pe.wait_ge(sq_ready, 2)
            pe.wait_ge(pads_zero, 2)
            N_KEYS = PAST + ROWS
            with pe.Fori(0, NB // 2) as j:
                for b, u, n in two(j):
                    pe.wait_ge(cache_in[u], 32 * n + 32)
                    for c in range(4):
                        nc.tensor.transpose(T[u][:, c * P:(c + 1) * P], lat_b[u][:, c, :], ident)
                    for c in range(4):
                        got = nc.tensor.transpose(T[u][0:HW, 512 + c * P:512 + (c + 1) * P], kr_b[u][:, c, :], ident)
                    got.then_inc(latb_ps, 1)
                for b, u, n in two(j):
                    pe.wait_ge(latb_ready, b + 1)
                    pe.wait_ge(bq_ready, b + 1)
                    pe.wait_ge(ctx_done, b + 1)
                    for c0, c1 in ((0, 512), (512, N_KEYS)):
                        nc.tensor.matmul(M[u][:, c0:c1], qa_b[u].rearrange("p h r -> p (h r)"), latTb[u][:, c0:c1], start=True, stop=False)
                        got = nc.tensor.matmul(M[u][:, c0:c1], qr_b[u][0:HW].rearrange("p h r -> p (h r)"), krTb[u][0:HW, c0:c1],
                                               start=False, stop=True)
                    got.then_inc(sb_ps, 1)
                for b, u, n in two(j):
                    pe.wait_ge(sb_p, b + 1)
                    transposes(T[u], p_b[u], 4)
                    nc.tensor.transpose(T[u][0:ROWS, 512:512 + P], p_b[u][:, PAST:], ident).then_inc(pTb_ps, 1)
                for b, u, n in two(j):
                    pe.wait_ge(pTb_ready, b + 1)
                    for c in range(4):
                        nc.tensor.matmul(M[u][:, 0:P], lat_b[u][:, c, :], pT_b[u][:, c, :], start=(c == 0), stop=False)
                    nc.tensor.matmul(M[u][:, 0:P], latn_b[u][0:ROWS, :], pT_b[u][0:ROWS, 4, :], start=False, stop=True).then_inc(ctx_ps, 1)
            pe.wait_ge(ctx_done, 2 + NB)
            for h in range(H):
                r = (h % 2) * DV
                got = nc.tensor.matmul(T[0][r:r + DV, (h // 2) * P:(h // 2 + 1) * P], w_ukv[:, h, DN:], ctxT[:, h, :],
                                       start=True, stop=True)
            got.then_inc(mixTs_ps, 1)

            pe.wait_ge(attn_copied, 1)
            pe.wait_ge(woq_in, 32)
            with pe.Fori(0, PT // 2) as j:
                def event(stage, u):
                    return 12 * j + 2 * stage + u + 1

                for t, u, n in two(j):
                    pe.wait_ge(attn_copied, t + 1)
                    pe.wait_ge(conv_ready, t + 1)
                    pe.wait_ge(logits_done, t + 1)
                    transposes(T[u], mix[u], 4)
                    transposes(T[u][:, 512:], conv_rows[u], 4).then_inc(rowsT_ps, 1)
                for t, u, n in two(j):
                    pe.wait_ge(rowsT_ready, event(0, u))
                    product(M[u], aT[u], w_out, BOTH).then_inc(product_ps, 1)
                LO, HI = [(0, 512)], [(512, 1024)]

                def turn(u, ready, rows):
                    pe.wait_ge(ready, 2 * j + u + 1)
                    transposes(T[u], rows[u], KT).then_inc(rowsT_ps, 1)

                def scores(u):
                    pe.wait_ge(rowsT_ready, event(2, u))
                    for h in range(XH):
                        for c in (0, 1):
                            got = nc.tensor.matmul(M[u][:, h * MEM:(h + 1) * MEM], aT[u][:, 2 * h + c, :], memkT[:, 2 * h + c, :],
                                                   start=(c == 0), stop=(c == 1))
                    got.then_inc(product_ps, 1)

                turn(0, x1_ready, xr)
                pe.wait_ge(rowsT_ready, event(1, 0))
                product(M[0], aT[0], w_xq, LO)
                turn(1, x1_ready, xr)
                product(M[0], aT[0], w_xq, HI, (1,)).then_inc(product_ps, 1)
                pe.wait_ge(rowsT_ready, event(1, 1))
                product(M[1], aT[1], w_xq, LO)
                turn(0, xq_rows, res)
                product(M[1], aT[1], w_xq, HI, (1,)).then_inc(product_ps, 1)
                scores(0)
                turn(1, xq_rows, res)
                scores(1)
                for t, u, n in two(j):
                    turn(u, px_ready, mix)
                    pe.wait_ge(rowsT_ready, event(3, u))
                    for h in range(XH):
                        for c in (0, 1):
                            got = nc.tensor.matmul(M[u][:, h * XD:(h + 1) * XD], aT[u][:, 2 * h + c, :], memv[:, c, h * XD:(h + 1) * XD],
                                                   start=(c == 0), stop=(c == 1))
                    got.then_inc(product_ps, 1)
                pe.wait_ge(wxo_in, 16)
                turn(0, ox_ready, res)
                pe.wait_ge(rowsT_ready, event(4, 0))
                product(M[0], aT[0], w_xo, LO)
                turn(1, ox_ready, res)
                product(M[0], aT[0], w_xo, HI, (1,)).then_inc(product_ps, 1)
                pe.wait_ge(rowsT_ready, event(4, 1))
                product(M[1], aT[1], w_xo, BOTH).then_inc(product_ps, 1)
                for t, u, n in two(j):
                    turn(u, x2_ready, xr)
                    pe.wait_ge(rowsT_ready, event(5, u))
                    for k in range(KT):
                        got = nc.tensor.matmul(M[u][:, 0:NG + NE], aT[u][:, k, :], w_router[:, k, :], start=(k == 0), stop=(k == KT - 1))
                    got.then_inc(product_ps, 1)

            E0 = 6 * PT
            pe.wait_ge(conv_ready, NT)
            pe.wait_ge(logits_done, NT)
            transposes(T[0][:, 512:], conv_rows[0], 4).then_inc(rowsT_ps, 1)
            pe.wait_ge(rowsT_ready, E0 + 1)
            product(M[0], aT[0], w_out, BOTH).then_inc(product_ps, 1)
            pe.wait_ge(x1_ready, NT)
            transposes(T[0], xr[0], KT).then_inc(rowsT_ps, 1)
            pe.wait_ge(rowsT_ready, E0 + 2)
            product(M[0], aT[0], w_xq, BOTH).then_inc(product_ps, 1)
            pe.wait_ge(xq_rows, NT)
            transposes(T[0], res[0], KT).then_inc(rowsT_ps, 1)
            pe.wait_ge(rowsT_ready, E0 + 3)

            def turn_memory(u, n):
                pe.wait_ge(mk_in[u], 16 * n + 16)
                for c in (0, 1):
                    got = transposes(T[c], mk_b[u][:, c, :], KT)
                got.then_inc(mkT_ps, 1)

            def attend_memory(b, u, n, last):
                pe.wait_ge(mkT_lo, b + 1)
                pe.wait_ge(mkT_hi, b + 1)
                pe.wait_ge(qx_ready, b + 1)
                for h in range(XH):
                    for c in (0, 1):
                        got = nc.tensor.matmul(M[0][h * 32:(h + 1) * 32, 0:MEM], qx_b[:, 2 * h + c, :], mkT_b[:, 2 * h + c, :],
                                               start=(c == 0), stop=(c == 1))
                got.then_inc(sx_ps, 1)
                if not last:
                    turn_memory(1 - u, n + u)
                pe.wait_ge(sx_p, b + 1)
                transposes(M[0][:, 512:], px_b, 2).then_inc(sxT_ps, 1)
                pe.wait_ge(sxT_ready, b + 1)
                pe.wait_ge(sxo_done, b + 1)
                pe.wait_ge(mv_in[u], 16 * n + 16)
                for h in range(XH):
                    for d in (0, 1):
                        for c in (0, 1):
                            got = nc.tensor.matmul(M[1][:, (2 * h + d) * ROWS:(2 * h + d + 1) * ROWS],
                                                   mv_b[u][:, c, h * XD + d * P:h * XD + (d + 1) * P],
                                                   pxT_b[:, c, h * 32:h * 32 + ROWS], start=(c == 0), stop=(c == 1))
                got.then_inc(sxo_ps, 1)

            turn_memory(0, 0)
            with pe.Fori(0, NB // 2 - 1) as j:
                for b, u, n in two(j):
                    attend_memory(b, u, n, False)
            for b, u, n in two(NB // 2 - 1):
                attend_memory(b, u, n, b == NB - 1)
            pe.wait_ge(sxo_done, NB + 1)
            product(M[0], oxT, w_xo, BOTH).then_inc(product_ps, 1)
            pe.wait_ge(x2_ready, NT)
            transposes(T[0], xr[0], KT).then_inc(rowsT_ps, 1)
            pe.wait_ge(rowsT_ready, E0 + 4)
            for k in range(KT):
                got = nc.tensor.matmul(M[0][:, 0:NG + NE], aT[0][:, k, :], w_router[:, k, :], start=(k == 0), stop=(k == KT - 1))
            got.then_inc(product_ps, 1)

            pe.wait_ge(softmax_in, 3)
            nc.tensor.matmul(T[0][:, 0:NT * NE], tri, picks, start=True, stop=True)
            nc.tensor.matmul(T[0][:, 512:512 + NT * NE], ones, picks, start=True, stop=True).then_inc(map_ps, 1)
            for i in range(2 * NT):
                pe.wait_ge(sel_ready, i + 1)
                nc.tensor.matmul(M[1][:, 0:NBLK], sel_slot[i % SEL], sel_blk[i % SEL], start=(i == 0), stop=(i == 2 * NT - 1)).then_inc(map_ps, 1)

            def split_product(out, x, w, c, first, last):
                for n, (xs, ws) in enumerate(((0, 0), (0, 1), (1, 0))):
                    got = nc.tensor.matmul(out, x[xs], (high, low)[ws](w)[:, c:c + 512], start=(first and n == 0), stop=(last and n == 2))
                return got

            def gate_up(b, u):
                pe.wait_ge(xgT_high, b + 1)
                pe.wait_ge(xgT_low, b + 1)
                pe.wait_ge(hid_ready, b + 1)
                for k in range(KT):
                    pe.wait_ge(gu_low, 8 * b + 8 + k + 1)
                    x = [xT_parts[u][s][:, k * P:(k + 1) * P] for s in (0, 1)]
                    for c in (0, FE):
                        got = split_product(M[0][:, c:c + 512], x, k, c, k == 0, k == KT - 1)
                    got.then_inc(gu_used, 1)

            def down(b, u):
                pe.wait_ge(hidT_high, b + 1)
                pe.wait_ge(hidT_low, b + 1)
                pe.wait_ge(ye_rows, b + 1)
                for k in range(4):
                    pe.wait_ge(down_low, 4 * b + 4 + k + 1)
                    x = [hidT_parts[u][s][:, k * P:(k + 1) * P] for s in (0, 1)]
                    for c in (0, 512):
                        got = split_product(M[1][:, c:c + 512], x, 8 + k, c, k == 0, k == 3)
                    got.then_inc(down_used, 1)

            def turn_rows(b, u, uses):
                pe.wait_ge(xg_in[u], 16 * uses + 16)
                if not (isinstance(b, int) and b == 0):
                    pe.wait_ge(xgT_low, b)
                    pe.wait_ge(xgT_high, b)
                transposes(T[0], xg[u], KT).then_inc(xgT_ps, 1)

            def turn_hidden(b, u):
                pe.wait_ge(hid_ready, b + 2)
                if u == 1:
                    pe.wait_ge(hidT_low, b)
                transposes(T[1], hid[u], 4).then_inc(hidT_ps, 1)

            pe.wait_ge(plan_ready, 1)
            pairs = pe.value_load(plan[0:1, NBLK:NBLK + 1], min_val=1, max_val=NBLK // 2)
            turn_rows(0, 0, 0)
            with pe.Fori(0, NBLK // 2) as j:
                with pe.If(j < pairs):
                    b0, b1 = 2 * j, 2 * j + 1
                    gate_up(b0, 0)
                    turn_rows(b1, 1, j)
                    turn_hidden(b0, 0)
                    gate_up(b1, 1)
                    down(b0, 0)
                    turn_hidden(b1, 1)
                    turn_rows(b1 + 1, 0, j + 1)
                    down(b1, 1)

        @block.scalar
        def _(act):
            act.sem_inc(q_rows, 2)
            act.sem_inc(exp_done, 2)
            act.sem_inc(sxo_done, 1)
            act.sem_inc(ye_rows, 1)
            for c in (0, 1):
                act.wait_ge(mem_ps, c + 1)
                nc.scalar.copy(memT[:, c, :, :].rearrange("p k c -> p (k c)"), T[c][:, :]).then_inc(mem_act, 1)
            def split_gates(chunks):
                for k in chunks:
                    act.wait_ge(raw_in[2], 96 if k < 6 else 128)
                    nc.scalar.copy(high(k), w_stage[k]).then_inc(win_high, 1)

            act.wait_ge(mem_ps, 4)
            split_gates(range(4))
            for c in (0, 1):
                act.wait_ge(mem_ps, 4 + c + 1)
                nc.scalar.copy(memv[:, c, :], T[c][:, :]).then_inc(mem_act, 1)
            split_gates(range(4, KT))
            act.wait_ge(win_low, KT)
            act.wait_ge(mem_out, 32)

            def project(tiles):
                for t, u, n in tiles:
                    act.wait_ge(xT_ps, t + 1)
                    nc.scalar.copy(xT_a[u].rearrange("p k c -> p (k c)"), T[u][:, :]).then_inc(xT_ready, 1)
                    nc.scalar.copy(x_high[u], T[u][:, :]).then_inc(xT_ready, 1)
                for t, u, n in tiles:
                    act.wait_ge(latent_ps, t + 1)
                    nc.scalar.activation(cqn[u], M[u][:, 0:QL], ACT.Square, scale=float(QL) ** -0.5, accum_out=sumsq[u][:, 0:1])
                    nc.scalar.activation(sq_junk[:, u * KL:(u + 1) * KL], M[u][:, QL:QL + KL], ACT.Square, scale=float(KL) ** -0.5,
                                         accum_out=sumsq[u][:, 1:2]).then_inc(sumsq_ready, 1)
                    act.wait_ge(gb_out[u], 16 * n + 16)
                    nc.scalar.copy(gbs[u], M[u][:, 512:1024])
                for t, u, n in tiles:
                    act.wait_ge(conv_ps, t + 1)
                    act.wait_ge(u_out[u], 16 * n + 16)
                    nc.scalar.copy(us[u], T[u][:, 512:1024]).then_inc(gates_ready, 1)
                for t, u, n in tiles:
                    act.wait_ge(cT_ps, t + 1)
                    nc.scalar.copy(cqT[u].rearrange("p k c -> p (k c)"), M[u][:, 0:2 * P]).then_inc(cqT_ready, 1)
                    if isinstance(t, int) and t == PT:
                        nc.scalar.copy(latT[:, PT * P:], M[u][:, 2 * P:3 * P])
                        nc.scalar.copy(krTs[DN:HW, :], M[u][DN:HW, 3 * P:4 * P])
                    else:
                        nc.scalar.copy(latT[:, ds(t * P, P)], M[u][:, 2 * P:3 * P])
                        nc.scalar.copy(kT[0][DN:HW, ds(t * P, P)], M[u][DN:HW, 3 * P:4 * P])
                        nc.scalar.copy(kT[1][DN:HW, ds(t * P, P)], M[u][DN:HW, 3 * P:4 * P])
                for t, u, n in tiles:
                    act.wait_ge(q_ps, t + 1)
                    act.wait_ge(q_out[u], 16 * n + 16)
                    nc.scalar.copy(qrow[u][:, 0:384], M[u][:, 512:896])
                    nc.scalar.copy(qrow[u][:, 384:768], T[u][:, 0:384]).then_inc(q_rows, 1)

            with act.Fori(0, PT // 2) as j:
                project(two(j))
            project(LAST_TILE)

            act.wait_ge(q_turned, NT)
            for u, uses in ((0, 5), (1, 4)):
                act.wait_ge(q_out[u], 16 + 16 * uses)
                act.wait_ge(lat_out[u], 32 + 32 * uses)
                act.wait_ge(u_out[u], 16 + 16 * uses)
                act.wait_ge(gb_out[u], 16 + 16 * uses)
            act.wait_ge(edge_out, 16 * (2 + NB))
            for c, src in enumerate((T[0], T[1], M[0], M[1])):
                act.wait_ge(value_ps, c + 1)
                nc.scalar.copy(value[:, 2 * c:2 * c + 2, :].rearrange("p i c -> p (i c)"), src[:, :]).then_inc(value_ready, 1)
            with act.Fori(0, H // 2) as j:
                for h, u, n in two(j):
                    act.wait_ge(qT_ps, h + 1)
                    nc.scalar.mul(qT[u][0:HW, :], M[0][0:HW, :], MLA_SCALE).then_inc(qT_ready, 1)
                    for n in range(PT):
                        w = (ORDER[n] + 1) * P
                        act.wait_ge(negmax_ready, PT * h + n + 1)
                        nc.scalar.activation(pr[n % 2][:, 0:w], T[n % 2][:, 0:w], ACT.Exp, bias=negmax[n % 2][:, 0:1],
                                             scale=1.0, accum_out=rsum[n % 2][:, 0:1]).then_inc(exp_done, 1)

            act.wait_ge(sq_ps, 1)
            nc.scalar.mul(qTs[0:HW, :, :].rearrange("p h c -> p (h c)"), M[0][0:HW, :], MLA_SCALE).then_inc(sq_ready, 1)
            act.wait_ge(sq_ps, 3)
            nc.scalar.copy(qabs.rearrange("p h c -> p (h c)"), M[1][:, :]).then_inc(sq_ready, 1)
            with act.Fori(0, NB // 2) as j:
                for b, u, n in two(j):
                    act.wait_ge(latb_ps, b + 1)
                    nc.scalar.copy(latTb[u][:, 0:PAST], T[u][:, 0:512])
                    nc.scalar.copy(krTb[u][DN:HW, 0:PAST], T[u][DN:HW, 512:1024]).then_inc(latb_ready, 1)
                for b, u, n in two(j):
                    act.wait_ge(sb_negmax, b + 1)
                    nc.scalar.activation(p_b[u], M[u][:, 0:PAST + ROWS], ACT.Exp, bias=negmax[u][:, 0:1], scale=1.0,
                                         accum_out=rsum[u][:, 0:1]).then_inc(sb_exp, 1)
                for b, u, n in two(j):
                    act.wait_ge(pTb_ps, b + 1)
                    nc.scalar.copy(pT_b[u][:, 0:4, :].rearrange("p c q -> p (c q)"), T[u][:, 0:512])
                    nc.scalar.copy(pT_b[u][0:ROWS, 4, :], T[u][0:ROWS, 512:512 + P]).then_inc(pTb_ready, 1)
            act.wait_ge(mixTs_ps, 1)
            nc.scalar.copy(mixTs.rearrange("p k c -> p (k c)"), T[0][:, 0:512])

            def turn(stage, u, base):
                act.wait_ge(rowsT_ps, base + 2 * stage + u + 1)
                nc.scalar.copy(aT[u].rearrange("p k c -> p (k c)"), T[u][:, :]).then_inc(rowsT_ready, 1)

            with act.Fori(0, PT // 2) as j:
                for t, u, n in two(j):
                    nc.scalar.copy(mix[u][:, 0:512], attn[:, ds(t, 1), :].rearrange("p a c -> p (a c)")).then_inc(attn_copied, 1)
                for t, u, n in two(j):
                    turn(0, u, 12 * j)
                for t, u, n in two(j):
                    turn(1, u, 12 * j)
                for t, u, n in two(j):
                    act.wait_ge(product_ps, 12 * j + 2 + u + 1)
                    nc.scalar.mul(res[u], M[u][:, :], X_SCALE).then_inc(xq_rows, 1)
                    turn(2, u, 12 * j)
                for t, u, n in two(j):
                    act.wait_ge(xmax_ready, t + 1)
                    for h in range(XH):
                        got = nc.scalar.activation(mix[u][:, h * MEM:(h + 1) * MEM], M[u][:, h * MEM:(h + 1) * MEM], ACT.Exp,
                                                   bias=xmax[u][:, h:h + 1], scale=1.0, accum_out=xsum[u][:, h:h + 1])
                    got.then_inc(px_ready, 1)
                    turn(3, u, 12 * j)
                for stage in (4, 5):
                    for t, u, n in two(j):
                        turn(stage, u, 12 * j)
            E0 = 6 * PT
            act.wait_ge(product_ps, E0)
            nc.scalar.copy(aT[0][:, 0:4, :].rearrange("p k c -> p (k c)"), mixTs.rearrange("p k c -> p (k c)"))
            act.wait_ge(rowsT_ps, E0 + 1)
            nc.scalar.copy(aT[0][:, 4:8, :].rearrange("p k c -> p (k c)"), T[0][:, 512:]).then_inc(rowsT_ready, 1)
            act.wait_ge(rowsT_ps, E0 + 2)
            nc.scalar.copy(aT[0].rearrange("p k c -> p (k c)"), T[0][:, :]).then_inc(rowsT_ready, 1)
            act.wait_ge(product_ps, E0 + 2)
            nc.scalar.mul(res[0], M[0][:, :], X_SCALE).then_inc(xq_rows, 1)
            act.wait_ge(rowsT_ps, E0 + 3)
            nc.scalar.copy(aT[0].rearrange("p k c -> p (k c)"), T[0][:, :]).then_inc(rowsT_ready, 1)

            def evacuate_memory(b):
                act.wait_ge(mkT_ps, b + 1)
                nc.scalar.copy(mkT_b[:, :, 0:P], T[0][:, :].rearrange("p (k c) -> p k c", k=KT)).then_inc(mkT_lo, 1)

            def attend_memory(b, last):
                act.wait_ge(sx_negmax, b + 1)
                nc.scalar.activation(px_b, M[0][:, 0:MEM], ACT.Exp, bias=negmax[0][:, 0:1], scale=1.0,
                                     accum_out=rsum[0][:, 0:1]).then_inc(sx_exp, 1)
                if not last:
                    evacuate_memory(b + 1)
                act.wait_ge(sxT_ps, b + 1)
                nc.scalar.copy(pxT_b.rearrange("p c q -> p (c q)"), M[0][:, 512:768]).then_inc(sxT_ready, 1)
                act.wait_ge(sxo_ps, b + 3)
                nc.scalar.copy(oxT[:, :, ds(b * ROWS, ROWS)], M[1][:, 0:P].rearrange("p (k r) -> p k r", k=KT)).then_inc(sxo_done, 1)

            evacuate_memory(0)
            with act.Fori(0, NB // 2 - 1) as j:
                for b, u, n in two(j):
                    attend_memory(b, False)
            for b, u, n in two(NB // 2 - 1):
                attend_memory(b, b == NB - 1)
            def split_gate_up(b, chunks):
                for c in chunks:
                    if c % 4 == 0:
                        act.wait_ge(raw_in[c // 4], 32 * b + 32)
                    act.wait_ge(gu_used, 8 * b + c + 1)
                    nc.scalar.copy(high(c), w_raw[c // 4][:, c % 4, :]).then_inc(gu_high, 1)

            def split_down(b, chunks):
                for c in chunks:
                    if c == 0:
                        act.wait_ge(raw_in[2], 16 * (KT + b) + 16)
                    act.wait_ge(down_used, 4 * b + c + 1)
                    nc.scalar.copy(high(8 + c), w_raw[2][:, c, :]).then_inc(down_high, 1)

            split_gate_up(0, range(8))
            act.wait_ge(rowsT_ps, E0 + 4)
            nc.scalar.copy(aT[0].rearrange("p k c -> p (k c)"), T[0][:, :]).then_inc(rowsT_ready, 1)

            act.wait_ge(softmax_in, 1)
            nc.scalar.activation(r_eg, r_gd, ACT.Exp).then_inc(softmax_exp, 1)
            act.wait_ge(softmax_in, 2)
            nc.scalar.activation(r_e2, r_d2, ACT.Exp).then_inc(softmax_exp, 1)

            act.wait_ge(plan_ready, 1)
            pairs = act.value_load(plan[0:1, NBLK:NBLK + 1], min_val=1, max_val=NBLK // 2)
            pairs_less_1 = act.value_load(plan[0:1, NBLK + 1:NBLK + 2], min_val=0, max_val=NBLK // 2 - 1)

            def silu(b, u):
                act.wait_ge(gu_used, 8 * b + 16)
                nc.scalar.activation(hid[u], M[0][:, 0:512], ACT.Silu).then_inc(silu_ready, 1)

            def rows_high(b, u):
                act.wait_ge(xgT_ps, b + 1)
                nc.scalar.copy(xT_parts[u][0], T[0][:, :]).then_inc(xgT_high, 1)

            def hidden_high(b, u):
                act.wait_ge(hidT_ps, b + 1)
                nc.scalar.copy(hidT_parts[u][0], T[1][:, 0:512]).then_inc(hidT_high, 1)

            def results(b, u):
                act.wait_ge(yo_free, j + 1)
                act.wait_ge(down_used, 4 * b + 8)
                nc.scalar.copy(yo[u], M[1][:, :]).then_inc(ye_rows, 1)

            rows_high(0, 0)
            with act.Fori(0, NBLK // 2) as j:
                with act.If(j < pairs):
                    b0, b1 = 2 * j, 2 * j + 1
                    split_gate_up(b1, range(7))
                    silu(b0, 0)
                    split_gate_up(b1, range(7, 8))
                    rows_high(b1, 1)
                    hidden_high(b0, 0)
                    split_down(b0, range(4))
                    with act.If(j < pairs_less_1):
                        split_gate_up(b1 + 1, range(7))
                    silu(b1, 1)
                    with act.If(j < pairs_less_1):
                        split_gate_up(b1 + 1, range(7, 8))
                    split_down(b1, range(2))
                    hidden_high(b1, 1)
                    results(b0, 0)
                    split_down(b1, range(2, 4))
                    rows_high(b1 + 1, 0)
                    results(b1, 1)

            def scale_residual(t, i, n):
                act.wait_ge(last_in[i], 32 * n + 32)
                nc.scalar.activation(xl[i], xl[i], ACT.Identity, scale=ALPHA).then_inc(xl_scaled, 1)

            def normalise(t, i, n):
                u = i % 2
                act.wait_ge(rstd_ready, NORMS + t + 1)
                nc.scalar.activation(rl[i], rl[i], ACT.Identity, scale=rstd[u][:, 0:1], bias=shift_by[u][:, 0:1]).then_inc(normed3, 1)

            with act.Fori(0, PT // 4) as g:
                in_turn(four(g), scale_residual, normalise)
            in_turn(LAST_OF_FOURS, scale_residual, normalise)

        @block.vector
        def _(dve):
            step = Count("dve")

            dve.sem_inc(o_done, 2)
            dve.sem_inc(pT_ready, 1)
            dve.sem_inc(ctx_done, 2)
            dve.sem_inc(logits_done, 2)
            dve.sem_inc(gu_low, 8)
            dve.sem_inc(down_low, 4)
            dve.sem_inc(hid_ready, 1)
            for c in (0, 1):
                dve.wait_ge(mem_ps, 2 + c + 1)
                nc.vector.tensor_copy(memk[:, c, :], M[c][:, :]).then_inc(mem_dve, 1)
            def take_low(out, x, highs):
                return nc.vector.tensor_tensor(out, x, highs.bitcast(f32), ALU.subtract)

            def split_gates(chunks):
                for k in chunks:
                    dve.wait_ge(win_high, k + 1)
                    take_low(low(k), w_stage[k], high(k)).then_inc(win_low, 1)

            split_gates(range(4))
            for c in (0, 1):
                dve.wait_ge(mem_ps, 6 + c + 1)
                nc.vector.tensor_copy(memkT[:, :, c * P:(c + 1) * P], M[c][:, :].rearrange("p (k c) -> p k c", k=KT)).then_inc(mem_dve, 1)
            split_gates(range(4, KT))
            dve.wait_ge(consts_in, 16 * 6)
            dve.wait_ge(pads_zero, 1)

            def turn_rows(t, x, heads, rot):
                half = DR // 2
                cos = rope[:, ds(t, 1), 0:DR].to_broadcast([P, heads, DR])
                msin = rope[:, ds(t, 1), DR:DR + half].to_broadcast([P, heads, half])
                sin = rope[:, ds(t, 1), DR + half:].to_broadcast([P, heads, half])
                a, b = rot
                nc.vector.tensor_tensor(a, x, cos, ALU.mult)
                nc.vector.tensor_tensor(b[:, :, 0:half], x[:, :, half:], msin, ALU.mult)
                nc.vector.tensor_tensor(b[:, :, half:], x[:, :, 0:half], sin, ALU.mult).then_inc(dve_step, step.next())
                dve.wait_ge(dve_step, step.value())
                return a, b

            def project(tiles):
                for t, u, n in tiles:
                    dve.wait_ge(xT_ready, 2 * t + 2)
                    take_low(x_low[u], T[u][:, :], x_high[u]).then_inc(xT_low, 1)
                for t, u, n in tiles:
                    dve.wait_ge(rrms_ready, t + 1)
                    nc.vector.scalar_tensor_tensor(cqn[u], M[u][:, 0:QL], rrms[u][:, 0:1], q_gain, ALU.mult, ALU.mult)
                    dve.wait_ge(lat_out[u], 32 * n + 32)
                    nc.vector.scalar_tensor_tensor(ckvn[u], M[u][:, QL:QL + KL], rrms[u][:, 1:2], kv_gain, ALU.mult, ALU.mult)
                    a, b = turn_rows(t, M[u][:, QL + KL:QL + KL + DR].rearrange("p (h c) -> p h c", h=1), 1, rot_k[u])
                    nc.vector.tensor_tensor(krpad[u][:, DN:].rearrange("p (h c) -> p h c", h=1), a, b, ALU.add).then_inc(norm_done, 1)
                for t, u, n in tiles:
                    dve.wait_ge(gates_ready, t + 1)
                    nc.vector.tensor_tensor(us[u], T[u][:, 0:CW], us[u], ALU.mult).then_inc(u_ready, 1)
                for t, u, n in tiles:
                    dve.wait_ge(q_rows, t + 3)
                    x = qrow[u].rearrange("p (h c) -> p h c", h=H)[:, :, DN:]
                    a, b = turn_rows(t, x, H, rot_q[u])
                    nc.vector.tensor_tensor(x, a, b, ALU.add).then_inc(q_turned, 1)

            with dve.Fori(0, PT // 2) as j, step.loop(j, 4, PT // 2):
                project(two(j))
            project(LAST_TILE)

            dve.wait_ge(value_ready, 4)
            with dve.Fori(0, H // 2) as j, step.loop(j, 4 * PT, H // 2):
                for h, u, n in two(j):
                    dve.wait_ge(kT_ps, h + 3)
                    nc.vector.tensor_copy(kT[u][0:DN, :], M[1][0:DN, :]).then_inc(kT_ready, 1)

                    def row_max(n):
                        s, w = n % 2, (ORDER[n] + 1) * P
                        dve.wait_ge(s_ps, PT * h + n + 1)
                        nc.vector.memset(T[s][0:64, w - 64:w], FAR).then_inc(dve_step, step.next())
                        dve.wait_ge(dve_step, step.value())
                        nc.vector.tensor_reduce(negmax[s][:, 0:1], T[s][:, 0:w], AX.X, ALU.max, negate=True).then_inc(negmax_ready, 1)

                    row_max(0)
                    row_max(1)
                    def scale_rows(n):
                        s = n % 2
                        dve.wait_ge(o_ps, PT * h + n + 1)
                        nc.vector.tensor_scalar(attn[:, ORDER[n], ds(h * DV, DV)], M[1][:, s * 512:s * 512 + DV], rinv[s][:, 0:1],
                                                None, ALU.mult).then_inc(o_done, 1)

                    for n in range(PT):
                        s, i = n % 2, ORDER[n]
                        dve.wait_ge(pT_ps, PT * h + n + 1)
                        nc.vector.tensor_copy(prT[s][:, 0:i + 1, :].rearrange("p i c -> p (i c)"), M[0][:, 0:(i + 1) * P]).then_inc(pT_ready, 1)
                        dve.wait_ge(o_done, PT * h + n + 1)
                        nc.vector.reciprocal(rinv[s][:, 0:1], rsum[s][:, 0:1]).then_inc(dve_step, step.next())
                        if n + 2 < PT:
                            row_max(n + 2)
                        if n > 0:
                            scale_rows(n - 1)
                    dve.wait_ge(dve_step, step.value())
                    scale_rows(PT - 1)

            dve.wait_ge(sq_ps, 2)
            nc.vector.tensor_copy(wukT[0:DN, :, :].rearrange("p h c -> p (h c)"), T[0][0:DN, :]).then_inc(wukT_ready, 1)
            dve.wait_ge(sq_ready, 2)
            dve.wait_ge(sq_in, 32)
            with dve.Fori(0, NB // 2) as j, step.loop(j, 2, NB // 2):
                for b, u, n in two(j):
                    dve.wait_ge(ctx_ps, b + 1)
                    nc.vector.tensor_copy(qa_b[u], qabs[:, :, ds(b * ROWS, ROWS)])
                    nc.vector.tensor_copy(qr_b[u][0:HW], qTs[0:HW, :, ds(b * ROWS, ROWS)])
                    nc.vector.tensor_copy(latn_b[u][0:ROWS, :], lat_new[0:ROWS, ds(b, 1), :].rearrange("p a c -> p (a c)"))
                    nc.vector.tensor_copy(latTb[u][:, PAST:], latT[:, ds(PT * P + b * ROWS, ROWS)])
                    nc.vector.tensor_copy(krTb[u][DN:HW, PAST:], krTs[DN:HW, ds(b * ROWS, ROWS)]).then_inc(bq_ready, 1)
                for b, u, n in two(j):
                    dve.wait_ge(sb_ps, b + 1)
                    nc.vector.tensor_reduce(negmax[u][:, 0:1], M[u][:, 0:PAST + ROWS], AX.X, ALU.max, negate=True).then_inc(sb_negmax, 1)
                for b, u, n in two(j):
                    dve.wait_ge(sb_exp, b + 1)
                    nc.vector.reciprocal(rinv[u][:, 0:1], rsum[u][:, 0:1]).then_inc(dve_step, step.next())
                    dve.wait_ge(dve_step, step.value())
                    nc.vector.tensor_scalar(p_b[u], p_b[u], rinv[u][:, 0:1], None, ALU.mult).then_inc(sb_p, 1)
                for b, u, n in two(j):
                    dve.wait_ge(ctx_ps, b + 3)
                    nc.vector.tensor_copy(ctxT[:, :, ds(b * ROWS, ROWS)], M[u][:, 0:P].rearrange("p (h r) -> p h r", h=H)).then_inc(ctx_done, 1)

            dve.wait_ge(ln_in, 48)
            dve.wait_ge(consts_in, 16 * 10)

            def add_norm(tiles, product_at, gain, shift, out_ready):
                for t, u, n in tiles:
                    dve.wait_ge(product_ps, product_at(u))
                    nc.vector.scalar_tensor_tensor(res[u], xr[u], ALPHA, M[u][:, :], ALU.mult, ALU.add).then_inc(dve_step, step.next())
                    dve.wait_ge(dve_step, step.value())
                    nc.vector.bn_stats(stats[u][:, 0:6], res[u][:, 0:512])
                    nc.vector.bn_stats(stats[u][:, 6:12], res[u][:, 512:]).then_inc(dve_step, step.next())
                    dve.wait_ge(dve_step, step.value())
                    dve.sem_inc(waited, 1)
                    nc.vector.bn_aggr(moments[u][:, :], stats[u][:, :]).then_inc(var_ready, 1)
                    dve.wait_ge(rstd_ready, norms[0] + u + 1)
                    nc.vector.tensor_scalar(res[u], res[u], moments[u][:, 0:1], rstd[u][:, 0:1], ALU.subtract, ALU.mult)\
                        .then_inc(dve_step, step.next())
                    dve.wait_ge(dve_step, step.value())
                    nc.vector.tensor_tensor(res[u], res[u], gain, ALU.mult).then_inc(dve_step, step.next())
                    dve.wait_ge(dve_step, step.value())
                    nc.vector.tensor_tensor(xr[u], res[u], shift, ALU.add).then_inc(out_ready, 1)

            with dve.Fori(0, PT // 2) as j, step.loop(j, 18, PT // 2):
                for t, u, n in two(j):
                    dve.wait_ge(xr_in[u], 16 * n + 16)
                norms = [4 * j]
                add_norm(two(j), lambda u: 12 * j + u + 1, gain1, shift1, x1_ready)
                for t, u, n in two(j):
                    dve.wait_ge(product_ps, 12 * j + 4 + u + 1)
                    nc.vector.tensor_reduce(xmax[u][:, :], M[u][:, :].rearrange("p (h m) -> p h m", h=XH), AX.X, ALU.max,
                                            negate=True).then_inc(xmax_ready, 1)
                for t, u, n in two(j):
                    dve.wait_ge(px_ready, t + 1)
                    nc.vector.reciprocal(xsum[u][:, :], xsum[u][:, :]).then_inc(dve_step, step.next())
                    dve.wait_ge(dve_step, step.value())
                    dve.wait_ge(product_ps, 12 * j + 6 + u + 1)
                    nc.vector.tensor_tensor(res[u].rearrange("p (h d) -> p h d", h=XH), M[u][:, :].rearrange("p (h d) -> p h d", h=XH),
                                            xsum[u][:, :].unsqueeze(2).to_broadcast([P, XH, XD]), ALU.mult).then_inc(ox_ready, 1)
                norms[0] = 4 * j + 2
                add_norm(two(j), lambda u: 12 * j + 8 + u + 1, gain2, shift2, x2_ready)
                for t, u, n in two(j):
                    dve.wait_ge(product_ps, 12 * j + 10 + u + 1)
                    nc.vector.tensor_tensor(logits[:, ds(t, 1), :].rearrange("p a c -> p (a c)"), M[u][:, 0:NG + NE], b_router[:, :],
                                            ALU.add).then_inc(logits_done, 1)

            E0 = 6 * PT
            norms = [2 * PT]
            dve.wait_ge(xr_in[0], 16 * 5)
            add_norm(LAST_TILE, lambda u: E0 + 1, gain1, shift1, x1_ready)
            dve.wait_ge(conv_ready, NT)
            nc.vector.memset(qx_b, 0.0).then_inc(dve_step, step.next())
            dve.wait_ge(dve_step, step.value())
            dve.wait_ge(rowsT_ready, E0 + 3)

            def evacuate_memory(b):
                dve.wait_ge(mkT_ps, b + 1)
                nc.vector.tensor_copy(mkT_b[:, :, P:], T[1][:, :].rearrange("p (k c) -> p k c", k=KT)).then_inc(mkT_hi, 1)

            def attend_memory(b, last):
                if not (isinstance(b, int) and b == 0):
                    dve.wait_ge(sx_ps, b)
                nc.vector.tensor_copy(qx_b[:, :, 0:ROWS], aT[0][:, :, ds(b * ROWS, ROWS)]).then_inc(qx_ready, 1)
                dve.wait_ge(sx_ps, b + 1)
                nc.vector.tensor_reduce(negmax[0][:, 0:1], M[0][:, 0:MEM], AX.X, ALU.max, negate=True).then_inc(sx_negmax, 1)
                dve.wait_ge(sx_exp, b + 1)
                nc.vector.reciprocal(rinv[0][:, 0:1], rsum[0][:, 0:1]).then_inc(dve_step, step.next())
                dve.wait_ge(dve_step, step.value())
                nc.vector.tensor_scalar(px_b, px_b, rinv[0][:, 0:1], None, ALU.mult).then_inc(sx_p, 1)
                if not last:
                    evacuate_memory(b + 1)

            evacuate_memory(0)
            attend_memory(0, False)
            attend_memory(1, False)
            with dve.Fori(1, NB // 2 - 1) as j, step.loop(j - 1, 2, NB // 2 - 2):
                for b, u, n in two(j):
                    attend_memory(b, False)
            for b, u, n in two(NB // 2 - 1):
                attend_memory(b, b == NB - 1)
            def split_gate_up(b, chunks):
                for c in chunks:
                    dve.wait_ge(gu_high, 8 * b + c + 1)
                    take_low(low(c), w_raw[c // 4][:, c % 4, :], high(c)).then_inc(gu_low, 1)

            def split_down(b, chunks):
                for c in chunks:
                    dve.wait_ge(down_high, 4 * b + c + 1)
                    take_low(low(8 + c), w_raw[2][:, c, :], high(8 + c)).then_inc(down_low, 1)

            split_gate_up(0, range(8))
            norms = [2 * PT + 1]
            add_norm(LAST_TILE, lambda u: E0 + 3, gain2, shift2, x2_ready)
            dve.wait_ge(product_ps, E0 + 4)
            nc.vector.tensor_tensor(logits[:, PT, :], M[0][:, 0:NG + NE], b_router[:, :], ALU.add).then_inc(logits_done, 1)

            def then(ins):
                ins.then_inc(dve_step, step.next())
                dve.wait_ge(dve_step, step.value())

            def wide(x, *shape):
                return x.unsqueeze(len(x.shape)).to_broadcast([P, *shape])

            def first_largest(values, n, best, scratch, pick):
                then(nc.vector.tensor_reduce(best, values, AX.X, ALU.max))
                then(nc.vector.tensor_tensor(scratch, values, wide(best, NT, n), ALU.is_equal))
                then(nc.vector.scalar_tensor_tensor(scratch, scratch, -64.0, iota[:, 0:n].unsqueeze(1).to_broadcast([P, NT, n]),
                                                    ALU.mult, ALU.add))
                then(nc.vector.tensor_reduce(r_first, scratch, AX.X, ALU.min))
                then(nc.vector.tensor_tensor(pick, scratch, wide(r_first, NT, n), ALU.is_equal))

            dve.wait_ge(logits_done, NT + 2)
            lg, le = logits[:, :, 0:NG], logits[:, :, NG:].rearrange("p t (g e) -> p t g e", g=NG)
            first_largest(lg, NG, r_best, r_s4, r_group)
            nc.vector.tensor_tensor(r_gd, lg, wide(r_best, NT, NG), ALU.subtract).then_inc(softmax_in, 1)
            then(nc.vector.tensor_tensor(r_all, le, wide(r_group, NT, NG, EG), ALU.mult))
            then(nc.vector.tensor_reduce(r_le, r_all.rearrange("p t g e -> p t e g"), AX.X, ALU.add))
            first_largest(r_le, EG, r_v1, r_s8, r_pick1)
            then(nc.vector.scalar_tensor_tensor(r_le, r_pick1, FAR, r_le, ALU.mult, ALU.add))
            first_largest(r_le, EG, r_v2, r_s8, r_pick2)
            nc.vector.tensor_tensor(r_d2, r_v2, r_v1, ALU.subtract).then_inc(softmax_in, 1)
            for k, pick in ((0, r_pick1), (1, r_pick2)):
                for g in range(NG):
                    got = nc.vector.tensor_tensor(r_hot[:, k, :, g * EG:(g + 1) * EG], pick,
                                                  r_group[:, :, g:g + 1].to_broadcast([P, NT, EG]), ALU.mult)
            then(got)
            nc.vector.tensor_tensor(picks.rearrange("p (t e) -> p t e", t=NT), r_hot[:, 0], r_hot[:, 1], ALU.add).then_inc(softmax_in, 1)
            dve.wait_ge(softmax_exp, 1)
            then(nc.vector.tensor_reduce(r_sum, r_eg, AX.X, ALU.add))
            dve.wait_ge(softmax_exp, 2)
            then(nc.vector.scalar_tensor_tensor(r_den, r_e2, 1.0, r_sum, ALU.add, ALU.mult))
            then(nc.vector.reciprocal(gates[:, 0, :], r_den))
            then(nc.vector.tensor_tensor(gates[:, 1, :], gates[:, 0, :], r_e2, ALU.mult))
            dve.wait_ge(map_ps, 1)
            then(nc.vector.memset(r_before[:, 0, :], 0.0))
            then(nc.vector.tensor_copy(r_total, T[0][:, 512:512 + NT * NE].rearrange("p (t e) -> p t e", t=NT)))
            for t in range(NT):
                then(nc.vector.tensor_tensor(r_before[:, t + 1, :], r_before[:, t, :], r_total[:, t, :], ALU.add))
            then(nc.vector.tensor_tensor(r_rank, r_before[:, 0:NT, :], T[0][:, 0:NT * NE].rearrange("p (t e) -> p t e", t=NT), ALU.add))
            then(nc.vector.tensor_scalar(r_lim, iota[:, 0:NT], float(P), None, ALU.mult))
            then(nc.vector.tensor_tensor(r_cmp, wide(r_before[:, NT, :], NE, NT), r_lim.unsqueeze(1).to_broadcast([P, NE, NT]), ALU.is_gt))
            then(nc.vector.tensor_reduce(r_blocks, r_cmp, AX.X, ALU.add))
            then(nc.vector.tensor_scalar(r_blocks, r_blocks, 1.0, None, ALU.max))
            then(nc.vector.tensor_tensor_scan(r_end, ones[:, 0:NE], r_blocks, 0.0, ALU.mult, ALU.add))
            then(nc.vector.tensor_tensor(r_start, r_end, r_blocks, ALU.subtract))
            then(nc.vector.tensor_tensor(r_plan[0:1], iota[0:1, 0:NBLK].unsqueeze(2).to_broadcast([1, NBLK, NE]),
                                         r_end[0:1, :].unsqueeze(1).to_broadcast([1, NBLK, NE]), ALU.is_ge))
            then(nc.vector.tensor_reduce(r_row[0:1, 0:NBLK], r_plan[0:1], AX.X, ALU.add))
            then(nc.vector.tensor_scalar(r_row[0:1, 0:NBLK], r_row[0:1, 0:NBLK], float(NE - 1), None, ALU.min))
            then(nc.vector.tensor_scalar(r_row[0:1, NBLK:NBLK + 1], r_end[0:1, NE - 1:NE], 1.0, None, ALU.add))
            then(nc.vector.tensor_copy(r_int3[0:1, :], r_row[0:1, 0:NBLK + 1]))
            then(nc.vector.tensor_single_scalar(plan[0:1, NBLK:NBLK + 1], r_int3[0:1, NBLK:NBLK + 1], 1, ALU.logical_shift_right))
            then(nc.vector.tensor_copy(plan[0:1, 0:NBLK], r_int3[0:1, 0:NBLK]))
            nc.vector.tensor_single_scalar(plan[0:1, NBLK + 1:NBLK + 2], plan[0:1, NBLK:NBLK + 1], 1, ALU.subtract).then_inc(plan_ready, 1)
            then(nc.vector.scalar_tensor_tensor(r_rank, r_start.unsqueeze(1).to_broadcast([P, NT, NE]), float(P), r_rank, ALU.mult, ALU.add))
            for k in (0, 1):
                then(nc.vector.tensor_tensor(r_hot[:, k], r_hot[:, k], r_rank, ALU.mult))
                then(nc.vector.tensor_reduce(r_slot[:, :, k], r_hot[:, k], AX.X, ALU.add))
            then(nc.vector.tensor_copy(r_int, r_slot.rearrange("p t k -> p (t k)")))
            then(nc.vector.tensor_single_scalar(r_int2, r_int, 7, ALU.logical_shift_right))
            then(nc.vector.tensor_copy(r_blk, r_int2))
            then(nc.vector.tensor_single_scalar(r_int2, r_int, P - 1, ALU.bitwise_and))
            then(nc.vector.tensor_copy(r_pos, r_int2))
            for i in range(2 * NT):
                if i >= SEL:
                    dve.wait_ge(map_ps, i - SEL + 2)
                nc.vector.tensor_scalar(sel_slot[i % SEL], iota, r_pos[:, i:i + 1], None, ALU.is_equal)
                nc.vector.tensor_scalar(sel_blk[i % SEL], iota[:, 0:NBLK], r_blk[:, i:i + 1], slot_id.rearrange("p t k -> p (t k)")[:, i:i + 1],
                                        ALU.is_equal, ALU.mult).then_inc(sel_ready, 1)
            dve.wait_ge(map_ps, 1 + 2 * NT)
            then(nc.vector.tensor_scalar(r_map, M[1][:, 0:NBLK], 0.0, 8192.0, ALU.is_equal, ALU.mult))
            then(nc.vector.scalar_tensor_tensor(r_map, M[1][:, 0:NBLK], -1.0, r_map, ALU.add, ALU.add))
            then(nc.vector.tensor_copy(route_out[:, 0:NBLK], r_map))
            then(nc.vector.tensor_copy(r_mapi, r_map))
            then(nc.vector.tensor_single_scalar(r_mapi2, r_mapi, 1, ALU.logical_shift_right))
            then(nc.vector.memset(route_tok[:, NBLK:], 4095))
            nc.vector.tensor_copy(route_tok[:, 0:NBLK], r_mapi2).then_inc(routes_ready, 1)

            dve.wait_ge(plan_ready, 1)
            pairs = dve.value_load(plan[0:1, NBLK:NBLK + 1], min_val=1, max_val=NBLK // 2)
            pairs_less_1 = dve.value_load(plan[0:1, NBLK + 1:NBLK + 2], min_val=0, max_val=NBLK // 2 - 1)

            def hidden(b, u):
                dve.wait_ge(silu_ready, b + 1)
                nc.vector.tensor_tensor(hid[u], hid[u], M[0][:, 512:1024], ALU.mult).then_inc(hid_ready, 1)

            def rows_low(b, u):
                dve.wait_ge(xgT_high, b + 1)
                take_low(xT_parts[u][1], T[0][:, :], xT_parts[u][0]).then_inc(xgT_low, 1)

            def hidden_low(b, u):
                dve.wait_ge(hidT_high, b + 1)
                take_low(hidT_parts[u][1], T[1][:, 0:512], hidT_parts[u][0]).then_inc(hidT_low, 1)

            rows_low(0, 0)
            with dve.Fori(0, NBLK // 2) as j:
                with dve.If(j < pairs):
                    b0, b1 = 2 * j, 2 * j + 1
                    split_gate_up(b1, range(7))
                    hidden(b0, 0)
                    split_gate_up(b1, range(7, 8))
                    rows_low(b1, 1)
                    hidden_low(b0, 0)
                    split_down(b0, range(4))
                    with dve.If(j < pairs_less_1):
                        split_gate_up(b1 + 1, range(7))
                    hidden(b1, 1)
                    with dve.If(j < pairs_less_1):
                        split_gate_up(b1 + 1, range(7, 8))
                    split_down(b1, range(2))
                    hidden_low(b1, 1)
                    split_down(b1, range(2, 4))
                    rows_low(b1 + 1, 0)

            dve.wait_ge(ln3_in, 32)

            def sum_rows(t, i, n):
                u = i % 2
                dve.wait_ge(last_in[i], 32 * n + 32)
                dve.wait_ge(xl_scaled, t + 1)
                dve.wait_ge(y_out[i], 16 * n + 16)
                then(nc.vector.scalar_tensor_tensor(rl[i], yk[i][:, 0, :], gates[:, 0, ds(t, 1)], xl[i], ALU.mult, ALU.add))
                then(nc.vector.scalar_tensor_tensor(rl[i], yk[i][:, 1, :], gates[:, 1, ds(t, 1)], rl[i], ALU.mult, ALU.add))
                nc.vector.bn_stats(stats[u][:, 0:6], rl[i][:, 0:512])
                then(nc.vector.bn_stats(stats[u][:, 6:12], rl[i][:, 512:]))
                dve.sem_inc(waited, 1)
                nc.vector.bn_aggr(moments[u][:, :], stats[u][:, :]).then_inc(var_ready, 1)

            def add_shift(t, i, n):
                dve.wait_ge(gain3_done, t + 1)
                nc.vector.tensor_tensor(rl[i], rl[i], shift3, ALU.add).then_inc(y_ready, 1)

            with dve.Fori(0, PT // 4) as g, step.loop(g, 12, PT // 4):
                in_turn(four(g), sum_rows, add_shift)
            in_turn(LAST_OF_FOURS, sum_rows, add_shift)

        @block.gpsimd
        def _(pool):
            step = Count("pool")
            pool.sem_inc(yo_free, 1)
            nc.gpsimd.memset(minus_half[:, :], -0.5)
            nc.gpsimd.memset(minus_one[:, :], -1.0)
            nc.gpsimd.memset(zero_row[:, :], 0.0)
            pool.wait_ge(mem_ps, 6)
            nc.gpsimd.memset(krpad[0][:, 0:DN], 0.0)
            nc.gpsimd.memset(krpad[1][:, 0:DN], 0.0).then_inc(pads_zero, 1)
            pool.wait_ge(pads_zero, 1)

            def inverse_root(out, x, eps):
                pool.sem_inc(waited, 1)
                nc.gpsimd.tensor_scalar(x, x, eps, None, ALU.add).then_inc(pool_step, step.next())
                pool.wait_ge(pool_step, step.value())
                return nc.gpsimd.tensor_tensor(out, x, minus_half[:, 0:x.shape[1]], ALU.pow)

            def latents(tiles):
                for t, u, n in tiles:
                    pool.wait_ge(sumsq_ready, t + 1)
                    inverse_root(rrms[u][:, :], sumsq[u][:, :], RMS_EPS).then_inc(rrms_ready, 1)

            with pool.Fori(0, PT // 2) as j, step.loop(j, 2, PT // 2):
                latents(two(j))
            latents(LAST_TILE)

            pool.wait_ge(kT_ps, 2 + H)
            pool.wait_ge(o_done, 2 + PT * H)
            for u in (0, 1):
                nc.gpsimd.memset(kr_b[u][:, :, 0:DN], 0.0)
                got = nc.gpsimd.memset(krTb[u][0:DN, :], 0.0)
            got.then_inc(pads_zero, 1)

            pool.wait_ge(consts_in, 16 * 10)

            def convolve(u, loads, turned):
                pool.wait_ge(conv_in, loads)
                if turned is not None:
                    pool.wait_ge(rowsT_ps, turned)
                out = conv_rows[u]
                nc.gpsimd.tensor_tensor(cv[:, 0:3, :], cv[:, 0:3, :], conv_w[:, :, :], ALU.mult).then_inc(pool_step, step.next())
                pool.wait_ge(pool_step, step.value())
                nc.gpsimd.tensor_tensor(out, cv[:, 0, :], cv[:, 1, :], ALU.add).then_inc(pool_step, step.next())
                pool.wait_ge(pool_step, step.value())
                nc.gpsimd.tensor_tensor(out, out, cv[:, 2, :], ALU.add).then_inc(pool_step, step.next())
                pool.wait_ge(pool_step, step.value())
                nc.gpsimd.tensor_tensor(out, out, cv[:, 3, :], ALU.mult).then_inc(conv_ready, 1)

            def deviation(u, at):
                pool.wait_ge(var_ready, at)
                inverse_root(rstd[u][:, :], moments[u][:, 1:2], LN_EPS).then_inc(rstd_ready, 1)

            convolve(0, 64, None)
            convolve(1, 128, None)
            with pool.Fori(0, PT // 2 - 1) as j, step.loop(j, 10, PT // 2 - 1):
                deviation(0, 4 * j + 1)
                deviation(1, 4 * j + 2)
                convolve(0, 128 * j + 192, 12 * j + 1)
                convolve(1, 128 * j + 256, 12 * j + 2)
                deviation(0, 4 * j + 3)
                deviation(1, 4 * j + 4)
            deviation(0, 13)
            deviation(1, 14)
            convolve(0, 64 * PT + 16 * (3 * NB + 1), 37)
            for at in (15, 16, 17, 18):
                deviation(0 if at != 16 else 1, at)

            pool.wait_ge(x2_out[0], 16 + 16 * 5)
            pool.wait_ge(x2_out[1], 16 + 16 * 4)
            pool.wait_ge(logits_done, NT + 2)
            nc.gpsimd.memset(xg[0], 0.0)
            nc.gpsimd.memset(xg[1], 0.0).then_inc(pool_step, step.next())
            pool.wait_ge(pool_step, step.value())
            pool.wait_ge(plan_ready, 1)
            pool.wait_ge(routes_ready, 1)

            def gather(b, u, copied):
                nc.gpsimd.tensor_copy(tok_now[u][:, :], route_tok[:, ds(b, 1)]).then_inc(idx_ready, 1)
                pool.wait_ge(idx_ready, copied)
                pool.sem_inc(waited, 1)
                nc.gpsimd.indirect_dma_start(out=xg[u], out_offset=None, in_=x2_dram,
                                             in_offset=bass.IndirectOffsetOnAxis(ap=tok_now[u][:, 0:1], axis=0),
                                             bounds_check=NT * P - 1, oob_is_err=False).then_inc(xg_in[u], 16)

            gather(0, 0, 1)
            gather(1, 1, 2)
            pairs = pool.value_load(plan[0:1, NBLK:NBLK + 1], min_val=1, max_val=NBLK // 2)
            with pool.Fori(0, NBLK // 2) as j:
                with pool.If(j < pairs):
                    for b, u, n in two(j):
                        pool.wait_ge(xgT_ps, b + 1)
                        gather(b + 2, u, 4 * j + 3 + u)
                    for b, u, n in two(j):
                        nc.gpsimd.tensor_copy(out_now[u][:, :], route_out[:, ds(b, 1)]).then_inc(idx_ready, 1)
                        pool.wait_ge(idx_ready, 4 * j + 5 + u)
                        pool.wait_ge(ye_rows, b + 2)
                        pool.sem_inc(waited, 1)
                        nc.gpsimd.indirect_dma_start(out=ye_dram, out_offset=bass.IndirectOffsetOnAxis(ap=out_now[u][:, 0:1], axis=0),
                                                     in_=yo[u], in_offset=None, bounds_check=2 * NT * P - 1,
                                                     oob_is_err=False).then_inc(ye_out[u], 16)
                    for b, u, n in two(j):
                        pool.wait_ge(ye_out[u], 16 * n + 16)
                    pool.sem_inc(yo_free, 1)

            def inverse_deviation(t, i, n):
                u = i % 2
                pool.wait_ge(var_ready, NORMS + t + 1)
                nc.gpsimd.tensor_tensor(moments[u][:, 0:1], moments[u][:, 0:1], minus_one[:, :], ALU.mult)
                inverse_root(rstd[u][:, :], moments[u][:, 1:2], LN_EPS).then_inc(pool_step, step.next())
                pool.wait_ge(pool_step, step.value())
                nc.gpsimd.tensor_tensor(shift_by[u][:, :], moments[u][:, 0:1], rstd[u][:, :], ALU.mult).then_inc(rstd_ready, 1)

            def times_gain(t, i, n):
                pool.wait_ge(normed3, t + 1)
                nc.gpsimd.tensor_tensor(rl[i], rl[i], gain3, ALU.mult).then_inc(gain3_done, 1)

            pool.wait_ge(ln3_in, 32)
            with pool.Fori(0, PT // 4) as g, step.loop(g, 8, PT // 4):
                for tile in four(g):
                    inverse_deviation(*tile)
                    times_gain(*tile)
            inverse_deviation(*LAST_OF_FOURS[0])
            times_gain(*LAST_OF_FOURS[0])


_INS = ['x_prompt', 'x_sample', 'cache_kv_latent', 'cache_k_rope', 'cache_conv', 'cache_mem_k', 'cache_mem_v',
        'mem_prompt', 'w_in', 'q_norm_g', 'kv_norm_g', 'w_uq', 'w_ukv', 'conv_w', 'w_out', 'ln1_g', 'ln1_b',
        'w_xq', 'w_xk', 'w_xv', 'w_xo', 'ln2_g', 'ln2_b', 'w_router_group', 'b_router_group',
        'w_router_expert', 'b_router_expert', 'w_exp_gate', 'w_exp_up', 'w_exp_down', 'ln3_g', 'ln3_b']
_OUTS = [('y_prompt', (1, 1024, 1024)), ('y_sample', (8, 16, 1024)), ('new_kv_latent_prompt', (1, 1, 1024, 128)),
         ('new_k_rope_prompt', (1, 1, 1024, 32)), ('new_conv_prompt', (1, 1, 2, 512)),
         ('new_mem_k_prompt', (1, 1, 256, 4, 256)), ('new_mem_v_prompt', (1, 1, 256, 4, 256)),
         ('new_kv_latent_sample', (1, 8, 16, 128)), ('new_k_rope_sample', (1, 8, 16, 32)),
         ('new_conv_sample', (1, 8, 2, 512))]


def kernel(**inputs):
    import numpy as _np
    import concourse.bacc as _bacc
    from concourse import mybir as _mybir
    from concourse.bass_utils import run_bass_kernel_spmd as _run

    nc = _bacc.Bacc("TRN2", target_bir_lowering=False, num_devices=1)
    arrays, ins, outs = {}, {}, {}
    for name in _INS:
        a = _np.ascontiguousarray(inputs[name])
        arrays[f"in_{name}"] = a
        ins[name] = nc.dram_tensor(f"in_{name}", a.shape, _mybir.dt.from_np(a.dtype), kind="ExternalInput").ap()
    arrays["in_tables"] = consts_table()
    ins["tables"] = nc.dram_tensor("in_tables", arrays["in_tables"].shape, _mybir.dt.float32, kind="ExternalInput").ap()
    for name, shape in _OUTS:
        outs[name] = nc.dram_tensor(f"out_{name}", shape, _mybir.dt.float32, kind="ExternalOutput").ap()
    encoder_layer_kernel(nc, ins, outs)
    r = _run(nc, [arrays], core_ids=[0])
    return tuple(r.results[0][f"out_{name}"] for name, _ in _OUTS)
```
